# Optimizing a Trainium2 kernel written in Bass

```python
import math
import jax, jax.numpy as jnp
from jax import lax
import numpy as np

D_MODEL = 1024
BATCH = 1
SEQ = 256
DEPTH = 2

CTX_LEN = 256
GRID_W = 64
N_MOD = 9
D_FF = 2816
NORM_EPS = 1e-6

ATT_HEADS = 8
ATT_KV_HEADS = 2
ATT_GROUP = ATT_HEADS // ATT_KV_HEADS
ATT_HD = 128
WINDOW = 128
ATT_BLOCK = 128
ROPE_THETA = 10000.0

ML_HEADS = 4
ML_HD = 256
ML_CHUNK = 64

GDN_HEADS = 8
GDN_HD = 128
GDN_CHUNK = 64
CONV_K = 5

N_BRANCH = 3
ATT_Q_W = ATT_HEADS * ATT_HD
ATT_KV_W = ATT_KV_HEADS * ATT_HD
ML_W = ML_HEADS * ML_HD
GDN_W = GDN_HEADS * GDN_HD
IN_SPLITS = (ATT_Q_W, ATT_KV_W, ATT_KV_W, ML_W, ML_W, ML_W, ML_W, 2 * ML_HEADS, 2 * ML_HEADS,
             GDN_W, GDN_W, GDN_W, GDN_W, 2 * GDN_HEADS, 2 * GDN_HEADS, N_BRANCH * D_MODEL)
N_IN = ATT_Q_W + 2 * ATT_KV_W + 4 * ML_W + 4 * ML_HEADS + 4 * GDN_W + 4 * GDN_HEADS + N_BRANCH * D_MODEL
CTX_OUTPUT_ONLY_PARTS = (0, 3, 6, 9, 12, 15)

kernel_name = 'hybrid_gated_parallel_mixer_dit_trunk'

def _rmsnorm(x, w):
    xf = x.astype(jnp.float32)
    y = xf * lax.rsqrt(jnp.mean(xf * xf, axis=-1, keepdims=True) + NORM_EPS)
    return (y * w.astype(jnp.float32)).astype(x.dtype)

def _l2norm(x):
    xf = x.astype(jnp.float32)
    return xf * lax.rsqrt(jnp.sum(xf * xf, axis=-1, keepdims=True) + NORM_EPS)

def _heads(a, n_heads):
    return a.reshape(a.shape[:-1] + (n_heads, a.shape[-1] // n_heads))

def _swiglu(x, w_gate, w_up, w_down):
    return (jax.nn.silu(x @ w_gate) * (x @ w_up)) @ w_down

def _adaln(cond, w_ada, b_ada):
    return (jax.nn.silu(cond) @ w_ada + b_ada).reshape(cond.shape[:-1] + (N_MOD, D_MODEL))

def _modulated_norm(h, mod, j, norm_w):
    shift, scale = mod[:, 3 * j][:, None], mod[:, 3 * j + 1][:, None]
    return _rmsnorm(h, norm_w) * (1 + scale) + shift

def _gated_residual(h, mod, j, y, weight):
    return h + weight * mod[:, 3 * j + 2][:, None] * y

def _in_proj(xn, w_in, skip):
    offs = np.cumsum((0,) + IN_SPLITS)
    return tuple(None if i in skip else xn @ w_in[:, offs[i]:offs[i + 1]] for i in range(len(IN_SPLITS)))

def _rope_half(x, cos, sin):
    x1, x2 = jnp.split(x, 2, axis=-1)
    return jnp.concatenate([x1 * cos - x2 * sin, x1 * sin + x2 * cos], axis=-1)

def _axial_rope(x, rows):
    half = ATT_HD // 2
    n_freq = half // 2
    inv_freq = ROPE_THETA ** (-jnp.arange(n_freq, dtype=jnp.float32) / n_freq)
    row = jnp.repeat(jnp.arange(rows, dtype=jnp.float32), GRID_W)
    col = jnp.tile(jnp.arange(GRID_W, dtype=jnp.float32), rows)
    ang_r = (row[:, None] * inv_freq)[:, None, :]
    ang_c = (col[:, None] * inv_freq)[:, None, :]
    xr = _rope_half(x[..., :half], jnp.cos(ang_r), jnp.sin(ang_r))
    xc = _rope_half(x[..., half:], jnp.cos(ang_c), jnp.sin(ang_c))
    return jnp.concatenate([xr, xc], axis=-1).astype(x.dtype)

def _latent_window_attention(q, k, v, kc, vc, sink):
    B, S = q.shape[:2]
    nb = S // ATT_BLOCK
    scale = ATT_HD ** -0.5
    qb = q.reshape(B, nb, ATT_BLOCK, ATT_KV_HEADS, ATT_GROUP, ATT_HD)
    pad = ((0, 0), (ATT_BLOCK, ATT_BLOCK), (0, 0), (0, 0))
    kp = jnp.pad(k, pad).reshape(B, nb + 2, ATT_BLOCK, ATT_KV_HEADS, ATT_HD)
    vp = jnp.pad(v, pad).reshape(B, nb + 2, ATT_BLOCK, ATT_KV_HEADS, ATT_HD)
    kband = jnp.concatenate([kp[:, :-2], kp[:, 1:-1], kp[:, 2:]], axis=2)
    vband = jnp.concatenate([vp[:, :-2], vp[:, 1:-1], vp[:, 2:]], axis=2)
    s_loc = jnp.einsum('bnqhgd,bnkhd->bnhgqk', qb, kband).astype(jnp.float32) * scale
    s_ctx = jnp.einsum('bnqhgd,bkhd->bnhgqk', qb, kc).astype(jnp.float32) * scale
    blk = jnp.arange(nb)[:, None, None]
    qpos = blk * ATT_BLOCK + jnp.arange(ATT_BLOCK)[None, :, None]
    kpos = (blk - 1) * ATT_BLOCK + jnp.arange(3 * ATT_BLOCK)[None, None, :]
    valid = (jnp.abs(kpos - qpos) <= WINDOW) & (kpos >= 0) & (kpos < S)
    s_loc = jnp.where(valid[None, :, None, None], s_loc, -jnp.inf)
    sink_l = jnp.broadcast_to(sink.astype(jnp.float32).reshape(1, 1, ATT_KV_HEADS, ATT_GROUP, 1, 1),
                              s_loc.shape[:-1] + (1,))
    p = jax.nn.softmax(jnp.concatenate([s_loc, s_ctx, sink_l], axis=-1), axis=-1).astype(v.dtype)
    n_loc = 3 * ATT_BLOCK
    n_ctx = kc.shape[1]
    o = (jnp.einsum('bnhgqk,bnkhd->bnqhgd', p[..., :n_loc], vband)
         + jnp.einsum('bnhgqk,bkhd->bnqhgd', p[..., n_loc:n_loc + n_ctx], vc))
    return o.reshape(B, S, ATT_Q_W)

def _context_attention(qc, kc, vc, sink):
    B, L = qc.shape[:2]
    qg = qc.reshape(B, L, ATT_KV_HEADS, ATT_GROUP, ATT_HD)
    s = jnp.einsum('bqhgd,bkhd->bhgqk', qg, kc).astype(jnp.float32) * (ATT_HD ** -0.5)
    sink_l = jnp.broadcast_to(sink.astype(jnp.float32).reshape(1, ATT_KV_HEADS, ATT_GROUP, 1, 1),
                              s.shape[:-1] + (1,))
    p = jax.nn.softmax(jnp.concatenate([s, sink_l], axis=-1), axis=-1).astype(vc.dtype)
    o = jnp.einsum('bhgqk,bkhd->bqhgd', p[..., :L], vc)
    return o.reshape(B, L, ATT_Q_W)

def _to_chunks(x, chunk):
    B, T = x.shape[:2]
    x = x.reshape((B, T // chunk, chunk) + x.shape[2:])
    return jnp.moveaxis(jnp.moveaxis(x, 1, 0), 2, 3)

def _from_chunks(x):
    x = jnp.moveaxis(jnp.moveaxis(x, 3, 2), 0, 1)
    return x.reshape((x.shape[0], x.shape[1] * x.shape[2]) + x.shape[3:])

def _mlstm_scan(feats, gates, state, with_out):
    q, k, v = feats
    k = _to_chunks(k.astype(jnp.float32), ML_CHUNK)
    v = _to_chunks(v.astype(jnp.float32), ML_CHUNK)
    ig = _to_chunks(gates[0], ML_CHUNK)
    lf = _to_chunks(gates[1], ML_CHUNK)
    _, B, H, L, dk = k.shape
    dv = v.shape[-1]
    if state is None:
        state = (jnp.zeros((B, H, dk, dv), jnp.float32), jnp.zeros((B, H, dk), jnp.float32),
                 jnp.zeros((B, H), jnp.float32))
    b = jnp.cumsum(lf, axis=-1)
    b_end = b[..., -1]
    a = b_end[..., None] - b + ig
    a_max = jnp.max(a, axis=-1)
    causal = jnp.tril(jnp.ones((L, L), dtype=bool))
    xs = (k, v, ig, b, b_end, a, a_max)
    if with_out:
        xs = xs + (_to_chunks(q.astype(jnp.float32), ML_CHUNK),)

    def step(carry, xs_c):
        C, n, m = carry
        k_c, v_c, ig_c, b_c, be_c, a_c, am_c = xs_c[:7]
        m_new = jnp.maximum(be_c + m, am_c)
        decay = jnp.exp(be_c + m - m_new)
        kw = k_c * jnp.exp(a_c - m_new[..., None])[..., None]
        C_new = decay[..., None, None] * C + jnp.einsum('bhsk,bhsv->bhkv', kw, v_c)
        n_new = decay[..., None] * n + jnp.sum(kw, axis=2)
        if not with_out:
            return (C_new, n_new, m_new), None
        q_c = xs_c[7]
        log_d = jnp.where(causal, b_c[..., :, None] - b_c[..., None, :] + ig_c[..., None, :], -jnp.inf)
        m_inter = b_c + m[..., None]
        m_t = jnp.maximum(m_inter, jnp.max(log_d, axis=-1))
        w_inter = jnp.exp(m_inter - m_t)
        s = jnp.einsum('bhtk,bhsk->bhts', q_c, k_c) * jnp.exp(log_d - m_t[..., None])
        num = w_inter[..., None] * jnp.einsum('bhtk,bhkv->bhtv', q_c, C) + jnp.einsum('bhts,bhsv->bhtv', s, v_c)
        den = w_inter * jnp.einsum('bhtk,bhk->bht', q_c, n) + jnp.sum(s, axis=-1)
        h = num / jnp.maximum(jnp.abs(den), jnp.exp(-m_t))[..., None]
        return (C_new, n_new, m_new), h

    state, h = lax.scan(step, state, xs)
    return state, (_from_chunks(h) if with_out else None)

def _gdn_scan(feats, gates, state, with_out):
    q, k, v = feats
    k = _to_chunks(k, GDN_CHUNK)
    v = _to_chunks(v, GDN_CHUNK)
    g = _to_chunks(gates[0], GDN_CHUNK)
    beta = _to_chunks(gates[1], GDN_CHUNK)
    _, B, H, L, dk = k.shape
    dv = v.shape[-1]
    if state is None:
        state = jnp.zeros((B, H, dk, dv), jnp.float32)
    gam = jnp.cumsum(g, axis=-1)
    g_end = gam[..., -1]
    incl = jnp.tril(jnp.ones((L, L), dtype=bool))
    strict = jnp.tril(jnp.ones((L, L), dtype=bool), -1)
    decay = jnp.exp(jnp.where(incl, gam[..., :, None] - gam[..., None, :], -jnp.inf))
    a_mat = jnp.where(strict, beta[..., :, None] * jnp.einsum('nbhtk,nbhsk->nbhts', k, k) * decay, 0.0)
    rhs = jnp.concatenate([beta[..., None] * v, (beta * jnp.exp(gam))[..., None] * k], axis=-1)
    sol = lax.linalg.triangular_solve(a_mat + jnp.eye(L, dtype=jnp.float32), rhs,
                                      left_side=True, lower=True, unit_diagonal=True)
    u, w = sol[..., :dv], sol[..., dv:]
    k_end = k * jnp.exp(g_end[..., None] - gam)[..., None]
    xs = (u, w, k_end, g_end)
    if with_out:
        qch = _to_chunks(q, GDN_CHUNK)
        xs = xs + (qch * jnp.exp(gam)[..., None], jnp.einsum('nbhtk,nbhsk->nbhts', qch, k) * decay)

    def step(S, xs_c):
        u_c, w_c, ke_c, ge_c = xs_c[:4]
        v_new = u_c - jnp.einsum('bhlk,bhkv->bhlv', w_c, S)
        S_new = jnp.exp(ge_c)[..., None, None] * S + jnp.einsum('bhlk,bhlv->bhkv', ke_c, v_new)
        if not with_out:
            return S_new, None
        qd_c, qk_c = xs_c[4:]
        o = jnp.einsum('bhlk,bhkv->bhlv', qd_c, S) + jnp.einsum('bhts,bhsv->bhtv', qk_c, v_new)
        return S_new, o

    state, o = lax.scan(step, state, xs)
    return state, (_from_chunks(o) if with_out else None)

def _flip_all(arrs):
    return tuple(None if a is None else jnp.flip(a, axis=1) for a in arrs)

def _bidirectional(scan_fn, lat_feats, ctx_feats, lat_gates, ctx_gates, need_ctx_out):
    y_lat, y_ctx = None, None
    for d in range(2):
        lf, cf, lg, cg = lat_feats, ctx_feats, lat_gates[d], ctx_gates[d]
        if d == 1:
            lf, cf, lg, cg = _flip_all(lf), _flip_all(cf), _flip_all(lg), _flip_all(cg)
        ctx_state, c_out = scan_fn(cf, cg, None, need_ctx_out)
        _, l_out = scan_fn(lf, lg, ctx_state, True)
        if d == 1:
            l_out = jnp.flip(l_out, axis=1)
            c_out = None if c_out is None else jnp.flip(c_out, axis=1)
        y_lat = l_out if y_lat is None else y_lat + l_out
        if need_ctx_out:
            y_ctx = c_out if y_ctx is None else y_ctx + c_out
    return y_lat, y_ctx

def _short_conv(x, w):
    y = lax.conv_general_dilated(x, w[:, None, :].astype(x.dtype), window_strides=(1,),
                                 padding=((CONV_K // 2, CONV_K // 2),),
                                 dimension_numbers=('NWC', 'WIO', 'NWC'),
                                 feature_group_count=x.shape[-1])
    return jax.nn.silu(y)

def _token_mixer(xn_lat, xn_ctx, rows, need_ctx_out, w_in, qk_norm_w, sink, ml_i_bias, ml_f_bias,
                 ml_norm_w, conv_w, a_log, dt_bias, gdn_norm_w, w_branch, w_out):
    dt = xn_lat.dtype
    f32 = jnp.float32
    pl = _in_proj(xn_lat, w_in, ())
    pc = _in_proj(xn_ctx, w_in, () if need_ctx_out else CTX_OUTPUT_ONLY_PARTS)

    q_l = _axial_rope(_rmsnorm(_heads(pl[0], ATT_HEADS), qk_norm_w[0]), rows)
    k_l = _axial_rope(_rmsnorm(_heads(pl[1], ATT_KV_HEADS), qk_norm_w[1]), rows)
    v_l = _heads(pl[2], ATT_KV_HEADS)
    k_c = _rmsnorm(_heads(pc[1], ATT_KV_HEADS), qk_norm_w[1])
    v_c = _heads(pc[2], ATT_KV_HEADS)
    ya_l = _latent_window_attention(q_l, k_l, v_l, k_c, v_c, sink)

    def ml_inputs(p):
        q = None if p[3] is None else _heads(p[3], ML_HEADS) * (ML_HD ** -0.5)
        feats = (q, _heads(p[4], ML_HEADS), _heads(p[5], ML_HEADS))
        ig = _heads(p[7].astype(f32), 2) + ml_i_bias
        lf = jax.nn.log_sigmoid(_heads(p[8].astype(f32), 2) + ml_f_bias)
        return feats, ((ig[:, :, 0], lf[:, :, 0]), (ig[:, :, 1], lf[:, :, 1]))

    ml_fl, ml_gl = ml_inputs(pl)
    ml_fc, ml_gc = ml_inputs(pc)
    hm_l, hm_c = _bidirectional(_mlstm_scan, ml_fl, ml_fc, ml_gl, ml_gc, need_ctx_out)

    def ml_out(h, p):
        hn = _rmsnorm(h, ml_norm_w).reshape(h.shape[:2] + (ML_W,))
        return (hn * jax.nn.sigmoid(p[6].astype(f32))).astype(dt)

    def gdn_inputs(p):
        q = None if p[9] is None else _l2norm(_heads(_short_conv(p[9], conv_w[0]), GDN_HEADS)) * (GDN_HD ** -0.5)
        k = _l2norm(_heads(_short_conv(p[10], conv_w[1]), GDN_HEADS))
        v = _heads(_short_conv(p[11], conv_w[2]), GDN_HEADS).astype(f32)
        beta = jax.nn.sigmoid(_heads(p[13].astype(f32), 2))
        g = -jnp.exp(a_log.astype(f32)) * jax.nn.softplus(_heads(p[14].astype(f32), 2) + dt_bias)
        return (q, k, v), ((g[:, :, 0], beta[:, :, 0]), (g[:, :, 1], beta[:, :, 1]))

    gd_fl, gd_gl = gdn_inputs(pl)
    gd_fc, gd_gc = gdn_inputs(pc)
    og_l, og_c = _bidirectional(_gdn_scan, gd_fl, gd_fc, gd_gl, gd_gc, need_ctx_out)

    def gdn_out(o, p):
        on = _rmsnorm(o, gdn_norm_w).reshape(o.shape[:2] + (GDN_W,))
        return (on * jax.nn.silu(p[12].astype(f32))).astype(dt)

    def merge(ya, ym, yg, p):
        gate = jax.nn.sigmoid(_heads(p[15], N_BRANCH))
        y = (gate[..., 0, :] * (ya @ w_branch[0]) + gate[..., 1, :] * (ym @ w_branch[1])
             + gate[..., 2, :] * (yg @ w_branch[2]))
        return y @ w_out

    out_lat = merge(ya_l, ml_out(hm_l, pl), gdn_out(og_l, pl), pl)
    out_ctx = None
    if need_ctx_out:
        q_c = _rmsnorm(_heads(pc[0], ATT_HEADS), qk_norm_w[0])
        ya_c = _context_attention(q_c, k_c, v_c, sink)
        out_ctx = merge(ya_c, ml_out(hm_c, pc), gdn_out(og_c, pc), pc)
    return out_lat, out_ctx

def setup_inputs(seed: int = 0) -> dict:
    key = jax.random.key(seed)
    ks = jax.random.split(key, 22)
    f32 = jnp.float32

    def nrm(k, shape, scale):
        return jax.random.normal(k, shape, f32) * scale

    x = nrm(ks[0], (BATCH, SEQ, D_MODEL), 1.0)
    c = nrm(ks[1], (BATCH, D_MODEL), 1.0)
    ctx = nrm(ks[2], (BATCH, CTX_LEN, D_MODEL), 1.0)
    c_ctx = nrm(ks[3], (D_MODEL,), 1.0)
    w_ada = nrm(ks[4], (DEPTH, D_MODEL, N_MOD * D_MODEL), 0.5 * D_MODEL ** -0.5)
    b_ada = nrm(ks[5], (DEPTH, N_MOD * D_MODEL), 0.02)
    norm_w = 1.0 + nrm(ks[6], (DEPTH, 3, D_MODEL), 0.1)
    ffn_w_gate = nrm(ks[7], (DEPTH, 2, D_MODEL, D_FF), D_MODEL ** -0.5)
    ffn_w_up = nrm(ks[8], (DEPTH, 2, D_MODEL, D_FF), D_MODEL ** -0.5)
    ffn_w_down = nrm(ks[9], (DEPTH, 2, D_FF, D_MODEL), D_FF ** -0.5)
    w_in = nrm(ks[10], (DEPTH, D_MODEL, N_IN), D_MODEL ** -0.5)
    attn_qk_norm = 1.0 + nrm(ks[11], (DEPTH, 2, ATT_HD), 0.1)
    attn_sink = nrm(ks[12], (DEPTH, ATT_HEADS), 1.0)
    ml_i_bias = nrm(ks[13], (DEPTH, 2, ML_HEADS), 0.1)
    ml_f_bias = jnp.linspace(3.0, 6.0, ML_HEADS, dtype=f32) + nrm(ks[14], (DEPTH, 2, ML_HEADS), 0.1)
    ml_norm_w = 1.0 + nrm(ks[15], (DEPTH, ML_HEADS, ML_HD), 0.1)
    gdn_conv_w = nrm(ks[16], (DEPTH, 3, CONV_K, GDN_W), CONV_K ** -0.5)
    gdn_a_log = jnp.log(jax.random.uniform(ks[17], (DEPTH, 2, GDN_HEADS), f32, 1.0, 16.0))
    dt0 = jnp.exp(jax.random.uniform(ks[18], (DEPTH, 2, GDN_HEADS), f32, math.log(1e-3), math.log(1e-1)))
    gdn_dt_bias = dt0 + jnp.log(-jnp.expm1(-dt0))
    gdn_norm_w = 1.0 + nrm(ks[19], (DEPTH, GDN_HD), 0.1)
    w_branch = nrm(ks[20], (DEPTH, N_BRANCH, D_MODEL, D_MODEL), D_MODEL ** -0.5)
    w_out = nrm(ks[21], (DEPTH, D_MODEL, D_MODEL), D_MODEL ** -0.5)
    return {'x': x, 'c': c, 'ctx': ctx, 'c_ctx': c_ctx, 'w_ada': w_ada, 'b_ada': b_ada, 'norm_w': norm_w,
            'ffn_w_gate': ffn_w_gate, 'ffn_w_up': ffn_w_up, 'ffn_w_down': ffn_w_down, 'w_in': w_in,
            'attn_qk_norm': attn_qk_norm, 'attn_sink': attn_sink, 'ml_i_bias': ml_i_bias,
            'ml_f_bias': ml_f_bias, 'ml_norm_w': ml_norm_w, 'gdn_conv_w': gdn_conv_w, 'gdn_a_log': gdn_a_log,
            'gdn_dt_bias': gdn_dt_bias, 'gdn_norm_w': gdn_norm_w, 'w_branch': w_branch, 'w_out': w_out}

def reference(x, c, ctx, c_ctx, w_ada, b_ada, norm_w, ffn_w_gate, ffn_w_up, ffn_w_down, w_in,
              attn_qk_norm, attn_sink, ml_i_bias, ml_f_bias, ml_norm_w, gdn_conv_w, gdn_a_log,
              gdn_dt_bias, gdn_norm_w, w_branch, w_out):
    rows = x.shape[1] // GRID_W
    h, hc = x, ctx
    for l in range(DEPTH):
        last = l == DEPTH - 1
        mod = _adaln(c, w_ada[l], b_ada[l])
        mod_c = _adaln(c_ctx[None], w_ada[l], b_ada[l])
        ffn_pre = (ffn_w_gate[l, 0], ffn_w_up[l, 0], ffn_w_down[l, 0])
        ffn_post = (ffn_w_gate[l, 1], ffn_w_up[l, 1], ffn_w_down[l, 1])
        h = _gated_residual(h, mod, 0, _swiglu(_modulated_norm(h, mod, 0, norm_w[l, 0]), *ffn_pre), 0.5)
        hc = _gated_residual(hc, mod_c, 0, _swiglu(_modulated_norm(hc, mod_c, 0, norm_w[l, 0]), *ffn_pre), 0.5)
        y, yc = _token_mixer(_modulated_norm(h, mod, 1, norm_w[l, 1]), _modulated_norm(hc, mod_c, 1, norm_w[l, 1]),
                             rows, not last, w_in[l], attn_qk_norm[l], attn_sink[l], ml_i_bias[l], ml_f_bias[l],
                             ml_norm_w[l], gdn_conv_w[l], gdn_a_log[l], gdn_dt_bias[l], gdn_norm_w[l],
                             w_branch[l], w_out[l])
        h = _gated_residual(h, mod, 1, y, 1.0)
        h = _gated_residual(h, mod, 2, _swiglu(_modulated_norm(h, mod, 2, norm_w[l, 2]), *ffn_post), 0.5)
        if not last:
            hc = _gated_residual(hc, mod_c, 1, yc, 1.0)
            hc = _gated_residual(hc, mod_c, 2, _swiglu(_modulated_norm(hc, mod_c, 2, norm_w[l, 2]), *ffn_post), 0.5)
    return h


_drawn_inputs = setup_inputs


def setup_inputs(seed=0):
    import zlib

    import numpy as np

    out = dict(_drawn_inputs(seed))
    spreads = {}
    factors = {'attn_qk_norm': 8.0,
     'attn_sink': 8.0,
     'ml_i_bias': 8.0,
     'ml_norm_w': 4.092,
     'gdn_norm_w': 3.353}
    for name, (base, spread) in spreads.items():
        noise = np.random.default_rng([zlib.crc32(name.encode()), seed]).standard_normal(out[name].shape)
        drawn = base * np.exp(spread * noise) if base else spread * noise
        out[name] = __import__('jax').numpy.asarray(drawn.astype(out[name].dtype))
    for name, factor in factors.items():
        out[name] = (out[name] * factor).astype(out[name].dtype)
    return out
```

```python
from contextlib import contextmanager

import numpy as np
import concourse.bass as bass
from concourse import mybir

F32 = mybir.dt.float32
F32R = mybir.dt.float32r
BF16 = mybir.dt.bfloat16
ALU = mybir.AluOpType
ACT = mybir.ActivationFunctionType
AX = mybir.AxisListType

P = 128
DEPTH, D, DFF, NMOD = 2, 1024, 2816, 9
KT = D // P
FT = DFF // P
CTX, SEQ = 256, 256
T = CTX + SEQ
NB = T // P
HALVES = ((0, CTX), (CTX, T))
EPS = 1e-6
FAR = 1e30
AH, AKV, AG = 8, 2, 4
MH, MT = 4, 2
GH = 8
CONV_K = 5
SPLITS = (1024, 256, 256, 1024, 1024, 1024, 1024, 8, 8, 1024, 1024, 1024, 1024, 16, 16, 3072)
OFF = [sum(SPLITS[:i]) for i in range(len(SPLITS) + 1)]

ML_ROW = (0, 32)
GD_ROW = (64, 96)

S_BADA, S_NORM, S_CONV, S_QKN, S_SINK = 0, 72, 96, 216, 218
S_MLN, S_GDN, S_BA, S_BB, S_SGN, S_ALOG = 226, 234, 235, 236, 237, 238
S_LAYER = 240
S_COND = DEPTH * S_LAYER
S_ALL = S_COND + 16
C_ID, C_ONE, C_ROT, C_COS, C_SIN, C_WIN, C_MIN, C_LEV = 0, 128, 256, 384, 640, 896, 1408, 1664
DOWN_CUTS = ((0, 8), (8, 7), (15, 7))
LEVELS = (1, 2, 4, 8, 16, 32, 64)
C_ALL = C_LEV
GDN_STEPS = 37
MLSTM_STEPS = 16
M_ALL = 2 * len(LEVELS) * P


class Event:

    def __init__(self, sem, per, times, credit=0):
        self.sem, self.per, self.times, self.credit = sem, per, times, credit

    def n(self, run, turn, j):
        return turn * self.per + (run * self.times * self.per + j + 1 + self.credit)


class Chain:

    def __init__(self, eng, sem):
        self.eng, self.sem, self.count, self.turn = eng, sem, 0, None

    def __call__(self, ins):
        ins.then_inc(self.sem, 1)
        self.count += 1
        self.eng.wait_ge(self.sem, self.count if self.turn is None else self.turn + self.count)

    @contextmanager
    def turns(self, start, end, per):
        base = self.count
        with self.eng.Fori(start, end) as i:
            self.turn = (i - start) * per
            yield i
        assert self.count == base + per, (self.count - base, per)
        self.turn = None
        self.count = base + per * (end - start)


class Job:

    def __init__(self, turns, units):
        self.turns, self.units = turns, units


def layer_steps(l):
    return [("norm", l, 0), ("ffn", l, 0), ("norm", l, 1), ("gates", l, 0), ("gdn", l, 0), ("merge", l, 2),
            ("mlstm", l, 0), ("merge", l, 1), ("attn", l, 0), ("merge", l, 0), ("out", l, 0),
            ("norm", l, 2), ("ffn", l, 1)]


STEPS = [s for l in range(DEPTH) for s in layer_steps(l)]


def weight_jobs(w_gates, w_gate, w_up, w_down, w_in, w_branch, w_out):
    jobs = {}
    for step in STEPS:
        kind, l, p = step
        if kind == "ffn":
            gu = []
            for j in range(2):
                gu += [(w_gate[l, p], 0, KT, P * j, 2 * P), (w_up[l, p], 0, KT, P * j, 2 * P)]
            down = [(w_down[l, p], P * k0, kn, P * j, 4 * P) for j in range(4) for k0, kn in DOWN_CUTS]
            jobs[step] = [Job(FT // 2, gu), Job(2, down)]
        elif kind == "gates":
            jobs[step] = [Job(1, [(w_gates[l], 0, KT, P * j, 0) for j in range(2)])]
        elif kind == "gdn":
            jobs[step] = [Job(GH, [(w_in[l], 0, KT, OFF[c], P) for c in (9, 10, 11, 12)])]
        elif kind == "mlstm":
            jobs[step] = [Job(MH, [(w_in[l], 0, KT, OFF[c] + P * t, MT * P) for c in (3, 4, 5, 6) for t in range(MT)])]
        elif kind == "attn":
            jobs[step] = [Job(1, [(w_in[l], 0, KT, OFF[1] + P * g, 0), (w_in[l], 0, KT, OFF[2] + P * g, 0)]
                              + [(w_in[l], 0, KT, OFF[0] + P * (AG * g + q), 0) for q in range(AG)])
                          for g in range(AKV)]
        elif kind == "merge":
            units = []
            for j in range(2):
                units += [(w_in[l], 0, KT, OFF[15] + p * D + P * j, 2 * P), (w_branch[l, p], 0, KT, P * j, 2 * P)]
            jobs[step] = [Job(KT // 2, units)]
        elif kind == "out":
            jobs[step] = [Job(2, [(w_out[l], 0, KT, P * j, 4 * P) for j in range(4)])]
        else:
            jobs[step] = []
    return jobs


def trunk_kernel(nc, tokens, smalls, consts, levels, w_ada, w_gates, w_gate, w_up, w_down, w_in, w_branch,
                 w_out, out, debug=None):
    jobs = weight_jobs(w_gates, w_gate, w_up, w_down, w_in, w_branch, w_out)

    at = [nc.sbuf_base]
    top = nc.sbuf_usable_end

    def place(name, shape, dt, where=None):
        size = int(np.prod(shape[1:])) * (2 if dt == BF16 else 4)
        where = at if where is None else where
        where[0] = (where[0] + 31) // 32 * 32
        t = nc.alloc_sbuf_tensor_at(name, shape, dt, offset=where[0])
        where[0] += size
        assert where[0] <= top, (name, where[0], top)
        return t

    H = place("H", [P, KT * T], F32)
    xn_hi = place("xn_hi", [P, KT, T], F32R)
    xn_lo = place("xn_lo", [P, KT, T], F32R)
    raw = place("raw", [P, 4, KT * P], F32)
    w_hi = place("w_hi", [P, 2, KT * P], F32R)
    w_lo = place("w_lo", [P, 2, KT * P], F32R)
    con = place("con", [P, C_ALL], F32)
    lev = place("lev", [P, M_ALL], BF16)
    sml = place("sml", [P, S_ALL], F32)
    cond = place("cond", [P, KT, 2], F32)
    mod = place("mod", [P, DEPTH, NMOD * KT, 2], F32)
    nscale = place("nscale", [P, DEPTH, 3, KT, 2], F32)
    rgate = place("rgate", [P, DEPTH, 3, KT, 2], F32)
    arena = at[0]

    ident, ones, rot = con[:, C_ID:C_ID + P], con[:, C_ONE:C_ONE + P], con[:, C_ROT:C_ROT + P]

    a = [arena]
    wide = [place(f"wide{j}", [P, KT, 512], F32, a) for j in range(2)]
    lev_f = place("lev_f", [P, M_ALL], F32, a)
    a = [arena]
    sq = place("sq", [P, KT, T], F32, a)
    rms = place("rms", [P, T], F32, a)
    a = [arena]
    hid_hi = place("hid_hi", [P, FT * T], F32R, a)
    hid_lo = place("hid_lo", [P, FT * T], F32R, a)
    silu_g = place("silu_g", [P, 2, T], F32, a)
    hid = place("hid", [P, 2, T], F32, a)

    a = [arena]
    gate_a = place("gate_a", [P, T], F32, a)
    rows_m = place("rows_m", [P, T], F32, a)
    rows_n = place("rows_n", [P, T], F32, a)
    col_a = place("col_a", [P, NB, P], F32, a)
    col_g = place("col_g", [P, NB, P], F32, a)
    col_b = place("col_b", [P, NB, P // 2], F32, a)
    y_hi = place("y_hi", [P, KT * T], F32R, a)
    y_lo = place("y_lo", [P, KT * T], F32R, a)
    mix = a[0]
    y_sum = place("y_sum", [P, KT * T], F32, a)
    branch = a[0]
    a = [mix]
    zed = place("zed", [P, T], F32, a)
    sofp = place("sofp", [P, T], F32, a)
    cum = place("cum", [P, T], F32, a)
    unit_row = place("unit_row", [P, T], F32, a)
    run_max = place("run_max", [P, T], F32, a)
    coef = place("coef", [P, 1], F32, a)
    PAD = CONV_K // 2
    a = [mix]
    padded = place("padded", [P, 3, 2, CTX + 2 * PAD], F32, a)
    conv = place("conv", [P, 3, T], F32, a)
    qkv = place("qkv", [P, 3, T], F32, a)
    g_gate = place("g_gate", [P, T], F32, a)
    k_tok = place("k_tok", [P, NB, P], F32, a)
    v_tok = place("v_tok", [P, NB, P], F32, a)
    o_sum = place("o_sum", [P, T], F32, a)
    conv_w = place("conv_w", [P, 3 * CONV_K], F32, a)
    pick = place("pick", [P, 2, P], F32, a)
    lane_col = place("lane_col", [P, 2, 3, NB], F32, a)
    end_col = place("end_col", [P, 2, 2, NB], F32, a)
    decay = place("decay", [P, 2, NB, P], F32, a)
    p_t = place("p_t", [P, 2, NB, P], F32, a)
    a_mat = place("a_mat", [P, 2, NB, P], F32, a)
    inv = place("inv", [P, 2, NB, P], F32, a)
    inv_t = place("inv_t", [P, 2, NB, P], F32, a)
    prod = place("prod", [P, 2, NB, P], F32, a)
    q_dec = place("q_dec", [P, 2, NB, P], F32, a)
    k_end = place("k_end", [P, 2, NB, P], F32, a)
    v_beta = place("v_beta", [P, 2, NB, P], F32, a)
    resid = place("resid", [P, 2, P], F32, a)
    v_new = place("v_new", [P, 2, P], F32, a)
    state = place("state", [P, 2, P], F32, a)
    a = [branch]
    m_qkv = place("m_qkv", [P, 3, MT, T], F32, a)
    m_gate = place("m_gate", [P, MT, T], F32, a)
    m_vtok = place("m_vtok", [P, NB, MT * P], F32, a)
    m_w = place("m_w", [P, NB, T], F32, a)
    m_den = place("m_den", [P, T], F32, a)
    m_floor = place("m_floor", [P, T], F32, a)
    m_h = place("m_h", [P, MT, T], F32, a)
    m_tmp = place("m_tmp", [P, MT, T], F32, a)
    m_pick = place("m_pick", [P, 2, P], F32, a)
    m_wn = place("m_wn", [P, MT], F32, a)
    m_col = place("m_col", [P, 2, NB], F32, a)
    a = [branch]
    t_raw = place("t_raw", [P, 6, T], F32, a)
    t_sq = place("t_sq", [P, 2, T], F32, a)
    t_rot = place("t_rot", [P, SEQ], F32, a)
    t_vtok = place("t_vtok", [P, NB, P], F32, a)
    t_s = place("t_s", [P, 2, T], F32, a)
    t_pt = place("t_pt", [P, NB, AG, P], F32, a)
    t_o = place("t_o", [P, AG, P], F32, a)
    t_col = place("t_col", [P, 2, 6], F32, a)
    t_w = place("t_w", [P, 2], F32, a)
    a = [branch]
    b_gate = place("b_gate", [P, 2, T], F32, a)
    b_tmp = place("b_tmp", [P, 2, T], F32, a)

    bank = [nc.alloc_psum_tensor(f"bank{i}", [P, 512], F32) for i in range(8)]

    def event(name, per, times, credit=0):
        return Event(nc.alloc_semaphore(name), per, times, credit)

    dma_small = nc.alloc_semaphore("dma_small")
    dma_wide = [nc.alloc_semaphore(f"dma_wide{j}") for j in range(2)]
    raw_landed = [nc.alloc_semaphore(f"raw_landed{j}") for j in range(4)]
    hi_done = nc.alloc_semaphore("hi_done")
    split_done = nc.alloc_semaphore("split_done")
    unit_done = nc.alloc_semaphore("unit_done")
    out_done = nc.alloc_semaphore("out_done")
    ada_done = event("ada_done", NMOD * 2, DEPTH)
    cond_done = event("cond_done", 1, 1)
    mod_done = event("mod_done", 1, 1)
    dve_step, pool_turn, sp_turn = (nc.alloc_semaphore(n) for n in ("dve_step", "pool_turn", "sp_turn"))

    sq_done = event("sq_done", KT, 1)
    ss_done = event("ss_done", 1, 1)
    rvar_done = event("rvar_done", 1, 1)
    rms_done = event("rms_done", 1, 1)
    nmul_done = event("nmul_done", KT, 1)
    nmod_done = event("nmod_done", KT, 1)
    xn_ready = event("xn_ready", KT, 1)
    stream_ready = event("stream_ready", KT, 1)
    silu_done = event("silu_done", 2, FT // 2)
    hid_ready = event("hid_ready", 2, FT // 2, credit=2)
    res_done = event("res_done", 4, 2, credit=2)

    gate_act = event("gate_act", 6, 1)
    gate_dve = event("gate_dve", 3, 1)
    gate_pe = event("gate_pe", 2, 1)
    pad_zeroed = event("pad_zeroed", 1, 1)
    conv_filled = event("conv_filled", 3, GH, credit=1)
    conv_done = event("conv_done", 3, GH, credit=3)
    conv_silu = event("conv_silu", 3, GH)
    g_gate_done = event("g_gate_done", 1, GH, credit=1)
    qk_sq = event("qk_sq", 2, GH)
    qk_ss = event("qk_ss", 2, GH)
    qk_var = event("qk_var", 2, GH)
    qk_rms = event("qk_rms", 2, GH)
    qk_ready = event("qk_ready", 2, GH)
    tok_t = event("tok_t", 2, GH)
    tok_ready = event("tok_ready", 2, GH)
    kk_done = event("kk_done", 2, GH)
    pick_ready = event("pick_ready", 2, GH)
    gam_row = event("gam_row", 2, GH)
    exp_gam = event("exp_gam", 2, GH)
    arg_ready = event("arg_ready", 2, GH)
    decay_done = event("decay_done", 2, GH)
    l_ready = event("l_ready", 2, GH)
    l_turned = event("l_turned", 2, GH)
    a_ready = event("a_ready", 2, GH)
    inv0_ready = event("inv0_ready", 2, GH)
    inv0_turned = event("inv0_turned", 2, GH)
    inv0_copied = event("inv0_copied", 2, GH)
    NL = len(LEVELS) - 1
    block_ready = event("block_ready", 2 * NL, GH)
    prod_done = event("prod_done", 2 * NL, GH)
    prod_ready = event("prod_ready", 2 * NL, GH)
    corr_done = event("corr_done", 2 * NL, GH)
    inv_ready = event("inv_ready", 2 * NL, GH)
    lane_ready = event("lane_ready", 2, GH)
    ks_done = event("ks_done", 2 * (NB - 1), GH)
    resid_ready = event("resid_ready", 2 * NB, GH)
    v_new_done = event("v_new_done", 2 * NB, GH)
    v_new_ready = event("v_new_ready", 2 * NB, GH)
    ds_done = event("ds_done", 2 * (NB - 1), GH)
    state_ready = event("state_ready", 2 * (NB - 1), GH)
    o_done = event("o_done", 2, GH)
    o_first = event("o_first", 1, GH)
    o_both = event("o_both", 1, GH)
    o_sq = event("o_sq", 1, GH)
    o_ss = event("o_ss", 1, GH)
    o_var = event("o_var", 1, GH)
    o_rms = event("o_rms", 1, GH)
    head_done = event("head_done", 1, GH, credit=1)
    m_filled = event("m_filled", 8, MH, credit=8)
    m_vt = event("m_vt", MT, MH)
    m_vt_ready = event("m_vt_ready", MT, MH, credit=MT)
    m_picked = event("m_picked", 2, MH)
    m_kq = event("m_kq", 3, MH)
    m_rows = event("m_rows", 2, MH)
    m_arg = event("m_arg", 2, MH)
    m_exp = event("m_exp", 2, MH)
    m_weighted = event("m_weighted", 2, MH)
    m_num = event("m_num", 2, MH)
    m_abs = event("m_abs", 2, MH)
    m_added = event("m_added", 2, MH, credit=2)
    m_sq = event("m_sq", 1, MH)
    m_ss = event("m_ss", 1, MH)
    m_var = event("m_var", 1, MH)
    m_rms = event("m_rms", 1, MH)
    m_head = event("m_head", 1, MH, credit=1)
    NU = 2 + AG
    t_filled = event("t_filled", NU, AKV, credit=NU)
    t_sqd = event("t_sqd", NU - 1, AKV)
    t_ss = event("t_ss", NU - 1, AKV)
    t_var = event("t_var", NU - 1, AKV)
    t_rms = event("t_rms", NU - 1, AKV)
    t_normed = event("t_normed", NU - 1, AKV)
    t_turned = event("t_turned", NU - 1, AKV)
    t_roped = event("t_roped", NU - 1, AKV)
    t_vt = event("t_vt", 1, AKV)
    t_vt_ready = event("t_vt_ready", 1, AKV)
    NQ = NB * AG
    t_scored = event("t_scored", NQ, AKV)
    t_masked = event("t_masked", NQ, AKV)
    t_exp = event("t_exp", NQ, AKV)
    t_prob = event("t_prob", NQ, AKV)
    t_pturn = event("t_pturn", NQ, AKV)
    t_pcopied = event("t_pcopied", NQ, AKV)
    t_out = event("t_out", NB, AKV)
    t_ocopy = event("t_ocopy", NB, AKV)
    t_osplit = event("t_osplit", NB, AKV)
    b_sig = event("b_sig", 2, KT // 2)
    b_done = event("b_done", 2, KT // 2, credit=2)
    y_split = event("y_split", KT, 1)
    out_res = event("out_res", 4, 2, credit=2)
    credits = (out_res, m_added, m_head, hid_ready, res_done, conv_done, head_done, b_done)

    def scan_order(d):
        return (0, 1, 2, 3) if d == 0 else (1, 0, 3, 2)

    def chunk_end(d):
        return P - 1 if d == 0 else 0

    merge_run = {s: n for n, s in enumerate(s for s in STEPS if s[0] == "merge")}

    def branch_whole(l, p):
        if p == 2:
            return head_done.sem, head_done.n(l, GH - 1, 0)
        if p == 1:
            return m_head.sem, m_head.n(l, MH - 1, 0)
        return t_osplit.sem, t_osplit.n(l, AKV - 1, NB - 1)

    def reach(d, sb):
        t0, t1 = P * sb, P * sb + P
        spans = [(t0, t1, True)]
        if d == 0:
            spans += [(t1, T, False)] if t1 < T else []
        else:
            lo = 0 if t0 < CTX else CTX
            spans += [(lo, t0, False)] if lo < t0 else []
            spans += [(CTX, T, False)] if t0 < CTX else []
        return spans

    def joined(d, sb):
        out = []
        for t0, t1, _ in sorted(reach(d, sb)):
            if out and out[-1][1] == t0:
                out[-1] = (out[-1][0], t1)
            else:
                out.append((t0, t1))
        return out

    def by_reach(d):
        return (0, 1, 2, 3) if d == 0 else (1, 0, 3, 2)

    def kq_view(sb):
        return (bank[2 + sb], 0, 0) if sb < 2 else (bank[4], CTX * (sb - 2), CTX)

    block = nc.Block()
    blk = block.__enter__()

    first_unit, u = {}, 0
    for step in STEPS:
        for n, job in enumerate(jobs[step]):
            first_unit[step, n] = u
            u += job.turns * len(job.units)

    def norm_run(l, j):
        return 3 * l + j

    @blk.sync
    def _(sp):
        sp.dma_start(sml[:, :], smalls).then_inc(dma_small, 16)
        sp.dma_start(con[:, :], consts).then_inc(dma_small, 16)
        sp.dma_start(lev_f[:, :], levels).then_inc(dma_small, 16)
        sp.dma_start(H[:, :].rearrange("p (k t) -> p k t", k=KT),
                     tokens.rearrange("(k p) t -> p k t", p=P)).then_inc(dma_small, 16)
        for l in range(DEPTH):
            for n in range(NMOD * 2):
                g = l * NMOD * 2 + n
                if g >= 2:
                    sp.wait_ge(ada_done.sem, ada_done.n(0, 0, g - 2))
                sp.dma_start(wide[g % 2][:, :, :], w_ada[l, :, 512 * n:512 * n + 512].rearrange(
                    "(k p) n -> p k n", p=P)).then_inc(dma_wide[g % 2], 16)

        def load(u, turn_units, i, unit):
            w, row, kn, col, step = unit
            if not isinstance(i, int) or u + turn_units * i >= 4:
                sp.wait_ge(split_done, turn_units * i + (u - 3))
                if not isinstance(i, int):
                    sp.sem_inc(sp_turn, 1)
            src = w[row:row + P * kn, bass.ds(i * step + col, P)] if not isinstance(i, int) else \
                w[row:row + P * kn, i * step + col:i * step + col + P]
            sp.dma_start(raw[:, u % 4, 0:kn * P].rearrange("p (k n) -> p k n", k=kn),
                         src.rearrange("(k p) n -> p k n", p=P)).then_inc(raw_landed[u % 4], 16)

        for step in STEPS:
            for n, job in enumerate(jobs[step]):
                u0, m = first_unit[step, n], len(job.units)
                start = 0
                if job.turns == 1 or u0 < 4:
                    for j, unit in enumerate(job.units):
                        load(u0 + j, m, 0, unit)
                    start = 1
                if start < job.turns:
                    with sp.Fori(start, job.turns) as i:
                        for j, unit in enumerate(job.units):
                            load(u0 + j, m, i, unit)
        sp.wait_ge(stream_ready.sem, stream_ready.n(len([s for s in STEPS if s[0] == "norm"]) - 1, 0, KT - 1))
        sp.dma_start(out.rearrange("(k p) t -> p k t", p=P),
                     H[:, :].rearrange("p (k t) -> p k t", k=KT)[:, :, CTX:T]).then_inc(out_done, 16)
        sp.wait_ge(out_done, 16)

    @blk.gpsimd
    def _(pool):
        def split(u, turn_units, i, kn):
            n = kn * P
            pool.wait_ge(raw_landed[u % 4], i * (4 * turn_units) + (16 * (u // 4) + 16))
            if not isinstance(i, int) or u + turn_units * i >= 2:
                pool.wait_ge(unit_done, turn_units * i + (u - 1))
            if not isinstance(i, int):
                pool.sem_inc(pool_turn, 1)
            nc.gpsimd.tensor_scalar(w_hi[:, u % 2, 0:n], raw[:, u % 4, 0:n], 1.0, 1.0, ALU.mult,
                                    ALU.mult).then_inc(hi_done, 1)
            pool.wait_ge(hi_done, turn_units * i + (u + 1))
            nc.gpsimd.tensor_tensor(w_lo[:, u % 2, 0:n], raw[:, u % 4, 0:n], w_hi[:, u % 2, 0:n].bitcast(F32),
                                    ALU.subtract).then_inc(split_done, 1)

        def split_job(step, n, start=0):
            job, u0 = jobs[step][n], first_unit[step, n]
            m = len(job.units)
            if job.turns == 1 or u0 < 2:
                for j, unit in enumerate(job.units):
                    split(u0 + j, m, 0, unit[2])
                start = 1
            if start < job.turns:
                with pool.Fori(start, job.turns) as i:
                    for j, unit in enumerate(job.units):
                        split(u0 + j, m, i, unit[2])

        def level_blocks(l, h):
            for v in range(NL):
                for d in range(2):
                    j = 2 * v + d
                    if v == 0:
                        pool.wait_ge(inv0_ready.sem, inv0_ready.n(l, h, d))
                    else:
                        pool.wait_ge(prod_done.sem, prod_done.n(l, h, j - 2))
                    m = lev[:, (d * len(LEVELS) + v + 1) * P:(d * len(LEVELS) + v + 2) * P].unsqueeze(1)
                    nc.gpsimd.tensor_tensor(decay[:, d, :, :], a_mat[:, d, :, :], m.to_broadcast([P, NB, P]),
                                            ALU.mult).then_inc(block_ready.sem, 1)

        for e in credits:
            if e.credit:
                pool.sem_inc(e.sem, e.credit)
        for step in STEPS:
            kind, l, p = step
            if kind == "gdn":
                job, u0 = jobs[step][0], first_unit[step, 0]
                with pool.Fori(0, GH) as h:
                    for j, un in enumerate(job.units):
                        split(u0 + j, 4, h, un[2])
                    level_blocks(l, h)
            else:
                for n in range(len(jobs[step])):
                    split_job(step, n)

    @blk.tensor
    def _(pe):
        mm = nc.tensor.matmul

        def unit(u, i, m, kn, dst, hi, lo, start=True, stop=True, ready=None):
            pe.wait_ge(split_done, m * i + (u + 1))
            for k in range(kn):
                if ready:
                    ready(k)
                wh, wl = w_hi[:, u % 2, P * k:P * k + P], w_lo[:, u % 2, P * k:P * k + P]
                mm(dst, wh, hi(k), start=start and k == 0, stop=False)
                mm(dst, wh, lo(k), start=False, stop=False)
                last = mm(dst, wl, hi(k), start=False, stop=stop and k == kn - 1)
            return last.then_inc(unit_done, 1)

        def xh(k):
            return xn_hi[:, k, :]

        def xl(k):
            return xn_lo[:, k, :]

        def ada():
            pe.wait_ge(dma_small, 64)
            pe.wait_ge(cond_done.sem, 1)
            for l in range(DEPTH):
                for n in range(NMOD * 2):
                    g = l * NMOD * 2 + n
                    pe.wait_ge(dma_wide[g % 2], 16 * (g // 2 + 1))
                    for t in range(4):
                        c = 2 * (4 * n + t)
                        for k in range(KT):
                            last = mm(bank[l][:, c:c + 2], wide[g % 2][:, k, P * t:P * t + P], cond[:, k, :],
                                      start=k == 0, stop=k == KT - 1)
                    last.then_inc(ada_done.sem, 1)

        def norm(l, j):
            r = norm_run(l, j)
            for k in range(KT):
                pe.wait_ge(sq_done.sem, sq_done.n(r, 0, k))
                last = mm(bank[7][:, :], ones, sq[:, k, :], start=k == 0, stop=k == KT - 1)
            last.then_inc(ss_done.sem, 1)

        def ffn(step, l, p):
            r = 2 * l + p
            u0, nr = first_unit[step, 0], norm_run(l, 2 * p)
            for k in range(KT):
                pe.wait_ge(xn_ready.sem, xn_ready.n(nr, 0, k))
            with pe.Fori(0, FT // 2) as i:
                for j in range(2):
                    pe.wait_ge(hid_ready.sem, hid_ready.n(r, i, j - 2))
                    unit(u0 + 2 * j, i, 4, KT, bank[2 * j][:, :], xh, xl)
                    unit(u0 + 2 * j + 1, i, 4, KT, bank[2 * j + 1][:, :], xh, xl)
            u0 = first_unit[step, 1]
            pe.wait_ge(hid_ready.sem, hid_ready.n(r, FT // 2 - 1, 1))
            with pe.Fori(0, 2) as i:
                for j in range(4):
                    pe.wait_ge(res_done.sem, res_done.n(r, i, j - 2))
                    for c, (k0, kn) in enumerate(DOWN_CUTS):
                        unit(u0 + 3 * j + c, i, 12, kn, bank[4 + j % 2][:, :],
                             lambda k: hid_hi[:, T * (k0 + k):T * (k0 + k) + T],
                             lambda k: hid_lo[:, T * (k0 + k):T * (k0 + k) + T],
                             start=c == 0, stop=c == 2)

        def gates(step, l):
            u0 = first_unit[step, 0]
            for k in range(KT):
                pe.wait_ge(xn_ready.sem, xn_ready.n(norm_run(l, 1), 0, k))
            for j in range(2):
                unit(u0 + j, 0, 2, KT, bank[j][:, :], xh, xl)
            pe.wait_ge(gate_dve.sem, gate_dve.n(l, 0, 1))
            for b in range(NB):
                last = nc.tensor.transpose(bank[2][:, P * b:P * b + P], gate_a[:, P * b:P * b + P], ident)
            last.then_inc(gate_pe.sem, 1)
            for b in range(NB):
                last = nc.tensor.transpose(bank[3][:, P * b:P * b + P], rows_m[:, P * b:P * b + P], ident)
            last.then_inc(gate_pe.sem, 1)

        def gdn_head(l, h, u0):
            q_t, k_t, v_t = (qkv[:, j, :] for j in range(3))

            def blocks(b):
                return slice(P * b, P * b + P)

            for j in range(4):
                if j == 0:
                    pe.wait_ge(conv_filled.sem, conv_filled.n(l, h, -1))
                elif j == 1:
                    pe.wait_ge(g_gate_done.sem, g_gate_done.n(l, h, -1))
                else:
                    pe.wait_ge(conv_filled.sem, conv_filled.n(l, h, j - 2))
                unit(u0 + j, h, 4, KT, bank[j % 2][:, :], xh, xl)
            pe.wait_ge(head_done.sem, head_done.n(l, h, -1))
            for j in range(2):
                pe.wait_ge(qk_sq.sem, qk_sq.n(l, h, j))
                mm(bank[2 + j][:, :], ones, conv[:, j, :], start=True, stop=True).then_inc(qk_ss.sem, 1)
            for d in range(2):
                pe.wait_ge(pick_ready.sem, pick_ready.n(l, h, d))
                mm(bank[4 + 2 * d][:, :], pick[:, d, :], rows_m[:, :], start=True,
                   stop=True).then_inc(gam_row.sem, 1)
            pe.wait_ge(qk_var.sem, qk_var.n(l, h, 1))
            pe.wait_ge(conv_silu.sem, conv_silu.n(l, h, 2))
            for b in range(NB):
                last = nc.tensor.transpose(bank[2][:, blocks(b)], v_t[:, blocks(b)], ident)
            last.then_inc(tok_t.sem, 1)
            pe.wait_ge(qk_ready.sem, qk_ready.n(l, h, 1))
            for b in range(NB):
                last = nc.tensor.transpose(bank[3][:, blocks(b)], k_t[:, blocks(b)], ident)
            last.then_inc(tok_t.sem, 1)
            for j, x in enumerate((k_t, q_t)):
                pe.wait_ge(tok_ready.sem, tok_ready.n(l, h, j))
                for b in range(NB):
                    last = mm(bank[2 + j][:, blocks(b)], k_t[:, blocks(b)], x[:, blocks(b)], start=True, stop=True)
                last.then_inc(kk_done.sem, 1)
            for d in range(2):
                pe.wait_ge(l_ready.sem, l_ready.n(l, h, d))
                for b in range(NB):
                    last = nc.tensor.transpose(bank[5 + 2 * d][:, blocks(b)], prod[:, d, b, :], ident)
                last.then_inc(l_turned.sem, 1)
            for d in range(2):
                pe.wait_ge(inv0_ready.sem, inv0_ready.n(l, h, d))
                for b in range(NB):
                    last = nc.tensor.transpose(bank[4 + 2 * d][:, blocks(b)], inv[:, d, b, :], ident)
                last.then_inc(inv0_turned.sem, 1)
            for v in range(NL):
                for d in range(2):
                    j = 2 * v + d
                    pe.wait_ge(block_ready.sem, block_ready.n(l, h, j))
                    if v == 0:
                        pe.wait_ge(inv0_copied.sem, inv0_copied.n(l, h, d))
                    else:
                        pe.wait_ge(inv_ready.sem, inv_ready.n(l, h, j - 2))
                    for b in range(NB):
                        last = mm(bank[4 + 2 * d][:, blocks(b)], decay[:, d, b, :], inv_t[:, d, b, :],
                                  start=True, stop=True)
                    last.then_inc(prod_done.sem, 1)
                for d in range(2):
                    j = 2 * v + d
                    pe.wait_ge(prod_ready.sem, prod_ready.n(l, h, j))
                    for b in range(NB):
                        last = mm(bank[5 + 2 * d][:, blocks(b)], inv[:, d, b, :], prod[:, d, b, :],
                                  start=True, stop=True)
                    if v < NL - 1:
                        for b in range(NB):
                            last = mm(bank[4 + 2 * d][:, blocks(b)], prod[:, d, b, :], inv[:, d, b, :],
                                      start=True, stop=True)
                    last.then_inc(corr_done.sem, 1)
            for i in range(NB):
                for d in range(2):
                    b = scan_order(d)[i]
                    if i == 0 and d == 0:
                        pe.wait_ge(inv_ready.sem, inv_ready.n(l, h, 2 * NL - 1))
                        pe.wait_ge(lane_ready.sem, lane_ready.n(l, h, 1))
                    elif i > 0:
                        pe.wait_ge(state_ready.sem, state_ready.n(l, h, 2 * (i - 1) + d))
                        mm(bank[4 + 2 * d][:, 0:P], k_t[:, blocks(b)], state[:, d, :], start=True,
                           stop=True).then_inc(ks_done.sem, 1)
                for d in range(2):
                    b = scan_order(d)[i]
                    if i > 0:
                        mm(bank[5 + 2 * d][:, blocks(b)], state[:, d, :], q_dec[:, d, b, :], start=True, stop=False)
                    pe.wait_ge(resid_ready.sem, resid_ready.n(l, h, 2 * i + d))
                    mm(bank[4 + 2 * d][:, P:2 * P], inv_t[:, d, b, :], resid[:, d, :], start=True,
                       stop=True).then_inc(v_new_done.sem, 1)
                for d in range(2):
                    b = scan_order(d)[i]
                    pe.wait_ge(v_new_ready.sem, v_new_ready.n(l, h, 2 * i + d))
                    if i < NB - 1:
                        mm(bank[4 + 2 * d][:, 2 * P:3 * P], k_end[:, d, b, :], v_new[:, d, :], start=True,
                           stop=True).then_inc(ds_done.sem, 1)
                    last = mm(bank[5 + 2 * d][:, blocks(b)], v_new[:, d, :], p_t[:, d, b, :], start=i == 0,
                              stop=True)
                    if i == NB - 1:
                        last.then_inc(o_done.sem, 1)
            pe.wait_ge(o_sq.sem, o_sq.n(l, h, 0))
            mm(bank[2][:, :], ones, conv[:, 0, :], start=True, stop=True).then_inc(o_ss.sem, 1)

        def gdn(step, l):
            with pe.Fori(0, GH) as h:
                gdn_head(l, h, first_unit[step, 0])

        def mlstm_head(l, h, u0):
            for j in range(8):
                pe.wait_ge(m_filled.sem, m_filled.n(l, h, j - 2))
                if j < 2:
                    pe.wait_ge(m_added.sem, m_added.n(l, h, -1))
                unit(u0 + j, h, 8, KT, bank[j % 2][:, :], xh, xl)
            for v in range(MT):
                pe.wait_ge(m_filled.sem, m_filled.n(l, h, 4 + v))
                if v == 0:
                    pe.wait_ge(m_head.sem, m_head.n(l, h, -1))
                for b in range(NB):
                    last = nc.tensor.transpose(bank[5 + v][:, P * b:P * b + P],
                                               m_qkv[:, 2, v, P * b:P * b + P], ident)
                last.then_inc(m_vt.sem, 1)
            for sb in range(NB):
                dst, c0, t0 = kq_view(sb)
                for v in range(MT):
                    last = mm(dst[:, c0:c0 + T - t0], m_qkv[:, 1, v, P * sb:P * sb + P], m_qkv[:, 0, v, t0:T],
                              start=v == 0, stop=v == MT - 1)
                if sb != 2:
                    last.then_inc(m_kq.sem, 1)
            for d in range(2):
                pe.wait_ge(m_picked.sem, m_picked.n(l, h, d))
                if d == 0:
                    pe.wait_ge(m_vt_ready.sem, m_vt_ready.n(l, h, MT - 1))
                else:
                    pe.wait_ge(m_added.sem, m_added.n(l, h, 0))
                mm(bank[5][:, :], m_pick[:, d, :], rows_m[:, :], start=True, stop=True)
                mm(bank[6][:, :], m_pick[0:64, d, :], rows_n[0:64, :], start=True, stop=True).then_inc(m_rows.sem, 1)
                pe.wait_ge(m_weighted.sem, m_weighted.n(l, h, d))
                pe.wait_ge(m_filled.sem, m_filled.n(l, h, 7))
                for n in range(1 + MT):
                    dst = bank[7] if n == 0 else bank[n - 1]
                    for i, sb in enumerate(by_reach(d)):
                        w = ones if n == 0 else m_vtok[:, sb, P * (n - 1):P * n]
                        for c0, c1 in joined(d, sb):
                            last = mm(dst[:, c0:c1], w, m_w[:, sb, c0:c1], start=i == 0, stop=i == NB - 1)
                last.then_inc(m_num.sem, 1)
            pe.wait_ge(m_sq.sem, m_sq.n(l, h, 0))
            for v in range(MT):
                last = mm(bank[5][:, :], ones, m_tmp[:, v, :], start=v == 0, stop=v == MT - 1)
            last.then_inc(m_ss.sem, 1)

        def mlstm(step, l):
            with pe.Fori(0, MH) as h:
                mlstm_head(l, h, first_unit[step, 0])

        def attn_group(l, g, u0):
            for j in range(NU):
                pe.wait_ge(t_filled.sem, t_filled.n(l, g, j - 2))
                unit(u0 + j, 0, 0, KT, bank[j % 2][:, :], xh, xl)
            pe.wait_ge(t_filled.sem, t_filled.n(l, g, 1))
            for b in range(NB):
                last = nc.tensor.transpose(bank[2][:, P * b:P * b + P], t_raw[:, 1, P * b:P * b + P], ident)
            last.then_inc(t_vt.sem, 1)
            for j in range(NU - 1):
                pe.wait_ge(t_sqd.sem, t_sqd.n(l, g, j))
                if j > 0:
                    pe.wait_ge(t_roped.sem, t_roped.n(l, g, j - 1))
                mm(bank[3][:, :], ones, t_sq[:, 0, :], start=True, stop=True).then_inc(t_ss.sem, 1)
                pe.wait_ge(t_normed.sem, t_normed.n(l, g, j))
                n = 0 if j == 0 else j + 1
                mm(bank[4][:, 0:SEQ], rot, t_raw[:, n, CTX:T], start=True, stop=True).then_inc(t_turned.sem, 1)
            pe.wait_ge(t_vt_ready.sem, t_vt_ready.n(l, g, 0))
            pe.wait_ge(t_roped.sem, t_roped.n(l, g, NU - 2))

            def score(n):
                b, q = divmod(n, AG)
                keys = CTX if b < 2 else T
                if n >= 2:
                    pe.wait_ge(t_exp.sem, t_exp.n(l, g, n - 2))
                mm(bank[5 + n % 2][:, 0:keys], t_raw[:, 2 + q, P * b:P * b + P], t_raw[:, 0, 0:keys],
                   start=True, stop=True).then_inc(t_scored.sem, 1)

            score(0)
            for n in range(NQ):
                b, q = divmod(n, AG)
                kb = 2 if b < 2 else NB
                if n + 1 < NQ:
                    score(n + 1)
                pe.wait_ge(t_prob.sem, t_prob.n(l, g, n))
                if n >= 2:
                    pe.wait_ge(t_pcopied.sem, t_pcopied.n(l, g, n - 2))
                for k in range(kb):
                    last = nc.tensor.transpose(bank[2 + n % 2][:, P * k:P * k + P],
                                               t_s[:, n % 2, P * k:P * k + P], ident)
                last.then_inc(t_pturn.sem, 1)
                if q == AG - 1:
                    pe.wait_ge(t_pcopied.sem, t_pcopied.n(l, g, n))
                    if b > 0:
                        pe.wait_ge(t_ocopy.sem, t_ocopy.n(l, g, b - 1))
                    for k in range(kb):
                        last = mm(bank[7][:, :], t_vtok[:, k, :],
                                  t_pt[:, k, :, :].rearrange("p q t -> p (q t)"), start=k == 0, stop=k == kb - 1)
                    last.then_inc(t_out.sem, 1)

        def attn(step, l):
            for g in range(AKV):
                attn_group(l, g, first_unit[step, g])

        def merge(step, l, p):
            u0, r = first_unit[step, 0], merge_run[step]
            pe.wait_ge(*branch_whole(l, p))
            with pe.Fori(0, KT // 2) as i:
                for j in range(2):
                    pe.wait_ge(b_done.sem, b_done.n(r, i, j - 2))
                    unit(u0 + 2 * j, i, 4, KT, bank[2 * j][:, :], xh, xl)
                    unit(u0 + 2 * j + 1, i, 4, KT, bank[2 * j + 1][:, :], yh, yl)
            pe.wait_ge(b_done.sem, b_done.n(r, KT // 2 - 1, 1))

        def yh(k):
            return y_hi[:, T * k:T * k + T]

        def yl(k):
            return y_lo[:, T * k:T * k + T]

        def project_out(step, l):
            u0 = first_unit[step, 0]
            pe.wait_ge(y_split.sem, y_split.n(l, 0, KT - 1))
            with pe.Fori(0, 2) as i:
                for j in range(4):
                    pe.wait_ge(out_res.sem, out_res.n(l, i, j - 2))
                    unit(u0 + j, i, 4, KT, bank[4 + j % 2][:, :], yh, yl)

        ada()
        for step in STEPS:
            kind, l, p = step
            if kind == "norm":
                norm(l, p)
            elif kind == "ffn":
                ffn(step, l, p)
            elif kind == "gates":
                gates(step, l)
            elif kind == "gdn":
                gdn(step, l)
            elif kind == "mlstm":
                mlstm(step, l)
            elif kind == "attn":
                attn(step, l)
            elif kind == "merge":
                merge(step, l, p)
            elif kind == "out":
                project_out(step, l)

    @blk.scalar
    def _(act):
        def silu(dst, src):
            return nc.scalar.activation(dst, src, ACT.Silu)

        def norm(l, j):
            r = norm_run(l, j)
            for k in range(KT):
                if r > 0:
                    act.wait_ge(stream_ready.sem, stream_ready.n(r - 1, 0, k))
                nc.scalar.activation(sq[:, k, :], H[:, T * k:T * k + T], ACT.Square).then_inc(sq_done.sem, 1)
            act.wait_ge(rvar_done.sem, rvar_done.n(r, 0, 0))
            nc.scalar.activation(rms[:, :], rms[:, :], ACT.Sqrt).then_inc(rms_done.sem, 1)
            for k in range(KT):
                act.wait_ge(nmul_done.sem, nmul_done.n(r, 0, k))
                for c, (a0, a1) in enumerate(HALVES):
                    last = nc.scalar.activation(sq[:, k, a0:a1], sq[:, k, a0:a1], ACT.Identity,
                                                scale=nscale[:, l, j, k, c:c + 1],
                                                bias=mod[:, l, 3 * j * KT + k, c:c + 1])
                last.then_inc(nmod_done.sem, 1)

        def ffn(step, l, p):
            r, u0 = 2 * l + p, first_unit[step, 0]
            with act.Fori(0, FT // 2) as i:
                for j in range(2):
                    act.wait_ge(unit_done, i * 4 + (u0 + 2 * j + 1))
                    act.wait_ge(hid_ready.sem, hid_ready.n(r, i, j - 2))
                    silu(silu_g[:, j, :], bank[2 * j][:, :]).then_inc(silu_done.sem, 1)

        def gates(step, l):
            u0, s0 = first_unit[step, 0], l * S_LAYER
            A = nc.scalar.activation
            act.wait_ge(unit_done, u0 + 1)
            A(gate_a[0:64, :], bank[0][0:64, :], ACT.Identity, bias=sml[0:64, s0 + S_BA:s0 + S_BA + 1])
            A(gate_a[64:P, :], bank[0][64:P, :], ACT.Sigmoid).then_inc(gate_act.sem, 1)
            A(coef[:, :], sml[:, s0 + S_ALOG:s0 + S_ALOG + 1], ACT.Exp).then_inc(gate_act.sem, 1)
            act.wait_ge(gate_dve.sem, gate_dve.n(l, 0, 0))
            A(sofp[:, :], zed[:, :], ACT.Abs).then_inc(gate_act.sem, 1)
            act.wait_ge(gate_act.sem, gate_act.n(l, 0, 2))
            A(sofp[:, :], sofp[:, :], ACT.Exp, scale=-1.0).then_inc(gate_act.sem, 1)
            act.wait_ge(gate_act.sem, gate_act.n(l, 0, 3))
            A(sofp[:, :], sofp[:, :], ACT.Ln, bias=1.0).then_inc(gate_act.sem, 1)
            act.wait_ge(gate_dve.sem, gate_dve.n(l, 0, 2))
            A(col_b[:, :, :], col_g[:, :, 64:P], ACT.Exp).then_inc(gate_act.sem, 1)

        def gdn_head(l, h, u0):
            A = nc.scalar.activation
            for j in range(3):
                act.wait_ge(unit_done, h * 4 + (u0 + j + 1))
                act.wait_ge(conv_done.sem, conv_done.n(l, h, j - 3))
                A(padded[:, j, :, PAD:PAD + CTX], bank[j % 2][:, :].rearrange("p (s t) -> p s t", s=2),
                  ACT.Copy).then_inc(conv_filled.sem, 1)
            act.wait_ge(unit_done, h * 4 + (u0 + 4))
            act.wait_ge(head_done.sem, head_done.n(l, h, -1))
            A(g_gate[:, :], bank[1][:, :], ACT.Silu).then_inc(g_gate_done.sem, 1)
            for j in range(3):
                act.wait_ge(conv_done.sem, conv_done.n(l, h, j))
                A(qkv[:, j, :], conv[:, j, :], ACT.Silu).then_inc(conv_silu.sem, 1)
                if j < 2:
                    act.wait_ge(conv_silu.sem, conv_silu.n(l, h, j))
                    A(conv[:, j, :], qkv[:, j, :], ACT.Square).then_inc(qk_sq.sem, 1)
            for j in range(2):
                act.wait_ge(qk_var.sem, qk_var.n(l, h, j))
                A(conv[:, j, :], conv[:, j, :], ACT.Sqrt).then_inc(qk_rms.sem, 1)
            for d in range(2):
                act.wait_ge(gam_row.sem, gam_row.n(l, h, d))
                A(inv_t[:, d, :, :], bank[4 + 2 * d][:, :].rearrange("p (b t) -> p b t", b=NB),
                  ACT.Exp).then_inc(exp_gam.sem, 1)
                act.wait_ge(arg_ready.sem, arg_ready.n(l, h, d))
                A(decay[:, d, :, :], decay[:, d, :, :], ACT.Exp).then_inc(decay_done.sem, 1)
            for j, dst in enumerate((v_tok, k_tok)):
                act.wait_ge(tok_t.sem, tok_t.n(l, h, j))
                A(dst[:, :, :], bank[2 + j][:, :].rearrange("p (b t) -> p b t", b=NB),
                  ACT.Copy).then_inc(tok_ready.sem, 1)
            for d in range(2):
                act.wait_ge(inv0_turned.sem, inv0_turned.n(l, h, d))
                A(inv_t[:, d, :, :], bank[4 + 2 * d][:, :].rearrange("p (b t) -> p b t", b=NB),
                  ACT.Copy).then_inc(inv0_copied.sem, 1)
            for j in range(2 * NL):
                d = j % 2
                act.wait_ge(prod_done.sem, prod_done.n(l, h, j))
                A(prod[:, d, :, :], bank[4 + 2 * d][:, :].rearrange("p (b t) -> p b t", b=NB),
                  ACT.Copy).then_inc(prod_ready.sem, 1)
            for j in range(2 * NB):
                d = j % 2
                act.wait_ge(v_new_done.sem, v_new_done.n(l, h, j))
                A(v_new[:, d, :], bank[4 + 2 * d][:, P:2 * P], ACT.Copy).then_inc(v_new_ready.sem, 1)
            act.wait_ge(o_done.sem, o_done.n(l, h, 0))
            A(o_sum[:, :], bank[5][:, :], ACT.Copy).then_inc(o_first.sem, 1)
            act.wait_ge(o_both.sem, o_both.n(l, h, 0))
            A(conv[:, 0, :], o_sum[:, :], ACT.Square).then_inc(o_sq.sem, 1)
            act.wait_ge(o_var.sem, o_var.n(l, h, 0))
            A(conv[:, 1, :], conv[:, 1, :], ACT.Sqrt).then_inc(o_rms.sem, 1)

        def gdn(step, l):
            act.wait_ge(pad_zeroed.sem, pad_zeroed.n(l, 0, 0))
            with act.Fori(0, GH) as h:
                gdn_head(l, h, first_unit[step, 0])

        def mlstm_head(l, h, u0):
            A = nc.scalar.activation
            for j in range(8):
                act.wait_ge(unit_done, h * 8 + (u0 + j + 1))
                if j == 0:
                    act.wait_ge(m_head.sem, m_head.n(l, h, -1))
                if j < 6:
                    A(m_qkv[:, j // 2, j % 2, :], bank[j % 2][:, :], ACT.Copy,
                      scale=(MT * P) ** -0.5 if j < 2 else 1.0).then_inc(m_filled.sem, 1)
                else:
                    A(m_gate[:, j % 2, :], bank[j % 2][:, :], ACT.Sigmoid).then_inc(m_filled.sem, 1)
            for v in range(MT):
                act.wait_ge(m_vt.sem, m_vt.n(l, h, v))
                A(m_vtok[:, :, P * v:P * v + P], bank[5 + v][:, :].rearrange("p (b t) -> p b t", b=NB),
                  ACT.Copy).then_inc(m_vt_ready.sem, 1)
            for d in range(2):
                act.wait_ge(m_arg.sem, m_arg.n(l, h, d))
                A(m_floor[:, :], bank[6][:, :], ACT.Exp)
                for sb in range(NB):
                    for t0, t1, diagonal in reach(d, sb):
                        w = m_w[:, sb, t0:t1]
                        if diagonal:
                            last = A(w, w, ACT.Exp)
                        else:
                            last = A(w, bank[5][:, t0:t1], ACT.Exp, bias=m_col[:, d, sb:sb + 1])
                last.then_inc(m_exp.sem, 1)
                act.wait_ge(m_num.sem, m_num.n(l, h, d))
                A(m_den[:, :], bank[7][:, :], ACT.Abs).then_inc(m_abs.sem, 1)
            act.wait_ge(m_added.sem, m_added.n(l, h, 1))
            for v in range(MT):
                last = A(m_tmp[:, v, :], m_h[:, v, :], ACT.Square)
            last.then_inc(m_sq.sem, 1)
            act.wait_ge(m_var.sem, m_var.n(l, h, 0))
            A(m_den[:, :], m_den[:, :], ACT.Sqrt).then_inc(m_rms.sem, 1)

        def mlstm(step, l):
            with act.Fori(0, MH) as h:
                mlstm_head(l, h, first_unit[step, 0])

        def attn_group(l, g, u0):
            A = nc.scalar.activation
            for j in range(NU):
                act.wait_ge(unit_done, u0 + j + 1)
                A(t_raw[:, j, :], bank[j % 2][:, :], ACT.Copy).then_inc(t_filled.sem, 1)
            act.wait_ge(t_vt.sem, t_vt.n(l, g, 0))
            A(t_vtok[:, :, :], bank[2][:, :].rearrange("p (b t) -> p b t", b=NB),
              ACT.Copy).then_inc(t_vt_ready.sem, 1)
            for j in range(NU - 1):
                n = 0 if j == 0 else j + 1
                act.wait_ge(t_filled.sem, t_filled.n(l, g, n))
                if j > 0:
                    act.wait_ge(t_roped.sem, t_roped.n(l, g, j - 1))
                A(t_sq[:, 0, :], t_raw[:, n, :], ACT.Square).then_inc(t_sqd.sem, 1)
                act.wait_ge(t_var.sem, t_var.n(l, g, j))
                A(t_sq[:, 1, :], t_sq[:, 1, :], ACT.Sqrt).then_inc(t_rms.sem, 1)
            for n in range(NQ):
                b, q = divmod(n, AG)
                keys, c = (CTX if b < 2 else T), t_col[:, n % 2, :]
                act.wait_ge(t_masked.sem, t_masked.n(l, g, n))
                A(c[:, 2:3], sml[:, l * S_LAYER + S_SINK + AG * g + q:l * S_LAYER + S_SINK + AG * g + q + 1],
                  ACT.Exp, bias=c[:, 1:2])
                src = bank[5 + n % 2][:, 0:keys] if b < 2 else t_s[:, n % 2, :]
                A(t_s[:, n % 2, 0:keys], src, ACT.Exp, bias=c[:, 1:2], accum_out=c[:, 3:4]).then_inc(t_exp.sem, 1)
                act.wait_ge(t_pturn.sem, t_pturn.n(l, g, n))
                if b > 0:
                    act.wait_ge(t_out.sem, t_out.n(l, g, b - 1))
                kb = keys // P
                A(t_pt[:, 0:kb, q, :], bank[2 + n % 2][:, 0:keys].rearrange("p (k t) -> p k t", k=kb),
                  ACT.Copy).then_inc(t_pcopied.sem, 1)
                if q == AG - 1:
                    act.wait_ge(t_out.sem, t_out.n(l, g, b))
                    if b > 0 or g > 0:
                        act.wait_ge(t_osplit.sem, t_osplit.n(l, g, b - 1))
                    A(t_o[:, :, :], bank[7][:, :].rearrange("p (q t) -> p q t", q=AG),
                      ACT.Copy).then_inc(t_ocopy.sem, 1)

        def attn(step, l):
            for g in range(AKV):
                attn_group(l, g, first_unit[step, g])

        def merge(step, l, p):
            u0, r = first_unit[step, 0], merge_run[step]
            with act.Fori(0, KT // 2) as i:
                for j in range(2):
                    act.wait_ge(unit_done, i * 4 + (u0 + 2 * j + 1))
                    act.wait_ge(b_done.sem, b_done.n(r, i, j - 2))
                    nc.scalar.activation(b_gate[:, j, :], bank[2 * j][:, :], ACT.Sigmoid).then_inc(b_sig.sem, 1)

        for e in (m_filled, m_vt_ready, t_filled, conv_filled):
            act.sem_inc(e.sem, e.credit)
        act.sem_inc(g_gate_done.sem, g_gate_done.credit)
        act.wait_ge(dma_small, 64)
        silu(cond[:, :, :], sml[:, S_COND:S_COND + 16].rearrange("p (k c) -> p k c", c=2)).then_inc(cond_done.sem, 1)
        act.wait_ge(mod_done.sem, 1)
        for step in STEPS:
            kind, l, p = step
            if kind == "norm":
                norm(l, p)
            elif kind == "ffn":
                ffn(step, l, p)
            elif kind == "gates":
                gates(step, l)
            elif kind == "gdn":
                gdn(step, l)
            elif kind == "mlstm":
                mlstm(step, l)
            elif kind == "attn":
                attn(step, l)
            elif kind == "merge":
                merge(step, l, p)

    @blk.vector
    def _(dve):
        step_of = Chain(dve, dve_step)
        V = nc.vector

        def modulation():
            dve.wait_ge(dma_small, 64)
            step_of(V.tensor_copy(lev[:, :], lev_f[:, :]))
            for l in range(DEPTH):
                dve.wait_ge(ada_done.sem, ada_done.n(0, 0, (l + 1) * NMOD * 2 - 1))
                b = sml[:, l * S_LAYER + S_BADA:l * S_LAYER + S_BADA + NMOD * KT].unsqueeze(2)
                step_of(V.tensor_tensor(mod[:, l, :, :], bank[l][:, 0:2 * NMOD * KT].rearrange(
                    "p (n c) -> p n c", c=2), b.to_broadcast([P, NMOD * KT, 2]), ALU.add))
                for j in range(3):
                    w = sml[:, l * S_LAYER + S_NORM + KT * j:l * S_LAYER + S_NORM + KT * (j + 1)].unsqueeze(2)
                    step_of(V.scalar_tensor_tensor(
                        out=nscale[:, l, j, :, :], in0=mod[:, l, (3 * j + 1) * KT:(3 * j + 2) * KT, :], scalar=1.0,
                        in1=w.to_broadcast([P, KT, 2]), op0=ALU.add, op1=ALU.mult))
                    step_of(V.tensor_scalar(rgate[:, l, j, :, :], mod[:, l, (3 * j + 2) * KT:(3 * j + 3) * KT, :],
                                            1.0 if j == 1 else 0.5, None, ALU.mult))
            V.memset(rms[:, :], 0.0).then_inc(mod_done.sem, 1)
            dve.wait_ge(mod_done.sem, 1)

        def norm(l, j):
            r = norm_run(l, j)
            dve.wait_ge(ss_done.sem, ss_done.n(r, 0, 0))
            step_of(V.tensor_scalar(rms[:, :], bank[7][:, :], 1.0 / D, EPS, ALU.mult, ALU.add))
            V.reciprocal(rms[:, :], rms[:, :]).then_inc(rvar_done.sem, 1)
            dve.wait_ge(rms_done.sem, rms_done.n(r, 0, 0))
            for k in range(KT):
                V.tensor_tensor(sq[:, k, :], H[:, T * k:T * k + T], rms[:, :], ALU.mult).then_inc(nmul_done.sem, 1)
            for k in range(KT):
                dve.wait_ge(nmod_done.sem, nmod_done.n(r, 0, k))
                step_of(V.tensor_copy(xn_hi[:, k, :], sq[:, k, :]))
                V.tensor_tensor(xn_lo[:, k, :], sq[:, k, :], xn_hi[:, k, :].bitcast(F32),
                                ALU.subtract).then_inc(xn_ready.sem, 1)

        def residual(n, i, l, j, src):
            at_n = (i * 4 + n) * T
            for c, (a0, a1) in enumerate(HALVES):
                h = H[:, bass.ds(at_n + a0, a1 - a0)] if not isinstance(i, int) else H[:, at_n + a0:at_n + a1]
                last = V.scalar_tensor_tensor(out=h, in0=src[:, a0:a1], scalar=rgate[:, l, j, i * 4 + n, c:c + 1],
                                              in1=h, op0=ALU.mult, op1=ALU.add)
            return last

        def ffn(step, l, p):
            r, u0 = 2 * l + p, first_unit[step, 0]
            with step_of.turns(0, FT // 2, 4) as i:
                for j in range(2):
                    dve.wait_ge(silu_done.sem, silu_done.n(r, i, j))
                    dve.wait_ge(unit_done, i * 4 + (u0 + 2 * j + 2))
                    step_of(V.tensor_tensor(hid[:, j, :], silu_g[:, j, :], bank[2 * j + 1][:, :], ALU.mult))
                    hi = hid_hi[:, bass.ds((i * 2 + j) * T, T)]
                    lo = hid_lo[:, bass.ds((i * 2 + j) * T, T)]
                    step_of(V.tensor_copy(hi, hid[:, j, :]))
                    V.tensor_tensor(lo, hid[:, j, :], hi.bitcast(F32), ALU.subtract).then_inc(hid_ready.sem, 1)
            u0 = first_unit[step, 1]
            dve.wait_ge(hid_ready.sem, hid_ready.n(r, FT // 2 - 1, 1))
            for i in range(2):
                for n in range(4):
                    dve.wait_ge(unit_done, i * 12 + (u0 + 3 * n + 3))
                    residual(n, i, l, 2 * p, bank[4 + n % 2]).then_inc(res_done.sem, 1)
            signal_stream(l, p)

        def signal_stream(l, p):
            dve.wait_ge(res_done.sem, res_done.n(2 * l + p, 1, 3))
            for k in range(KT):
                dve.sem_inc(stream_ready.sem, 1)

        def gates(step, l):
            u0, s0 = first_unit[step, 0], l * S_LAYER

            def col(c, a0=0, a1=P):
                return sml[a0:a1, s0 + c:s0 + c + 1]

            def scan(dst, src, rows, reverse, length, reset, op0, op1, data0):
                prev = None
                for n, t0 in enumerate(range(0, T, length)):
                    if t0 % reset == 0:
                        prev = 0.0
                    cut = slice(t0, t0 + length)
                    views = [x[rows, cut][:, ::-1] if reverse else x[rows, cut] for x in (dst, data0, src)]
                    step_of(V.tensor_tensor_scan(views[0], views[1], views[2], prev, op0, op1))
                    e = t0 if reverse else t0 + length - 1
                    prev = dst[rows, e:e + 1]

            step_of(V.memset(unit_row[:, :], 1.0))
            dve.wait_ge(unit_done, u0 + 2)
            V.tensor_scalar(zed[:, :], bank[1][:, :], col(S_BB), col(S_SGN), ALU.add,
                            ALU.mult).then_inc(gate_dve.sem, 1)
            dve.wait_ge(gate_act.sem, gate_act.n(l, 0, 4))
            step_of(V.scalar_tensor_tensor(out=zed[:, :], in0=zed[:, :], scalar=0.0, in1=sofp[:, :],
                                           op0=ALU.max, op1=ALU.add))
            step_of(V.tensor_scalar(zed[:, :], zed[:, :], coef[:, 0:1], -1.0, ALU.mult, ALU.mult))
            for d in range(2):
                scan(cum, zed, slice(32 * d, 32 * d + 32), d == 1, CTX, T, ALU.mult, ALU.add, unit_row)
                scan(cum, zed, slice(64 + 32 * d, 96 + 32 * d), d == 1, P, P, ALU.mult, ALU.add, unit_row)
            step_of(V.tensor_tensor(gate_a[0:64, :], gate_a[0:64, :], cum[0:64, :], ALU.subtract))
            for d in range(2):
                scan(run_max, gate_a, slice(32 * d, 32 * d + 32), d == 1, CTX, T, ALU.max, ALU.max, gate_a)
            step_of(V.tensor_scalar(rows_m[0:64, :], run_max[0:64, :], -1.0, None, ALU.mult))
            step_of(V.tensor_copy(rows_m[64:P, :], cum[64:P, :]))
            V.scalar_tensor_tensor(out=rows_n[0:64, :], in0=cum[0:64, :], scalar=-1.0, in1=run_max[0:64, :],
                                   op0=ALU.mult, op1=ALU.subtract).then_inc(gate_dve.sem, 1)
            for j, dst in enumerate((col_a, col_g)):
                dve.wait_ge(gate_pe.sem, gate_pe.n(l, 0, j))
                c = V.tensor_copy(dst[:, :, :], bank[2 + j][:, :].rearrange("p (b t) -> p b t", b=NB))
                if j == 0:
                    step_of(c)
            c.then_inc(gate_dve.sem, 1)
            dve.wait_ge(gate_act.sem, gate_act.n(l, 0, 5))
            step_of(V.scalar_tensor_tensor(out=col_b[:, :, :], in0=col_b[:, :, :], scalar=-1.0,
                                           in1=col_a[:, :, 64:P], op0=ALU.mult, op1=ALU.mult))

        def gdn_head(l, h, u0):
            s0 = l * S_LAYER
            q_t, k_t = qkv[:, 0, :], qkv[:, 1, :]

            def b4(x):
                return x.rearrange("p (b t) -> p b t", b=NB)

            def spread(x):
                return x.unsqueeze(2).to_broadcast([P, NB, P])

            for d in range(2):
                row = h + GD_ROW[d]
                for j, src in enumerate((col_g[:, :, bass.ds(row, 1)], col_a[:, :, bass.ds(row, 1)],
                                         col_b[:, :, bass.ds(row - 64, 1)])):
                    step_of(V.tensor_copy(lane_col[:, d, j, :].unsqueeze(2), src))
                V.tensor_copy(pick[:, d, :], con[:, bass.ds(row + C_ID, 1)].to_broadcast([P, P])).then_inc(
                    pick_ready.sem, 1)
            for j in range(3):
                dve.wait_ge(conv_filled.sem, conv_filled.n(l, h, j))
                acc = conv[:, j, :].rearrange("p (s t) -> p s t", s=2)
                for k in range(CONV_K):
                    tap = conv_w[:, j * CONV_K + k:j * CONV_K + k + 1]
                    src = padded[:, j, :, k:k + CTX]
                    if k == 0:
                        ins = V.tensor_scalar(acc, src, tap, None, ALU.mult)
                    else:
                        ins = V.scalar_tensor_tensor(out=acc, in0=src, scalar=tap, in1=acc, op0=ALU.mult,
                                                     op1=ALU.add)
                    if k < CONV_K - 1:
                        step_of(ins)
                ins.then_inc(conv_done.sem, 1)
            for j in range(2):
                dve.wait_ge(qk_ss.sem, qk_ss.n(l, h, j))
                step_of(V.tensor_scalar(conv[:, j, :], bank[2 + j][:, :], EPS, None, ALU.add))
                V.reciprocal(conv[:, j, :], conv[:, j, :]).then_inc(qk_var.sem, 1)
            for j in range(2):
                dve.wait_ge(qk_rms.sem, qk_rms.n(l, h, j))
                V.scalar_tensor_tensor(out=qkv[:, j, :], in0=qkv[:, j, :], scalar=P ** -0.5 if j == 0 else 1.0,
                                       in1=conv[:, j, :], op0=ALU.mult, op1=ALU.mult).then_inc(qk_ready.sem, 1)
            for d in range(2):
                dve.wait_ge(exp_gam.sem, exp_gam.n(l, h, d))
                for b in range(NB):
                    last = V.scalar_tensor_tensor(
                        out=decay[:, d, b, :], in0=bank[4 + 2 * d][:, P * b:P * b + P],
                        scalar=lane_col[:, d, 0, b:b + 1], in1=con[:, C_MIN + P * d:C_MIN + P * d + P],
                        op0=ALU.subtract, op1=ALU.min)
                last.then_inc(arg_ready.sem, 1)
            for d in range(2):
                e = chunk_end(d)
                dve.wait_ge(kk_done.sem, kk_done.n(l, h, 0))
                dve.wait_ge(decay_done.sem, decay_done.n(l, h, d))
                V.tensor_tensor(prod[:, d, :, :], b4(bank[2][:, :]), decay[:, d, :, :], ALU.mult).then_inc(
                    l_ready.sem, 1)
                dve.wait_ge(kk_done.sem, kk_done.n(l, h, 1))
                step_of(V.tensor_tensor(p_t[:, d, :, :], b4(bank[3][:, :]), decay[:, d, :, :], ALU.mult))
                step_of(V.tensor_copy(end_col[:, d, 0, :].unsqueeze(2), decay[:, d, :, e:e + 1]))
                dve.wait_ge(exp_gam.sem, exp_gam.n(l, h, d))
                step_of(V.tensor_copy(end_col[:, d, 1, :].unsqueeze(2), inv_t[:, d, :, e:e + 1]))
                step_of(V.tensor_tensor(q_dec[:, d, :, :], b4(q_t), inv_t[:, d, :, :], ALU.mult))
            for d in range(2):
                dve.wait_ge(l_turned.sem, l_turned.n(l, h, d))
                V.tensor_tensor(a_mat[:, d, :, :], b4(bank[5 + 2 * d][:, :]), spread(lane_col[:, d, 1, :]),
                                ALU.mult).then_inc(a_ready.sem, 1)
                dve.wait_ge(a_ready.sem, a_ready.n(l, h, d))
                m = lev[:, d * len(LEVELS) * P:(d * len(LEVELS) + 1) * P].unsqueeze(1).to_broadcast([P, NB, P])
                step_of(V.tensor_tensor(inv[:, d, :, :], a_mat[:, d, :, :], m, ALU.mult))
                V.tensor_tensor(inv[:, d, :, :], ident.unsqueeze(1).to_broadcast([P, NB, P]), inv[:, d, :, :],
                                ALU.subtract).then_inc(inv0_ready.sem, 1)
            for d in range(2):
                dve.wait_ge(tok_ready.sem, tok_ready.n(l, h, 1))
                step_of(V.tensor_tensor(k_end[:, d, :, :], k_tok[:, :, :], spread(end_col[:, d, 0, :]), ALU.mult))
                V.tensor_tensor(v_beta[:, d, :, :], v_tok[:, :, :], spread(lane_col[:, d, 1, :]),
                                ALU.mult).then_inc(lane_ready.sem, 1)
            for j in range(2 * NL):
                v, d = divmod(j, 2)
                dve.wait_ge(corr_done.sem, corr_done.n(l, h, j))
                if j < 2:
                    dve.wait_ge(inv0_copied.sem, inv0_copied.n(l, h, d))
                if v < NL - 1:
                    V.tensor_tensor(inv[:, d, :, :], inv[:, d, :, :], b4(bank[4 + 2 * d][:, :]), ALU.subtract)
                V.tensor_tensor(inv_t[:, d, :, :], inv_t[:, d, :, :], b4(bank[5 + 2 * d][:, :]),
                                ALU.subtract).then_inc(inv_ready.sem, 1)
            for i in range(NB):
                for d in range(2):
                    b = scan_order(d)[i]
                    if i == 0:
                        dve.wait_ge(lane_ready.sem, lane_ready.n(l, h, d))
                        V.tensor_copy(resid[:, d, :], v_beta[:, d, b, :]).then_inc(resid_ready.sem, 1)
                    else:
                        dve.wait_ge(ks_done.sem, ks_done.n(l, h, 2 * (i - 1) + d))
                        V.scalar_tensor_tensor(
                            out=resid[:, d, :], in0=bank[4 + 2 * d][:, 0:P], scalar=lane_col[:, d, 2, b:b + 1],
                            in1=v_beta[:, d, b, :], op0=ALU.mult, op1=ALU.add).then_inc(resid_ready.sem, 1)
                if i < NB - 1:
                    for d in range(2):
                        b = scan_order(d)[i]
                        dve.wait_ge(ds_done.sem, ds_done.n(l, h, 2 * i + d))
                        if i == 0:
                            V.tensor_copy(state[:, d, :], bank[4 + 2 * d][:, 2 * P:3 * P]).then_inc(
                                state_ready.sem, 1)
                        else:
                            V.scalar_tensor_tensor(
                                out=state[:, d, :], in0=state[:, d, :], scalar=end_col[:, d, 1, b:b + 1],
                                in1=bank[4 + 2 * d][:, 2 * P:3 * P], op0=ALU.mult,
                                op1=ALU.add).then_inc(state_ready.sem, 1)
            dve.wait_ge(o_done.sem, o_done.n(l, h, 1))
            dve.wait_ge(o_first.sem, o_first.n(l, h, 0))
            V.tensor_tensor(o_sum[:, :], o_sum[:, :], bank[7][:, :], ALU.add).then_inc(o_both.sem, 1)
            dve.wait_ge(o_ss.sem, o_ss.n(l, h, 0))
            step_of(V.tensor_scalar(conv[:, 1, :], bank[2][:, :], 1.0 / P, EPS, ALU.mult, ALU.add))
            V.reciprocal(conv[:, 1, :], conv[:, 1, :]).then_inc(o_var.sem, 1)
            dve.wait_ge(o_rms.sem, o_rms.n(l, h, 0))
            step_of(V.tensor_tensor(o_sum[:, :], o_sum[:, :], conv[:, 1, :], ALU.mult))
            step_of(V.scalar_tensor_tensor(out=o_sum[:, :], in0=o_sum[:, :],
                                           scalar=sml[:, s0 + S_GDN:s0 + S_GDN + 1], in1=g_gate[:, :],
                                           op0=ALU.mult, op1=ALU.mult))
            hi, lo = y_hi[:, bass.ds(h * T, T)], y_lo[:, bass.ds(h * T, T)]
            step_of(V.tensor_copy(hi, o_sum[:, :]))
            V.tensor_tensor(lo, o_sum[:, :], hi.bitcast(F32), ALU.subtract).then_inc(head_done.sem, 1)

        def gdn(step, l):
            V.memset(padded[:, :, :, :].rearrange("p a b c -> p (a b c)"), 0.0).then_inc(pad_zeroed.sem, 1)
            dve.wait_ge(pad_zeroed.sem, pad_zeroed.n(l, 0, 0))
            with step_of.turns(0, GH, GDN_STEPS) as h:
                w0 = l * S_LAYER + S_CONV
                step_of(V.tensor_copy(conv_w[:, :], sml[:, bass.ds(h * (3 * CONV_K) + w0, 3 * CONV_K)]))
                gdn_head(l, h, first_unit[step, 0])

        def mlstm_head(l, h, u0):
            for d in range(2):
                row = h + ML_ROW[d]
                step_of(V.tensor_copy(m_col[:, d, :].unsqueeze(2), col_a[:, :, bass.ds(row, 1)]))
                V.tensor_copy(m_pick[:, d, :], con[:, bass.ds(row + C_ID, 1)].to_broadcast([P, P])).then_inc(
                    m_picked.sem, 1)
            for d in range(2):
                dve.wait_ge(m_rows.sem, m_rows.n(l, h, d))
                for sb in range(NB):
                    cut = slice(P * sb, P * sb + P)
                    last = V.scalar_tensor_tensor(
                        out=m_w[:, sb, cut], in0=bank[5][:, cut], scalar=m_col[:, d, sb:sb + 1],
                        in1=con[:, C_MIN + P * d:C_MIN + P * d + P], op0=ALU.add, op1=ALU.min)
                last.then_inc(m_arg.sem, 1)
                dve.wait_ge(m_exp.sem, m_exp.n(l, h, d))
                dve.wait_ge(m_kq.sem, m_kq.n(l, h, 2))
                for sb in range(NB):
                    src, c0, f = kq_view(sb)
                    for t0, t1 in joined(d, sb):
                        w = m_w[:, sb, t0:t1]
                        last = V.tensor_tensor(w, src[:, c0 + t0 - f:c0 + t1 - f], w, ALU.mult)
                last.then_inc(m_weighted.sem, 1)
                dve.wait_ge(m_abs.sem, m_abs.n(l, h, d))
                step_of(V.tensor_tensor(m_den[:, :], m_den[:, :], m_floor[:, :], ALU.max))
                step_of(V.reciprocal(m_den[:, :], m_den[:, :]))
                if d == 0:
                    for v in range(MT):
                        last = V.tensor_tensor(m_h[:, v, :], bank[v][:, :], m_den[:, :], ALU.mult)
                else:
                    for v in range(MT):
                        step_of(V.tensor_tensor(m_tmp[:, v, :], bank[v][:, :], m_den[:, :], ALU.mult))
                        last = V.tensor_tensor(m_h[:, v, :], m_h[:, v, :], m_tmp[:, v, :], ALU.add)
                last.then_inc(m_added.sem, 1)
            dve.wait_ge(m_ss.sem, m_ss.n(l, h, 0))
            step_of(V.tensor_scalar(m_den[:, :], bank[5][:, :], 1.0 / (MT * P), EPS, ALU.mult, ALU.add))
            V.reciprocal(m_den[:, :], m_den[:, :]).then_inc(m_var.sem, 1)
            dve.wait_ge(m_rms.sem, m_rms.n(l, h, 0))
            step_of(V.tensor_copy(m_wn[:, :], sml[:, bass.ds(h * MT + l * S_LAYER + S_MLN, MT)]))
            for v in range(MT):
                step_of(V.tensor_tensor(m_h[:, v, :], m_h[:, v, :], m_den[:, :], ALU.mult))
                step_of(V.scalar_tensor_tensor(out=m_h[:, v, :], in0=m_h[:, v, :], scalar=m_wn[:, v:v + 1],
                                               in1=m_gate[:, v, :], op0=ALU.mult, op1=ALU.mult))
                hi, lo = (y[:, bass.ds((h * MT + v) * T, T)] for y in (y_hi, y_lo))
                step_of(V.tensor_copy(hi, m_h[:, v, :]))
                last = V.tensor_tensor(lo, m_h[:, v, :], hi.bitcast(F32), ALU.subtract)
            last.then_inc(m_head.sem, 1)

        def mlstm(step, l):
            with step_of.turns(0, MH, MLSTM_STEPS) as h:
                mlstm_head(l, h, first_unit[step, 0])

        def attn_group(l, g, u0):
            s0 = l * S_LAYER
            step_of(V.tensor_scalar(t_w[:, 0:1], sml[:, s0 + S_QKN:s0 + S_QKN + 1], P ** -0.5, None, ALU.mult))
            step_of(V.tensor_copy(t_w[:, 1:2], sml[:, s0 + S_QKN + 1:s0 + S_QKN + 2]))
            for j in range(NU - 1):
                n = 0 if j == 0 else j + 1
                x, lat = t_raw[:, n, :], t_raw[:, n, CTX:T]
                dve.wait_ge(t_ss.sem, t_ss.n(l, g, j))
                step_of(V.tensor_scalar(t_sq[:, 1, :], bank[3][:, :], 1.0 / P, EPS, ALU.mult, ALU.add))
                V.reciprocal(t_sq[:, 1, :], t_sq[:, 1, :]).then_inc(t_var.sem, 1)
                dve.wait_ge(t_rms.sem, t_rms.n(l, g, j))
                V.scalar_tensor_tensor(out=x, in0=x, scalar=t_w[:, 1:2] if j == 0 else t_w[:, 0:1],
                                       in1=t_sq[:, 1, :], op0=ALU.mult, op1=ALU.mult).then_inc(t_normed.sem, 1)
                dve.wait_ge(t_turned.sem, t_turned.n(l, g, j))
                step_of(V.tensor_tensor(t_rot[:, :], bank[4][:, 0:SEQ], con[:, C_SIN:C_SIN + SEQ], ALU.mult))
                step_of(V.tensor_tensor(lat, lat, con[:, C_COS:C_COS + SEQ], ALU.mult))
                V.tensor_tensor(lat, lat, t_rot[:, :], ALU.add).then_inc(t_roped.sem, 1)
            for n in range(NQ):
                b, q = divmod(n, AG)
                keys, c = (CTX if b < 2 else T), t_col[:, n % 2, :]
                s = t_s[:, n % 2, 0:keys]
                dve.wait_ge(t_scored.sem, t_scored.n(l, g, n))
                if n >= 2:
                    dve.wait_ge(t_pturn.sem, t_pturn.n(l, g, n - 2))
                if b < 2:
                    step_of(V.tensor_reduce(c[:, 0:1], bank[5 + n % 2][:, 0:keys], AX.X, ALU.max))
                else:
                    step_of(V.tensor_copy(s[:, 0:CTX], bank[5 + n % 2][:, 0:CTX]))
                    step_of(V.tensor_tensor(s[:, CTX:T], bank[5 + n % 2][:, CTX:T],
                                            con[:, C_WIN + (b - 2) * SEQ:C_WIN + (b - 1) * SEQ], ALU.add))
                    step_of(V.tensor_reduce(c[:, 0:1], s, AX.X, ALU.max))
                k = s0 + S_SINK + AG * g + q
                V.tensor_scalar(c[:, 1:2], c[:, 0:1], sml[:, k:k + 1], -1.0, ALU.max, ALU.mult).then_inc(
                    t_masked.sem, 1)
                dve.wait_ge(t_exp.sem, t_exp.n(l, g, n))
                step_of(V.tensor_tensor(c[:, 4:5], c[:, 2:3], c[:, 3:4], ALU.add))
                step_of(V.reciprocal(c[:, 5:6], c[:, 4:5]))
                V.tensor_scalar(s, s, c[:, 5:6], None, ALU.mult).then_inc(t_prob.sem, 1)
                if q == AG - 1:
                    dve.wait_ge(t_ocopy.sem, t_ocopy.n(l, g, b))
                    hi, lo = (y[:, :].rearrange("p (h t) -> p h t", h=KT)[:, AG * g:AG * g + AG, P * b:P * b + P]
                              for y in (y_hi, y_lo))
                    step_of(V.tensor_copy(hi, t_o[:, :, :]))
                    V.tensor_tensor(lo, t_o[:, :, :], hi.bitcast(F32), ALU.subtract).then_inc(t_osplit.sem, 1)

        def attn(step, l):
            for g in range(AKV):
                attn_group(l, g, first_unit[step, g])

        def merge(step, l, p):
            u0, r = first_unit[step, 0], merge_run[step]
            opens = not any(s[0] == "merge" for s in STEPS[STEPS.index(step) - 2:STEPS.index(step)]) and                 ("gates", l, 0) in STEPS[STEPS.index(step) - 3:STEPS.index(step)]
            with step_of.turns(0, KT // 2, 0 if opens else 2) as i:
                for j in range(2):
                    dve.wait_ge(b_sig.sem, b_sig.n(r, i, j))
                    dve.wait_ge(unit_done, i * 4 + (u0 + 2 * j + 2))
                    y = y_sum[:, bass.ds((i * 2 + j) * T, T)]
                    if opens:
                        V.tensor_tensor(y, b_gate[:, j, :], bank[2 * j + 1][:, :], ALU.mult).then_inc(
                            b_done.sem, 1)
                    else:
                        step_of(V.tensor_tensor(b_tmp[:, j, :], b_gate[:, j, :], bank[2 * j + 1][:, :], ALU.mult))
                        V.tensor_tensor(y, y, b_tmp[:, j, :], ALU.add).then_inc(b_done.sem, 1)

        def project_out(step, l):
            u0 = first_unit[step, 0]
            dve.wait_ge(b_done.sem, b_done.n(max(r for s, r in merge_run.items() if s[1] == l), KT // 2 - 1, 1))
            for k in range(KT):
                cut = slice(T * k, T * k + T)
                step_of(V.tensor_copy(y_hi[:, cut], y_sum[:, cut]))
                V.tensor_tensor(y_lo[:, cut], y_sum[:, cut], y_hi[:, cut].bitcast(F32),
                                ALU.subtract).then_inc(y_split.sem, 1)
            for i in range(2):
                for n in range(4):
                    dve.wait_ge(unit_done, i * 4 + (u0 + n + 1))
                    residual(n, i, l, 1, bank[4 + n % 2]).then_inc(out_res.sem, 1)
            dve.wait_ge(out_res.sem, out_res.n(l, 1, 3))
            for k in range(KT):
                dve.sem_inc(stream_ready.sem, 1)

        modulation()
        for step in STEPS:
            kind, l, p = step
            if kind == "norm":
                norm(l, p)
            elif kind == "ffn":
                ffn(step, l, p)
            elif kind == "gates":
                gates(step, l)
            elif kind == "gdn":
                gdn(step, l)
            elif kind == "mlstm":
                mlstm(step, l)
            elif kind == "attn":
                attn(step, l)
            elif kind == "merge":
                merge(step, l, p)
            elif kind == "out":
                project_out(step, l)

    block.__exit__(None, None, None)


def _layout(**inputs):
    a = {k: np.asarray(v) for k, v in inputs.items()}
    f = np.float32
    arrays = {"tokens": np.ascontiguousarray(np.concatenate([a["ctx"][0], a["x"][0]], 0).T)}

    def tiles(v, n):
        return v.reshape(n, P).T

    small = np.zeros((P, S_ALL), f)
    for l in range(DEPTH):
        s = small[:, l * S_LAYER:(l + 1) * S_LAYER]
        s[:, S_BADA:S_BADA + NMOD * KT] = tiles(a["b_ada"][l], NMOD * KT)
        s[:, S_NORM:S_NORM + 3 * KT] = tiles(a["norm_w"][l].reshape(-1), 3 * KT)
        s[:, S_CONV:S_CONV + 3 * GH * CONV_K] = a["gdn_conv_w"][l].reshape(3, CONV_K, GH, P).transpose(
            3, 2, 0, 1).reshape(P, -1)
        s[:, S_QKN:S_QKN + 2] = a["attn_qk_norm"][l].T
        s[:, S_SINK:S_SINK + AH] = a["attn_sink"][l][None, :]
        s[:, S_MLN:S_MLN + MH * MT] = tiles(a["ml_norm_w"][l].reshape(-1), MH * MT)
        s[:, S_GDN] = a["gdn_norm_w"][l]
        s[:, S_SGN] = 1.0
        for d in range(2):
            s[ML_ROW[d]:ML_ROW[d] + MH, S_BA] = a["ml_i_bias"][l, d]
            s[ML_ROW[d]:ML_ROW[d] + MH, S_BB] = a["ml_f_bias"][l, d]
            s[ML_ROW[d]:ML_ROW[d] + MH, S_SGN] = -1.0
            s[GD_ROW[d]:GD_ROW[d] + GH, S_BB] = a["gdn_dt_bias"][l, d]
            s[GD_ROW[d]:GD_ROW[d] + GH, S_ALOG] = a["gdn_a_log"][l, d]
    for n, v in enumerate((a["c_ctx"], a["c"][0])):
        small[:, S_COND + n:S_COND + 16:2] = tiles(v, KT)
    arrays["smalls"] = small

    wg = np.zeros((DEPTH, D, 2 * P), f)
    for d in range(2):
        for t, part in enumerate((7, 8)):
            c = OFF[part] + d * MH
            wg[:, :, t * P + ML_ROW[d]:t * P + ML_ROW[d] + MH] = a["w_in"][:, :, c:c + MH]
        for t, part in enumerate((13, 14)):
            c = OFF[part] + d * GH
            wg[:, :, t * P + GD_ROW[d]:t * P + GD_ROW[d] + GH] = a["w_in"][:, :, c:c + GH]
    arrays["w_gates"] = wg
    for k, n in (("w_ada", "w_ada"), ("w_gate", "ffn_w_gate"), ("w_up", "ffn_w_up"), ("w_down", "ffn_w_down"),
                 ("w_in", "w_in"), ("w_branch", "w_branch"), ("w_out", "w_out")):
        arrays[k] = np.ascontiguousarray(a[n])

    con = np.zeros((P, C_ALL), f)
    con[:, C_ID:C_ID + P] = np.eye(P)
    con[:, C_ONE:C_ONE + P] = 1.0
    half, quarter = P // 2, P // 4
    for i in range(P):
        j = i % half
        if j < quarter:
            con[i + quarter, C_ROT + i] = -1.0
        else:
            con[i - quarter, C_ROT + i] = 1.0
    inv = (f(10000.0) ** (-np.arange(quarter, dtype=f) / f(quarter))).astype(f)
    tok = np.arange(SEQ)
    for i in range(P):
        pos = (tok // 64 if i < half else tok % 64).astype(f)
        ang = pos * inv[i % quarter]
        con[i, C_COS:C_COS + SEQ] = np.cos(ang)
        con[i, C_SIN:C_SIN + SEQ] = np.sin(ang)
    for b in range(2):
        q = b * P + np.arange(P)[:, None]
        con[:, C_WIN + b * SEQ:C_WIN + (b + 1) * SEQ] = np.where(np.abs(np.arange(SEQ)[None] - q) <= 128, 0.0, -FAR)
    s, t = np.arange(P)[:, None], np.arange(P)[None]
    con[:, C_MIN:C_MIN + P] = np.where(s <= t, 0.0, -FAR)
    con[:, C_MIN + P:C_MIN + 2 * P] = np.where(s >= t, 0.0, -FAR)
    arrays["consts"] = con
    lev = np.zeros((P, 2, len(LEVELS), P), f)
    for n, b in enumerate(LEVELS):
        m = (s // (2 * b) == t // (2 * b)) & ((s // b) % 2 == 1) & ((t // b) % 2 == 0)
        lev[:, 0, n], lev[:, 1, n] = m, m.T
    arrays["levels"] = lev.reshape(P, M_ALL)
    return arrays


_NAMES = ("tokens", "smalls", "consts", "levels", "w_ada", "w_gates", "w_gate", "w_up", "w_down", "w_in",
          "w_branch", "w_out")


def kernel(**inputs):
    import concourse.bacc as _bacc
    from concourse.bass_utils import run_bass_kernel_spmd as _run

    nc = _bacc.Bacc("TRN2", target_bir_lowering=False, num_devices=1)
    arrays = _layout(**inputs)
    args = [nc.dram_tensor(n, arrays[n].shape, mybir.dt.from_np(arrays[n].dtype), kind="ExternalInput").ap()
            for n in _NAMES]
    out = nc.dram_tensor("out", (D, SEQ), F32, kind="ExternalOutput").ap()
    trunk_kernel(nc, *args, out)
    r = _run(nc, [arrays], core_ids=[0])
    return np.ascontiguousarray(r.results[0]["out"].T)[None]
```

```python
from contextlib import contextmanager

import numpy as np
import concourse.bass as bass
from concourse import mybir

F32 = mybir.dt.float32
F32R = mybir.dt.float32r
BF16 = mybir.dt.bfloat16
ALU = mybir.AluOpType
ACT = mybir.ActivationFunctionType
AX = mybir.AxisListType

P = 128
DEPTH, D, DFF, NMOD = 2, 1024, 2816, 9
KT = D // P
FT = DFF // P
CTX, SEQ = 256, 256
T = CTX + SEQ
NB = T // P
HALVES = ((0, CTX), (CTX, T))
EPS = 1e-6
FAR = 1e30
AH, AKV, AG = 8, 2, 4
MH, MT = 4, 2
GH = 8
CONV_K = 5
SPLITS = (1024, 256, 256, 1024, 1024, 1024, 1024, 8, 8, 1024, 1024, 1024, 1024, 16, 16, 3072)
OFF = [sum(SPLITS[:i]) for i in range(len(SPLITS) + 1)]

ML_ROW = (0, 32)
GD_ROW = (64, 96)

S_BADA, S_NORM, S_CONV, S_QKN, S_SINK = 0, 72, 96, 216, 218
S_MLN, S_GDN, S_BA, S_BB, S_SGN, S_ALOG = 226, 234, 235, 236, 237, 238
S_LAYER = 240
S_COND = DEPTH * S_LAYER
S_ALL = S_COND + 16
C_ID, C_ONE, C_ROT, C_COS, C_SIN, C_WIN, C_MIN, C_LEV = 0, 128, 256, 384, 640, 896, 1408, 1664
DOWN_CUTS = ((0, 8), (8, 7), (15, 7))
LEVELS = (1, 2, 4, 8, 16, 32, 64)
C_ALL = C_LEV
NWIDE = 4
ADA_M = 2 * NMOD * 2
GDN_STEPS = 34
MLSTM_STEPS = 15
M_ALL = 2 * len(LEVELS) * P


class Event:

    def __init__(self, sem, per, times, credit=0):
        self.sem, self.per, self.times, self.credit = sem, per, times, credit

    def n(self, run, turn, j):
        return turn * self.per + (run * self.times * self.per + j + 1 + self.credit)


class Chain:

    def __init__(self, eng, sem):
        self.eng, self.sem, self.count, self.turn = eng, sem, 0, None

    def __call__(self, ins):
        ins.then_inc(self.sem, 1)
        self.count += 1
        self.eng.wait_ge(self.sem, self.count if self.turn is None else self.turn + self.count)

    @contextmanager
    def turns(self, start, end, per):
        base = self.count
        with self.eng.Fori(start, end) as i:
            self.turn = (i - start) * per
            yield i
        assert self.count == base + per, (self.count - base, per)
        self.turn = None
        self.count = base + per * (end - start)


class Job:

    def __init__(self, turns, units):
        self.turns, self.units = turns, units


def layer_steps(l):
    return [("norm", l, 0), ("ffn", l, 0), ("norm", l, 1), ("gates", l, 0), ("gdn", l, 0), ("merge", l, 2),
            ("mlstm", l, 0), ("merge", l, 1), ("attn", l, 0), ("merge", l, 0), ("out", l, 0),
            ("norm", l, 2), ("ffn", l, 1)]


STEPS = [s for l in range(DEPTH) for s in layer_steps(l)]


def weight_jobs(w_gates, w_gate, w_up, w_down, w_in, w_branch, w_out):
    jobs = {}
    for step in STEPS:
        kind, l, p = step
        if kind == "ffn":
            gu = []
            for j in range(2):
                gu += [(w_gate[l, p], 0, KT, P * j, 2 * P), (w_up[l, p], 0, KT, P * j, 2 * P)]
            down = [(w_down[l, p], P * k0, kn, P * j, 4 * P) for j in range(4) for k0, kn in DOWN_CUTS]
            jobs[step] = [Job(FT // 2, gu), Job(2, down)]
        elif kind == "gates":
            jobs[step] = [Job(1, [(w_gates[l], 0, KT, P * j, 0) for j in range(2)])]
        elif kind == "gdn":
            jobs[step] = [Job(GH, [(w_in[l], 0, KT, OFF[c], P) for c in (9, 10, 11, 12)])]
        elif kind == "mlstm":
            jobs[step] = [Job(MH, [(w_in[l], 0, KT, OFF[c] + P * t, MT * P) for c in (3, 4, 5, 6) for t in range(MT)])]
        elif kind == "attn":
            jobs[step] = [Job(1, [(w_in[l], 0, KT, OFF[1] + P * g, 0), (w_in[l], 0, KT, OFF[2] + P * g, 0)]
                              + [(w_in[l], 0, KT, OFF[0] + P * (AG * g + q), 0) for q in range(AG)])
                          for g in range(AKV)]
        elif kind == "merge":
            units = []
            for j in range(2):
                units += [(w_in[l], 0, KT, OFF[15] + p * D + P * j, 2 * P), (w_branch[l, p], 0, KT, P * j, 2 * P)]
            jobs[step] = [Job(KT // 2, units)]
        elif kind == "out":
            jobs[step] = [Job(2, [(w_out[l], 0, KT, P * j, 4 * P) for j in range(4)])]
        else:
            jobs[step] = []
    return jobs


def trunk_kernel(nc, tokens, smalls, consts, levels, w_ada, w_gates, w_gate, w_up, w_down, w_in, w_branch,
                 w_out, out, debug=None):
    jobs = weight_jobs(w_gates, w_gate, w_up, w_down, w_in, w_branch, w_out)

    at = [nc.sbuf_base]
    top = nc.sbuf_usable_end

    def place(name, shape, dt, where=None):
        size = int(np.prod(shape[1:])) * (2 if dt == BF16 else 4)
        where = at if where is None else where
        where[0] = (where[0] + 31) // 32 * 32
        t = nc.alloc_sbuf_tensor_at(name, shape, dt, offset=where[0])
        where[0] += size
        assert where[0] <= top, (name, where[0], top)
        return t

    H = place("H", [P, KT * T], F32)
    xn_hi = place("xn_hi", [P, KT, T], F32R)
    xn_lo = place("xn_lo", [P, KT, T], F32R)
    raw = place("raw", [P, 4, KT * P], F32)
    w_hi = place("w_hi", [P, 2, KT * P], F32R)
    w_lo = place("w_lo", [P, 2, KT * P], F32R)
    con = place("con", [P, C_ALL], F32)
    lev = place("lev", [P, M_ALL], BF16)
    sml = place("sml", [P, S_ALL], F32)
    mod = place("mod", [P, DEPTH, NMOD * KT, 2], F32)
    nscale = place("nscale", [P, DEPTH, 3, KT, 2], F32)
    eps_col = place("eps_col", [P, 1], F32)
    rgate = place("rgate", [P, DEPTH, 3, KT, 2], F32)
    arena = at[0]

    ident, ones, rot = con[:, C_ID:C_ID + P], con[:, C_ONE:C_ONE + P], con[:, C_ROT:C_ROT + P]

    a = [arena]
    wide = [place(f"wide{j}", [P, KT, 512], F32, a) for j in range(NWIDE)]
    cond_at = place("cond_at", [P, KT, 2 * ADA_M - 2], F32, a)
    ada_rows = place("ada_rows", [P, DEPTH, 512], F32, a)
    lev_f = place("lev_f", [P, M_ALL], F32, a)
    a = [arena]
    sq = place("sq", [P, KT, T], F32, a)
    rms = place("rms", [P, T], F32, a)
    a = [arena]
    hid_hi = place("hid_hi", [P, FT * T], F32R, a)
    hid_lo = place("hid_lo", [P, FT * T], F32R, a)
    silu_g = place("silu_g", [P, 2, T], F32, a)
    hid = place("hid", [P, 2, T], F32, a)

    a = [arena]
    gate_a = place("gate_a", [P, T], F32, a)
    rows_m = place("rows_m", [P, T], F32, a)
    rows_n = place("rows_n", [P, T], F32, a)
    col_a = place("col_a", [P, NB, P], F32, a)
    col_g = place("col_g", [P, NB, P], F32, a)
    col_b = place("col_b", [P, NB, P // 2], F32, a)
    y_hi = place("y_hi", [P, KT * T], F32R, a)
    y_lo = place("y_lo", [P, KT * T], F32R, a)
    mix = a[0]
    y_sum = place("y_sum", [P, KT * T], F32, a)
    branch = a[0]
    a = [mix]
    zed = place("zed", [P, T], F32, a)
    sofp = place("sofp", [P, T], F32, a)
    cum = place("cum", [P, T], F32, a)
    unit_row = place("unit_row", [P, T], F32, a)
    run_max = place("run_max", [P, T], F32, a)
    coef = place("coef", [P, 1], F32, a)
    PAD = CONV_K // 2
    a = [mix]
    padded = place("padded", [P, 3, 2, CTX + 2 * PAD], F32, a)
    conv = place("conv", [P, 3, T], F32, a)
    qkv = place("qkv", [P, 3, T], F32, a)
    qk_n = place("qk_n", [P, 2, T], F32, a)
    g_raw = place("g_raw", [P, T], F32, a)
    g_gate = place("g_gate", [P, T], F32, a)
    k_tok = place("k_tok", [P, NB, P], F32, a)
    v_tok = place("v_tok", [P, NB, P], F32, a)
    conv_w = place("conv_w", [P, 3 * CONV_K], F32, a)
    pick = place("pick", [P, 2, P], F32, a)
    lane_col = place("lane_col", [P, 2, 3, NB], F32, a)
    end_col = place("end_col", [P, 2, 2, NB], F32, a)
    decay = place("decay", [P, 2, NB, P], F32, a)
    p_t = place("p_t", [P, 2, NB, P], F32, a)
    a_mat = place("a_mat", [P, 2, NB, P], F32, a)
    o_sum = decay[:, 0, :, :].rearrange("p b t -> p (b t)")
    inv = place("inv", [P, 2, NB, P], F32, a)
    inv_t = place("inv_t", [P, 2, NB, P], F32, a)
    prod = place("prod", [P, 2, NB, P], F32, a)
    q_dec = place("q_dec", [P, 2, NB, P], F32, a)
    k_end = place("k_end", [P, 2, NB, P], F32, a)
    v_beta = place("v_beta", [P, 2, NB, P], F32, a)
    resid = place("resid", [P, 2, P], F32, a)
    v_new = place("v_new", [P, 2, P], F32, a)
    state = place("state", [P, 2, P], F32, a)
    a = [branch]
    m_qkv = place("m_qkv", [P, 3, MT, T], F32, a)
    m_gate = place("m_gate", [P, MT, T], F32, a)
    m_vtok = place("m_vtok", [P, NB, MT * P], F32, a)
    m_w = place("m_w", [P, NB, T], F32, a)
    m_den = place("m_den", [P, T], F32, a)
    m_floor = place("m_floor", [P, T], F32, a)
    m_h = place("m_h", [P, MT, T], F32, a)
    m_tmp = place("m_tmp", [P, MT, T], F32, a)
    m_pick = place("m_pick", [P, 2, P], F32, a)
    m_wn = place("m_wn", [P, MT], F32, a)
    m_col = place("m_col", [P, 2, NB], F32, a)
    a = [branch]
    t_raw = place("t_raw", [P, 6, T], F32, a)
    t_sq = place("t_sq", [P, 2, T], F32, a)
    t_root = place("t_root", [P, 2, T], F32, a)
    t_rot = place("t_rot", [P, SEQ], F32, a)
    t_vtok = place("t_vtok", [P, NB, P], F32, a)
    t_s = place("t_s", [P, 3, T], F32, a)
    t_pt = place("t_pt", [P, 2, NB, AG * P], F32, a)
    t_o = place("t_o", [P, AG, P], F32, a)
    t_col = place("t_col", [P, 3, 6], F32, a)
    t_w = place("t_w", [P, 2], F32, a)
    a = [branch]
    b_gate = place("b_gate", [P, 2, T], F32, a)
    b_tmp = place("b_tmp", [P, 2, T], F32, a)

    bank = [nc.alloc_psum_tensor(f"bank{i}", [P, 512], F32) for i in range(8)]

    def event(name, per, times, credit=0):
        return Event(nc.alloc_semaphore(name), per, times, credit)

    dma_small = nc.alloc_semaphore("dma_small")
    dma_wide = [nc.alloc_semaphore(f"dma_wide{j}") for j in range(NWIDE)]
    raw_landed = [nc.alloc_semaphore(f"raw_landed{j}") for j in range(4)]
    hi_done = nc.alloc_semaphore("hi_done")
    split_done = nc.alloc_semaphore("split_done")
    unit_done = nc.alloc_semaphore("unit_done")
    out_done = nc.alloc_semaphore("out_done")
    ada_done = event("ada_done", NMOD * 2, DEPTH)
    ada_copied = event("ada_copied", DEPTH, 1)
    ada_turned = event("ada_turned", DEPTH, 1)
    cond_zeroed = event("cond_zeroed", 1, 1)
    cond_done = event("cond_done", 1, 1)
    mod_done = event("mod_done", 1, 1)
    dve_step, pool_turn, sp_turn = (nc.alloc_semaphore(n) for n in ("dve_step", "pool_turn", "sp_turn"))

    sq_done = event("sq_done", KT, 1)
    ss_done = event("ss_done", 1, 1)
    rvar_done = event("rvar_done", 1, 1)
    rms_done = event("rms_done", 1, 1)
    nmul_done = event("nmul_done", KT, 1)
    nmod_done = event("nmod_done", KT, 1)
    xn_ready = event("xn_ready", KT, 1)
    stream_ready = event("stream_ready", KT, 1)
    silu_done = event("silu_done", 2, FT // 2)
    hid_ready = event("hid_ready", 2, FT // 2, credit=2)
    res_done = event("res_done", 4, 2, credit=2)

    gate_act = event("gate_act", 6, 1)
    gate_dve = event("gate_dve", 3, 1)
    gate_pe = event("gate_pe", 2, 1)
    pad_zeroed = event("pad_zeroed", 1, 1)
    conv_filled = event("conv_filled", 3, GH, credit=1)
    conv_done = event("conv_done", 3, GH, credit=3)
    conv_silu = event("conv_silu", 3, GH)
    g_filled = event("g_filled", 1, GH)
    g_gate_done = event("g_gate_done", 1, GH)
    qk_sq = event("qk_sq", 2, GH)
    qk_ss = event("qk_ss", 2, GH)
    qk_var = event("qk_var", 2, GH)
    qk_rms = event("qk_rms", 2, GH)
    qk_ready = event("qk_ready", 2, GH)
    tok_t = event("tok_t", 2, GH)
    tok_ready = event("tok_ready", 2, GH)
    kk_done = event("kk_done", 2, GH)
    pick_ready = event("pick_ready", 2, GH)
    gam_row = event("gam_row", 2, GH)
    exp_gam = event("exp_gam", 2, GH)
    arg_ready = event("arg_ready", 2, GH)
    decay_done = event("decay_done", 2, GH)
    l_ready = event("l_ready", 2, GH)
    l_turned = event("l_turned", 2, GH)
    a_ready = event("a_ready", 2, GH)
    inv0_ready = event("inv0_ready", 2, GH)
    inv0_turned = event("inv0_turned", 2, GH)
    inv0_copied = event("inv0_copied", 2, GH)
    NL = len(LEVELS) - 1
    block_ready = event("block_ready", 2 * NL, GH)
    prod_done = event("prod_done", 2 * NL, GH)
    prod_ready = event("prod_ready", 2 * NL, GH)
    corr_done = event("corr_done", 2 * NL, GH)
    inv_ready = event("inv_ready", 2 * NL, GH)
    lane_ready = event("lane_ready", 2, GH)
    ks_done = event("ks_done", 2 * (NB - 1), GH)
    resid_ready = event("resid_ready", 2 * NB, GH)
    v_new_done = event("v_new_done", 2 * NB, GH)
    v_new_ready = event("v_new_ready", 2 * NB, GH)
    ds_done = event("ds_done", 2 * (NB - 1), GH)
    state_ready = event("state_ready", 2 * (NB - 1), GH)
    o_done = event("o_done", 2, GH)
    o_first = event("o_first", 1, GH)
    o_both = event("o_both", 1, GH)
    o_sq = event("o_sq", 1, GH)
    o_ss = event("o_ss", 1, GH)
    o_var = event("o_var", 1, GH)
    o_rms = event("o_rms", 1, GH)
    head_done = event("head_done", 1, GH, credit=1)
    m_filled = event("m_filled", 8, MH, credit=8)
    m_vt = event("m_vt", MT, MH)
    m_vt_ready = event("m_vt_ready", MT, MH, credit=MT)
    m_picked = event("m_picked", 2, MH)
    m_kq = event("m_kq", 3, MH)
    m_rows = event("m_rows", 2, MH)
    m_arg = event("m_arg", 2, MH)
    m_exp = event("m_exp", 2, MH)
    m_weighted = event("m_weighted", 2, MH)
    m_num = event("m_num", 2, MH)
    m_abs = event("m_abs", 2, MH)
    m_added = event("m_added", 2, MH, credit=2)
    m_sq = event("m_sq", 1, MH)
    m_ss = event("m_ss", 1, MH)
    m_var = event("m_var", 1, MH)
    m_rms = event("m_rms", 1, MH)
    m_head = event("m_head", 1, MH, credit=1)
    NU = 2 + AG
    t_filled = event("t_filled", NU, AKV, credit=NU)
    t_sqd = event("t_sqd", NU - 1, AKV)
    t_ss = event("t_ss", NU - 1, AKV)
    t_var = event("t_var", NU - 1, AKV)
    t_rms = event("t_rms", NU - 1, AKV)
    t_normed = event("t_normed", NU - 1, AKV)
    t_turned = event("t_turned", NU - 1, AKV)
    t_roped = event("t_roped", NU - 1, AKV)
    t_vt = event("t_vt", 1, AKV)
    t_vt_ready = event("t_vt_ready", 1, AKV)
    NQ = NB * AG
    t_scored = event("t_scored", NQ, AKV)
    t_masked = event("t_masked", NQ, AKV)
    t_exp = event("t_exp", NQ, AKV)
    t_prob = event("t_prob", NQ, AKV)
    t_pturn = event("t_pturn", NQ, AKV)
    t_pcopied = event("t_pcopied", NQ, AKV)
    t_out = event("t_out", NB, AKV)
    t_ocopy = event("t_ocopy", NB, AKV)
    t_osplit = event("t_osplit", NB, AKV)
    b_sig = event("b_sig", 2, KT // 2)
    b_done = event("b_done", 2, KT // 2, credit=2)
    y_split = event("y_split", KT, 1)
    out_res = event("out_res", 4, 2, credit=2)
    credits = (out_res, m_added, m_head, hid_ready, res_done, conv_done, head_done, b_done)

    def b_first(l):
        return 0

    def n_first(l):
        return AG * b_first(l)

    def scan_order(d):
        return (0, 1, 2, 3) if d == 0 else (1, 0, 3, 2)

    def chunk_end(d):
        return P - 1 if d == 0 else 0

    merge_run = {s: n for n, s in enumerate(s for s in STEPS if s[0] == "merge")}

    def branch_whole(l, p):
        if p == 2:
            return head_done.sem, head_done.n(l, GH - 1, 0)
        if p == 1:
            return m_head.sem, m_head.n(l, MH - 1, 0)
        return t_osplit.sem, t_osplit.n(l, AKV - 1, NB - 1)

    def reach(d, sb):
        t0, t1 = P * sb, P * sb + P
        spans = [(t0, t1, True)]
        if d == 0:
            spans += [(t1, T, False)] if t1 < T else []
        else:
            lo = 0 if t0 < CTX else CTX
            spans += [(lo, t0, False)] if lo < t0 else []
            spans += [(CTX, T, False)] if t0 < CTX else []
        return spans

    def joined(d, sb):
        out = []
        for t0, t1, _ in sorted(reach(d, sb)):
            if out and out[-1][1] == t0:
                out[-1] = (out[-1][0], t1)
            else:
                out.append((t0, t1))
        return out

    def by_reach(d):
        return (0, 1, 2, 3) if d == 0 else (1, 0, 3, 2)

    def kq_view(sb):
        return (bank[2 + sb], 0, 0) if sb < 2 else (bank[4], CTX * (sb - 2), CTX)

    block = nc.Block()
    blk = block.__enter__()

    first_unit, u = {}, 0
    for step in STEPS:
        for n, job in enumerate(jobs[step]):
            first_unit[step, n] = u
            u += job.turns * len(job.units)

    def norm_run(l, j):
        return 3 * l + j

    @blk.sync
    def _(sp):
        sp.dma_start(sml[:, :], smalls).then_inc(dma_small, 16)
        sp.dma_start(con[:, :], consts).then_inc(dma_small, 16)
        sp.dma_start(lev_f[:, :], levels).then_inc(dma_small, 16)
        sp.dma_start(H[:, :].rearrange("p (k t) -> p k t", k=KT),
                     tokens.rearrange("(k p) t -> p k t", p=P)).then_inc(dma_small, 16)
        for l in range(DEPTH):
            for n in range(NMOD * 2):
                g = l * NMOD * 2 + n
                if g >= NWIDE:
                    sp.wait_ge(ada_done.sem, ada_done.n(0, 0, g - NWIDE))
                sp.dma_start(wide[g % NWIDE][:, :, :], w_ada[l, :, 512 * n:512 * n + 512].rearrange(
                    "(k p) n -> p k n", p=P)).then_inc(dma_wide[g % NWIDE], 16)

        def load(u, turn_units, i, unit):
            w, row, kn, col, step = unit
            if not isinstance(i, int) or u + turn_units * i >= 4:
                sp.wait_ge(split_done, turn_units * i + (u - 3))
                if not isinstance(i, int):
                    sp.sem_inc(sp_turn, 1)
            src = w[row:row + P * kn, bass.ds(i * step + col, P)] if not isinstance(i, int) else \
                w[row:row + P * kn, i * step + col:i * step + col + P]
            sp.dma_start(raw[:, u % 4, 0:kn * P].rearrange("p (k n) -> p k n", k=kn),
                         src.rearrange("(k p) n -> p k n", p=P)).then_inc(raw_landed[u % 4], 16)

        for step in STEPS:
            for n, job in enumerate(jobs[step]):
                u0, m = first_unit[step, n], len(job.units)
                start = 0
                if job.turns == 1 or u0 < 4:
                    for j, unit in enumerate(job.units):
                        load(u0 + j, m, 0, unit)
                    start = 1
                if start < job.turns:
                    with sp.Fori(start, job.turns) as i:
                        for j, unit in enumerate(job.units):
                            load(u0 + j, m, i, unit)
        sp.wait_ge(stream_ready.sem, stream_ready.n(len([s for s in STEPS if s[0] == "norm"]) - 1, 0, KT - 1))
        sp.dma_start(out.rearrange("(k p) t -> p k t", p=P),
                     H[:, :].rearrange("p (k t) -> p k t", k=KT)[:, :, CTX:T]).then_inc(out_done, 16)
        sp.wait_ge(out_done, 16)

    @blk.gpsimd
    def _(pool):
        def split(u, turn_units, i, kn):
            n = kn * P
            pool.wait_ge(raw_landed[u % 4], i * (4 * turn_units) + (16 * (u // 4) + 16))
            if not isinstance(i, int) or u + turn_units * i >= 2:
                pool.wait_ge(unit_done, turn_units * i + (u - 1))
            if not isinstance(i, int):
                pool.sem_inc(pool_turn, 1)
            nc.gpsimd.tensor_scalar(w_hi[:, u % 2, 0:n], raw[:, u % 4, 0:n], 1.0, 1.0, ALU.mult,
                                    ALU.mult).then_inc(hi_done, 1)
            pool.wait_ge(hi_done, turn_units * i + (u + 1))
            nc.gpsimd.tensor_tensor(w_lo[:, u % 2, 0:n], raw[:, u % 4, 0:n], w_hi[:, u % 2, 0:n].bitcast(F32),
                                    ALU.subtract).then_inc(split_done, 1)

        def split_job(step, n, start=0):
            job, u0 = jobs[step][n], first_unit[step, n]
            m = len(job.units)
            if job.turns == 1 or u0 < 2:
                for j, unit in enumerate(job.units):
                    split(u0 + j, m, 0, unit[2])
                start = 1
            if start < job.turns:
                with pool.Fori(start, job.turns) as i:
                    for j, unit in enumerate(job.units):
                        split(u0 + j, m, i, unit[2])

        def level_blocks(l, h, levels):
            for v in levels:
                for d in range(2):
                    j = 2 * v + d
                    if v == 0:
                        pool.wait_ge(inv0_ready.sem, inv0_ready.n(l, h, d))
                    else:
                        pool.wait_ge(prod_done.sem, prod_done.n(l, h, j - 2))
                    m = lev[:, (d * len(LEVELS) + v + 1) * P:(d * len(LEVELS) + v + 2) * P].unsqueeze(1)
                    nc.gpsimd.tensor_tensor(decay[:, d, :, :], a_mat[:, d, :, :], m.to_broadcast([P, NB, P]),
                                            ALU.mult).then_inc(block_ready.sem, 1)

        for e in credits:
            if e.credit:
                pool.sem_inc(e.sem, e.credit)
        for step in STEPS:
            kind, l, p = step
            if kind == "gdn":
                u0 = first_unit[step, 0]
                for j in range(4):
                    split(u0 + j, 4, 0, KT)
                with pool.Fori(0, GH - 1) as h:
                    for j in range(3):
                        split(u0 + 4 + j, 4, h, KT)
                    level_blocks(l, h, (0,))
                    split(u0 + 7, 4, h, KT)
                    level_blocks(l, h, range(1, NL))
                level_blocks(l, GH - 1, range(NL))
            else:
                for n in range(len(jobs[step])):
                    split_job(step, n)

    @blk.tensor
    def _(pe):
        mm = nc.tensor.matmul

        def unit(u, i, m, kn, dst, hi, lo, start=True, stop=True, rows=None):
            rows = range(kn) if rows is None else rows
            if rows[0] == 0:
                pe.wait_ge(split_done, m * i + (u + 1))
            for k in rows:
                wh, wl = w_hi[:, u % 2, P * k:P * k + P], w_lo[:, u % 2, P * k:P * k + P]
                mm(dst, wh, hi(k), start=start and k == 0, stop=False)
                mm(dst, wh, lo(k), start=False, stop=False)
                last = mm(dst, wl, hi(k), start=False, stop=stop and k == kn - 1)
            if rows[-1] == kn - 1:
                last.then_inc(unit_done, 1)

        def xh(k):
            return xn_hi[:, k, :]

        def xl(k):
            return xn_lo[:, k, :]

        def ada():
            pe.wait_ge(dma_small, 64)
            pe.wait_ge(cond_done.sem, 1)
            for l in range(DEPTH):
                for n in range(NMOD * 2):
                    g = l * NMOD * 2 + n
                    pe.wait_ge(dma_wide[g % NWIDE], 16 * (g // NWIDE + 1))
                    for k in range(KT):
                        last = mm(bank[l][0:ADA_M, :], cond_at[:, k, ADA_M - 2 - 2 * n:2 * ADA_M - 2 - 2 * n],
                                  wide[g % NWIDE][:, k, :], start=n == 0 and k == 0,
                                  stop=n == NMOD * 2 - 1 and k == KT - 1)
                    last.then_inc(ada_done.sem, 1)
            for l in range(DEPTH):
                pe.wait_ge(ada_copied.sem, ada_copied.n(0, 0, l))
                for t in range(4):
                    last = nc.tensor.transpose(bank[2 + l][:, ADA_M * t:ADA_M * t + ADA_M],
                                               ada_rows[0:ADA_M, l, P * t:P * t + P], ident[0:ADA_M, 0:ADA_M])
                last.then_inc(ada_turned.sem, 1)

        def norm(l, j):
            r = norm_run(l, j)
            for k in range(KT):
                pe.wait_ge(sq_done.sem, sq_done.n(r, 0, k))
                last = mm(bank[7][:, :], ones, sq[:, k, :], start=k == 0, stop=k == KT - 1)
            last.then_inc(ss_done.sem, 1)

        def ffn(step, l, p):
            r = 2 * l + p
            u0, nr = first_unit[step, 0], norm_run(l, 2 * p)
            for k in range(KT):
                pe.wait_ge(xn_ready.sem, xn_ready.n(nr, 0, k))
            with pe.Fori(0, FT // 2) as i:
                for j in range(2):
                    pe.wait_ge(hid_ready.sem, hid_ready.n(r, i, j - 2))
                    unit(u0 + 2 * j, i, 4, KT, bank[2 * j][:, :], xh, xl)
                    unit(u0 + 2 * j + 1, i, 4, KT, bank[2 * j + 1][:, :], xh, xl)
            u0 = first_unit[step, 1]
            pe.wait_ge(hid_ready.sem, hid_ready.n(r, FT // 2 - 1, 1))
            with pe.Fori(0, 2) as i:
                for j in range(4):
                    pe.wait_ge(res_done.sem, res_done.n(r, i, j - 2))
                    for c, (k0, kn) in enumerate(DOWN_CUTS):
                        unit(u0 + 3 * j + c, i, 12, kn, bank[4 + j % 2][:, :],
                             lambda k: hid_hi[:, T * (k0 + k):T * (k0 + k) + T],
                             lambda k: hid_lo[:, T * (k0 + k):T * (k0 + k) + T],
                             start=c == 0, stop=c == 2)

        def gates(step, l):
            u0 = first_unit[step, 0]
            for k in range(KT):
                pe.wait_ge(xn_ready.sem, xn_ready.n(norm_run(l, 1), 0, k))
            for j in range(2):
                unit(u0 + j, 0, 2, KT, bank[j][:, :], xh, xl)
            pe.wait_ge(gate_dve.sem, gate_dve.n(l, 0, 1))
            for b in range(NB):
                last = nc.tensor.transpose(bank[2][:, P * b:P * b + P], gate_a[:, P * b:P * b + P], ident)
            last.then_inc(gate_pe.sem, 1)
            for b in range(NB):
                last = nc.tensor.transpose(bank[3][:, P * b:P * b + P], rows_m[:, P * b:P * b + P], ident)
            last.then_inc(gate_pe.sem, 1)

        def gdn_project(l, h, j, u, i, rows=range(KT)):
            if rows[0] == 0:
                if j == 0:
                    pe.wait_ge(conv_filled.sem, conv_filled.n(l, h, -1))
                elif j == 1:
                    pe.wait_ge(g_filled.sem, g_filled.n(l, h, -1))
                else:
                    pe.wait_ge(conv_filled.sem, conv_filled.n(l, h, j - 2))
            unit(u + j, i, 4, KT, bank[j % 2][:, :], xh, xl, rows=rows)

        def gdn_squares(l, h):
            for j in range(2):
                pe.wait_ge(qk_sq.sem, qk_sq.n(l, h, j))
                mm(bank[2 + j][:, :], ones, conv[:, j, :], start=True, stop=True).then_inc(qk_ss.sem, 1)

        def gdn_head(l, h, u0, more):
            q_t, k_t, v_t = qk_n[:, 0, :], qk_n[:, 1, :], qkv[:, 2, :]

            def blocks(b):
                return slice(P * b, P * b + P)

            def project(j, k0, k1):
                if more:
                    gdn_project(l, h + 1, j, u0 + 4, h, range(k0, k1))

            pe.wait_ge(qk_ready.sem, qk_ready.n(l, h, 0))
            for b in range(NB):
                last = nc.tensor.transpose(bank[3][:, blocks(b)], k_t[:, blocks(b)], ident)
            last.then_inc(tok_t.sem, 1)
            for d in range(2):
                pe.wait_ge(pick_ready.sem, pick_ready.n(l, h, d))
                mm(bank[4 + 2 * d][:, :], pick[:, d, :], rows_m[:, :], start=True,
                   stop=True).then_inc(gam_row.sem, 1)
            pe.wait_ge(o_var.sem, o_var.n(l, h, -1))
            pe.wait_ge(conv_silu.sem, conv_silu.n(l, h, 2))
            for b in range(NB):
                last = nc.tensor.transpose(bank[2][:, blocks(b)], v_t[:, blocks(b)], ident)
            last.then_inc(tok_t.sem, 1)
            pe.wait_ge(qk_ready.sem, qk_ready.n(l, h, 1))
            for j, x in enumerate((k_t, q_t)):
                pe.wait_ge(tok_ready.sem, tok_ready.n(l, h, j))
                for b in range(NB):
                    last = mm(bank[3 - j][:, blocks(b)], k_t[:, blocks(b)], x[:, blocks(b)], start=True, stop=True)
                last.then_inc(kk_done.sem, 1)
                if j == 0:
                    project(0, 0, 4)
            for d in range(2):
                pe.wait_ge(l_ready.sem, l_ready.n(l, h, d))
                for b in range(NB):
                    last = nc.tensor.transpose(bank[5 + 2 * d][:, blocks(b)], prod[:, d, b, :], ident)
                last.then_inc(l_turned.sem, 1)
            project(0, 4, KT)
            project(1, 0, KT)
            for d in range(2):
                pe.wait_ge(inv0_ready.sem, inv0_ready.n(l, h, d))
                for b in range(NB):
                    last = nc.tensor.transpose(bank[4 + 2 * d][:, blocks(b)], inv[:, d, b, :], ident)
                last.then_inc(inv0_turned.sem, 1)
            for v in range(NL):
                for d in range(2):
                    j = 2 * v + d
                    pe.wait_ge(block_ready.sem, block_ready.n(l, h, j))
                    if v == 0:
                        pe.wait_ge(inv0_copied.sem, inv0_copied.n(l, h, d))
                    else:
                        pe.wait_ge(inv_ready.sem, inv_ready.n(l, h, j - 2))
                    for b in range(NB):
                        last = mm(bank[4 + 2 * d][:, blocks(b)], decay[:, d, b, :], inv_t[:, d, b, :],
                                  start=True, stop=True)
                    last.then_inc(prod_done.sem, 1)
                if v == 0:
                    project(2, 0, 4)
                elif v == 4 and more:
                    gdn_squares(l, h + 1)
                for d in range(2):
                    j = 2 * v + d
                    pe.wait_ge(prod_ready.sem, prod_ready.n(l, h, j))
                    for b in range(NB):
                        last = mm(bank[5 + 2 * d][:, blocks(b)], inv[:, d, b, :], prod[:, d, b, :],
                                  start=True, stop=True)
                    if v < NL - 1:
                        for b in range(NB):
                            last = mm(bank[4 + 2 * d][:, blocks(b)], prod[:, d, b, :], inv[:, d, b, :],
                                      start=True, stop=True)
                    last.then_inc(corr_done.sem, 1)
                if v == 0:
                    project(2, 4, KT)
            for i in range(NB):
                for d in range(2):
                    b = scan_order(d)[i]
                    if i == 0 and d == 0:
                        pe.wait_ge(inv_ready.sem, inv_ready.n(l, h, 2 * NL - 1))
                        pe.wait_ge(lane_ready.sem, lane_ready.n(l, h, 1))
                    elif i > 0:
                        pe.wait_ge(state_ready.sem, state_ready.n(l, h, 2 * (i - 1) + d))
                        mm(bank[4 + 2 * d][:, 0:P], k_t[:, blocks(b)], state[:, d, :], start=True,
                           stop=True).then_inc(ks_done.sem, 1)
                if i > 0:
                    project(3, i - 1, i)
                for d in range(2):
                    b = scan_order(d)[i]
                    if i > 0:
                        mm(bank[5 + 2 * d][:, blocks(b)], state[:, d, :], q_dec[:, d, b, :], start=True, stop=False)
                    pe.wait_ge(resid_ready.sem, resid_ready.n(l, h, 2 * i + d))
                    mm(bank[4 + 2 * d][:, P:2 * P], inv_t[:, d, b, :], resid[:, d, :], start=True,
                       stop=True).then_inc(v_new_done.sem, 1)
                if i == NB - 1:
                    project(3, 3, 5)
                for d in range(2):
                    b = scan_order(d)[i]
                    pe.wait_ge(v_new_ready.sem, v_new_ready.n(l, h, 2 * i + d))
                    if i < NB - 1:
                        mm(bank[4 + 2 * d][:, 2 * P:3 * P], k_end[:, d, b, :], v_new[:, d, :], start=True,
                           stop=True).then_inc(ds_done.sem, 1)
                    last = mm(bank[5 + 2 * d][:, blocks(b)], v_new[:, d, :], p_t[:, d, b, :], start=i == 0,
                              stop=True)
                    if i == NB - 1:
                        last.then_inc(o_done.sem, 1)
            project(3, 5, KT)
            pe.wait_ge(o_sq.sem, o_sq.n(l, h, 0))
            mm(bank[2][:, :], ones, prod[:, 0, :, :].rearrange("p b t -> p (b t)"), start=True,
               stop=True).then_inc(o_ss.sem, 1)

        def gdn(step, l):
            u0 = first_unit[step, 0]
            for j in range(4):
                gdn_project(l, 0, j, u0, 0)
            pe.wait_ge(gate_dve.sem, gate_dve.n(l, 0, 2))
            gdn_squares(l, 0)
            with pe.Fori(0, GH - 1) as h:
                gdn_head(l, h, u0, True)
            gdn_head(l, GH - 1, u0, False)

        def mlstm_project(l, h, j, u0, m=8):
            pe.wait_ge(m_filled.sem, m_filled.n(l, h, j - 2))
            unit(u0 + j, h, m, KT, bank[j % 2][:, :], xh, xl)

        def mlstm_head(l, h, u0, more):
            def project(*js):
                for j in js if more else ():
                    pe.wait_ge(m_filled.sem, m_filled.n(l, h + 1, j - 2))
                    unit(u0 + 8 + j, h, 8, KT, bank[j % 2][:, :], xh, xl)

            pe.wait_ge(m_filled.sem, m_filled.n(l, h, 5))
            pe.wait_ge(m_head.sem, m_head.n(l, h, -1))
            for v in range(MT):
                for b in range(NB):
                    last = nc.tensor.transpose(bank[5 + v][:, P * b:P * b + P],
                                               m_qkv[:, 2, v, P * b:P * b + P], ident)
                last.then_inc(m_vt.sem, 1)
            for sb in range(NB):
                dst, c0, t0 = kq_view(sb)
                for v in range(MT):
                    last = mm(dst[:, c0:c0 + T - t0], m_qkv[:, 1, v, P * sb:P * sb + P], m_qkv[:, 0, v, t0:T],
                              start=v == 0, stop=v == MT - 1)
                if sb != 2:
                    last.then_inc(m_kq.sem, 1)
            project(0)
            for d in range(2):
                pe.wait_ge(m_picked.sem, m_picked.n(l, h, d))
                if d == 0:
                    pe.wait_ge(m_vt_ready.sem, m_vt_ready.n(l, h, MT - 1))
                else:
                    pe.wait_ge(m_added.sem, m_added.n(l, h, 0))
                mm(bank[5][:, :], m_pick[:, d, :], rows_m[:, :], start=True, stop=True)
                mm(bank[6][:, :], m_pick[0:64, d, :], rows_n[0:64, :], start=True, stop=True).then_inc(m_rows.sem, 1)
                project(*((1,) if d == 0 else (3, 4)))
                pe.wait_ge(m_weighted.sem, m_weighted.n(l, h, d))
                for n in range(1 + MT):
                    dst = bank[7] if n == 0 else bank[4 + n]
                    for i, sb in enumerate(by_reach(d)):
                        w = ones if n == 0 else m_vtok[:, sb, P * (n - 1):P * n]
                        for c0, c1 in joined(d, sb):
                            last = mm(dst[:, c0:c1], w, m_w[:, sb, c0:c1], start=i == 0, stop=i == NB - 1)
                last.then_inc(m_num.sem, 1)
                project(*((2,) if d == 0 else (5, 6)))
            pe.wait_ge(m_sq.sem, m_sq.n(l, h, 0))
            for v in range(MT):
                last = mm(bank[5][:, :], ones, m_tmp[:, v, :], start=v == 0, stop=v == MT - 1)
            last.then_inc(m_ss.sem, 1)
            project(7)

        def mlstm(step, l):
            u0 = first_unit[step, 0]
            for j in range(8):
                mlstm_project(l, 0, j, u0)
            with pe.Fori(0, MH - 1) as h:
                mlstm_head(l, h, u0, True)
            mlstm_head(l, MH - 1, u0, False)

        def attn_group(l, g, u0):
            def mean_square(j):
                pe.wait_ge(t_sqd.sem, t_sqd.n(l, g, j))
                if j > 0:
                    pe.wait_ge(t_var.sem, t_var.n(l, g, j - 1))
                mm(bank[3][:, :], ones, t_sq[:, j % 2, :], start=True, stop=True).then_inc(t_ss.sem, 1)

            def rotary_partner(j):
                pe.wait_ge(t_normed.sem, t_normed.n(l, g, j))
                if j > 0:
                    pe.wait_ge(t_roped.sem, t_roped.n(l, g, j - 1))
                mm(bank[4][:, 0:SEQ], rot, t_raw[:, 0 if j == 0 else j + 1, CTX:T], start=True,
                   stop=True).then_inc(t_turned.sem, 1)

            for j in range(NU):
                pe.wait_ge(t_filled.sem, t_filled.n(l, g, j - 2))
                unit(u0 + j, 0, 0, KT, bank[j % 2][:, :], xh, xl)
                if j == 1:
                    mean_square(0)
                elif j == 2:
                    pe.wait_ge(t_filled.sem, t_filled.n(l, g, 1))
                    for b in range(NB):
                        last = nc.tensor.transpose(bank[2][:, P * b:P * b + P], t_raw[:, 1, P * b:P * b + P], ident)
                    last.then_inc(t_vt.sem, 1)
                    rotary_partner(0)
                elif j > 2:
                    mean_square(j - 2)
                if j > 3:
                    rotary_partner(j - 3)
            mean_square(AG)
            rotary_partner(AG - 1)
            rotary_partner(AG)
            pe.wait_ge(t_vt_ready.sem, t_vt_ready.n(l, g, 0))
            pe.wait_ge(t_roped.sem, t_roped.n(l, g, NU - 2))

            def score(n):
                b, q = divmod(n, AG)
                keys = CTX if b < 2 else T
                if n >= n_first(l) + 2:
                    pe.wait_ge(t_exp.sem, t_exp.n(l, g, n - 2))
                mm(bank[5 + n % 2][:, 0:keys], t_raw[:, 2 + q, P * b:P * b + P], t_raw[:, 0, 0:keys],
                   start=True, stop=True).then_inc(t_scored.sem, 1)

            def blend(b):
                kb = 2 if b < 2 else NB
                pe.wait_ge(t_pcopied.sem, t_pcopied.n(l, g, AG * b + AG - 1))
                if b > b_first(l):
                    pe.wait_ge(t_ocopy.sem, t_ocopy.n(l, g, b - 1))
                for k in range(kb):
                    last = mm(bank[7][:, :], t_vtok[:, k, :], t_pt[:, b % 2, k, :], start=k == 0, stop=k == kb - 1)
                last.then_inc(t_out.sem, 1)

            score(n_first(l))
            score(n_first(l) + 1)
            for n in range(n_first(l), NQ):
                b, q = divmod(n, AG)
                kb = 2 if b < 2 else NB
                if n + 2 < NQ:
                    score(n + 2)
                pe.wait_ge(t_prob.sem, t_prob.n(l, g, n))
                if n >= n_first(l) + 2:
                    pe.wait_ge(t_pcopied.sem, t_pcopied.n(l, g, n - 2))
                for k in range(kb):
                    last = nc.tensor.transpose(bank[2 + n % 2][:, P * k:P * k + P],
                                               t_s[:, n % 3, P * k:P * k + P], ident)
                last.then_inc(t_pturn.sem, 1)
                if q == 1 and b > b_first(l):
                    blend(b - 1)
            blend(NB - 1)

        def attn(step, l):
            for g in range(AKV):
                attn_group(l, g, first_unit[step, g])

        def merge(step, l, p):
            u0, r = first_unit[step, 0], merge_run[step]
            pe.wait_ge(*branch_whole(l, p))
            with pe.Fori(0, KT // 2) as i:
                for j in range(2):
                    pe.wait_ge(b_done.sem, b_done.n(r, i, j - 2))
                    unit(u0 + 2 * j, i, 4, KT, bank[2 * j][:, :], xh, xl)
                    unit(u0 + 2 * j + 1, i, 4, KT, bank[2 * j + 1][:, :], yh, yl)
            pe.wait_ge(b_done.sem, b_done.n(r, KT // 2 - 1, 1))

        def yh(k):
            return y_hi[:, T * k:T * k + T]

        def yl(k):
            return y_lo[:, T * k:T * k + T]

        def project_out(step, l):
            u0 = first_unit[step, 0]
            pe.wait_ge(y_split.sem, y_split.n(l, 0, KT - 1))
            with pe.Fori(0, 2) as i:
                for j in range(4):
                    pe.wait_ge(out_res.sem, out_res.n(l, i, j - 2))
                    unit(u0 + j, i, 4, KT, bank[4 + j % 2][:, :], yh, yl)

        ada()
        for step in STEPS:
            kind, l, p = step
            if kind == "norm":
                norm(l, p)
            elif kind == "ffn":
                ffn(step, l, p)
            elif kind == "gates":
                gates(step, l)
            elif kind == "gdn":
                gdn(step, l)
            elif kind == "mlstm":
                mlstm(step, l)
            elif kind == "attn":
                attn(step, l)
            elif kind == "merge":
                merge(step, l, p)
            elif kind == "out":
                project_out(step, l)

    @blk.scalar
    def _(act):
        def silu(dst, src):
            return nc.scalar.activation(dst, src, ACT.Silu)

        def inv_root(dst, src, scale, turn, logged, done):
            nc.scalar.activation(dst, src, ACT.Ln, scale=scale, bias=eps_col[:, 0:1]).then_inc(logged[0].sem, 1)
            act.wait_ge(logged[0].sem, logged[0].n(*turn, logged[1]))
            nc.scalar.activation(dst, dst, ACT.Exp, scale=-0.5).then_inc(done.sem, 1)

        def log_exp_tables():
            act.preload_act_table_set("natural_log_exp_and_others")

        def norm(l, j):
            r = norm_run(l, j)
            for k in range(KT):
                if r > 0:
                    act.wait_ge(stream_ready.sem, stream_ready.n(r - 1, 0, k))
                nc.scalar.activation(sq[:, k, :], H[:, T * k:T * k + T], ACT.Square).then_inc(sq_done.sem, 1)
            log_exp_tables()
            act.wait_ge(ss_done.sem, ss_done.n(r, 0, 0))
            inv_root(rms[:, :], bank[7][:, :], 1.0 / D, (r, 0), (rvar_done, 0), rms_done)
            for k in range(KT):
                act.wait_ge(nmul_done.sem, nmul_done.n(r, 0, k))
                for c, (a0, a1) in enumerate(HALVES):
                    last = nc.scalar.activation(sq[:, k, a0:a1], sq[:, k, a0:a1], ACT.Identity,
                                                scale=nscale[:, l, j, k, c:c + 1],
                                                bias=mod[:, l, 3 * j * KT + k, c:c + 1])
                last.then_inc(nmod_done.sem, 1)

        def ffn(step, l, p):
            r, u0 = 2 * l + p, first_unit[step, 0]
            with act.Fori(0, FT // 2) as i:
                for j in range(2):
                    act.wait_ge(unit_done, i * 4 + (u0 + 2 * j + 1))
                    act.wait_ge(hid_ready.sem, hid_ready.n(r, i, j - 2))
                    silu(silu_g[:, j, :], bank[2 * j][:, :]).then_inc(silu_done.sem, 1)

        def gates(step, l):
            u0, s0 = first_unit[step, 0], l * S_LAYER
            A = nc.scalar.activation
            act.wait_ge(unit_done, u0 + 1)
            A(gate_a[0:64, :], bank[0][0:64, :], ACT.Identity, bias=sml[0:64, s0 + S_BA:s0 + S_BA + 1])
            A(gate_a[64:P, :], bank[0][64:P, :], ACT.Sigmoid).then_inc(gate_act.sem, 1)
            A(coef[:, :], sml[:, s0 + S_ALOG:s0 + S_ALOG + 1], ACT.Exp).then_inc(gate_act.sem, 1)
            act.wait_ge(gate_dve.sem, gate_dve.n(l, 0, 0))
            A(sofp[:, :], zed[:, :], ACT.Abs).then_inc(gate_act.sem, 1)
            act.wait_ge(gate_act.sem, gate_act.n(l, 0, 2))
            A(sofp[:, :], sofp[:, :], ACT.Exp, scale=-1.0).then_inc(gate_act.sem, 1)
            act.wait_ge(gate_act.sem, gate_act.n(l, 0, 3))
            A(sofp[:, :], sofp[:, :], ACT.Ln, bias=1.0).then_inc(gate_act.sem, 1)
            act.wait_ge(gate_dve.sem, gate_dve.n(l, 0, 2))
            A(col_b[:, :, :], col_g[:, :, 64:P], ACT.Exp).then_inc(gate_act.sem, 1)

        def gdn_fill(l, h, j, landed):
            act.wait_ge(unit_done, landed)
            if j < 3:
                act.wait_ge(conv_done.sem, conv_done.n(l, h, j - 3))
                nc.scalar.activation(padded[:, j, :, PAD:PAD + CTX], bank[j % 2][:, :].rearrange(
                    "p (s t) -> p s t", s=2), ACT.Copy).then_inc(conv_filled.sem, 1)
            else:
                nc.scalar.activation(g_raw[:, :], bank[1][:, :], ACT.Copy).then_inc(g_filled.sem, 1)

        def gdn_silu(l, h, j):
            act.wait_ge(conv_done.sem, conv_done.n(l, h, j))
            if j == 0:
                act.wait_ge(qk_ready.sem, qk_ready.n(l, h, -1))
            silu(qkv[:, j, :], conv[:, j, :]).then_inc(conv_silu.sem, 1)

        def gdn_square(l, h, j):
            act.wait_ge(conv_silu.sem, conv_silu.n(l, h, j))
            nc.scalar.activation(conv[:, j, :], qkv[:, j, :], ACT.Square).then_inc(qk_sq.sem, 1)

        def gdn_root(l, h):
            for j in range(2):
                act.wait_ge(qk_ss.sem, qk_ss.n(l, h, j))
                inv_root(conv[:, j, :], bank[2 + j][:, :], 1.0, (l, h), (qk_var, j), qk_rms)

        def gdn_head(l, h, u0, more):
            A = nc.scalar.activation

            def by_block(x):
                return x.rearrange("p (b t) -> p b t", b=NB)

            def fill(j):
                if more:
                    gdn_fill(l, h + 1, j, h * 4 + (u0 + 4 + j + 1))

            act.wait_ge(tok_t.sem, tok_t.n(l, h, 0))
            A(k_tok[:, :, :], by_block(bank[3][:, :]), ACT.Copy).then_inc(tok_ready.sem, 1)
            for d in range(2):
                act.wait_ge(gam_row.sem, gam_row.n(l, h, d))
                A(inv_t[:, d, :, :], by_block(bank[4 + 2 * d][:, :]), ACT.Exp).then_inc(exp_gam.sem, 1)
            act.wait_ge(tok_t.sem, tok_t.n(l, h, 1))
            A(v_tok[:, :, :], by_block(bank[2][:, :]), ACT.Copy).then_inc(tok_ready.sem, 1)
            for d in range(2):
                act.wait_ge(arg_ready.sem, arg_ready.n(l, h, d))
                A(decay[:, d, :, :], decay[:, d, :, :], ACT.Exp).then_inc(decay_done.sem, 1)
            fill(0)
            fill(1)
            for d in range(2):
                act.wait_ge(inv0_turned.sem, inv0_turned.n(l, h, d))
                A(inv_t[:, d, :, :], by_block(bank[4 + 2 * d][:, :]), ACT.Copy).then_inc(inv0_copied.sem, 1)
            for v in range(NL):
                for d in range(2):
                    act.wait_ge(prod_done.sem, prod_done.n(l, h, 2 * v + d))
                    A(prod[:, d, :, :], by_block(bank[4 + 2 * d][:, :]), ACT.Copy).then_inc(prod_ready.sem, 1)
                if v == 0:
                    fill(2)
                if v == 2 and more:
                    gdn_silu(l, h + 1, 0)
                    gdn_square(l, h + 1, 0)
                if v == 3:
                    if more:
                        gdn_silu(l, h + 1, 1)
                        gdn_square(l, h + 1, 1)
                    act.wait_ge(g_filled.sem, g_filled.n(l, h, 0))
                    act.wait_ge(head_done.sem, head_done.n(l, h, -1))
                    silu(g_gate[:, :], g_raw[:, :]).then_inc(g_gate_done.sem, 1)
                if v == 4:
                    if more:
                        gdn_silu(l, h + 1, 2)
                    log_exp_tables()
            if more:
                gdn_root(l, h + 1)
            for j in range(2 * NB):
                d = j % 2
                act.wait_ge(v_new_done.sem, v_new_done.n(l, h, j))
                A(v_new[:, d, :], bank[4 + 2 * d][:, P:2 * P], ACT.Copy).then_inc(v_new_ready.sem, 1)
            act.wait_ge(o_done.sem, o_done.n(l, h, 0))
            A(o_sum, bank[5][:, :], ACT.Copy).then_inc(o_first.sem, 1)
            act.wait_ge(o_both.sem, o_both.n(l, h, 0))
            A(prod[:, 0, :, :], by_block(o_sum), ACT.Square).then_inc(o_sq.sem, 1)
            fill(3)
            act.wait_ge(o_ss.sem, o_ss.n(l, h, 0))
            inv_root(prod[:, 1, :, :], by_block(bank[2][:, :]), 1.0 / P, (l, h), (o_var, 0), o_rms)

        def gdn(step, l):
            u0 = first_unit[step, 0]
            act.wait_ge(pad_zeroed.sem, pad_zeroed.n(l, 0, 0))
            for j in range(4):
                gdn_fill(l, 0, j, u0 + j + 1)
            for j in range(3):
                gdn_silu(l, 0, j)
                if j < 2:
                    gdn_square(l, 0, j)
            log_exp_tables()
            gdn_root(l, 0)
            with act.Fori(0, GH - 1) as h:
                gdn_head(l, h, u0, True)
            gdn_head(l, GH - 1, u0, False)

        def mlstm_head(l, h, u0, more):
            A = nc.scalar.activation

            def fill(h, j, u):
                act.wait_ge(unit_done, u)
                if j < 6:
                    A(m_qkv[:, j // 2, j % 2, :], bank[j % 2][:, :], ACT.Copy,
                      scale=(MT * P) ** -0.5 if j < 2 else 1.0).then_inc(m_filled.sem, 1)
                else:
                    A(m_gate[:, j % 2, :], bank[j % 2][:, :], ACT.Sigmoid).then_inc(m_filled.sem, 1)

            def refill(*js):
                for j in js if more else ():
                    fill(h + 1, j, h * 8 + (u0 + 8 + j + 1))

            if isinstance(h, int) and h == -1:
                for j in range(8):
                    fill(0, j, u0 + j + 1)
                return
            for v in range(MT):
                act.wait_ge(m_vt.sem, m_vt.n(l, h, v))
                A(m_vtok[:, :, P * v:P * v + P], bank[5 + v][:, :].rearrange("p (b t) -> p b t", b=NB),
                  ACT.Copy).then_inc(m_vt_ready.sem, 1)
            act.wait_ge(m_kq.sem, m_kq.n(l, h, 2))
            refill(0)
            log_exp_tables()
            for d in range(2):
                act.wait_ge(m_arg.sem, m_arg.n(l, h, d))
                A(m_floor[:, :], bank[6][:, :], ACT.Exp)
                for sb in range(NB):
                    for t0, t1, diagonal in reach(d, sb):
                        w = m_w[:, sb, t0:t1]
                        if diagonal:
                            last = A(w, w, ACT.Exp)
                        else:
                            last = A(w, bank[5][:, t0:t1], ACT.Exp, bias=m_col[:, d, sb:sb + 1])
                last.then_inc(m_exp.sem, 1)
                refill(*((1,) if d == 0 else (3, 4)))
                act.wait_ge(m_num.sem, m_num.n(l, h, d))
                A(m_den[:, :], bank[7][:, :], ACT.Abs).then_inc(m_abs.sem, 1)
                refill(*((2,) if d == 0 else ()))
            act.wait_ge(m_added.sem, m_added.n(l, h, 1))
            for v in range(MT):
                last = A(m_tmp[:, v, :], m_h[:, v, :], ACT.Square)
            last.then_inc(m_sq.sem, 1)
            refill(5)
            act.wait_ge(m_ss.sem, m_ss.n(l, h, 0))
            inv_root(m_den[:, :], bank[5][:, :], 1.0 / (MT * P), (l, h), (m_var, 0), m_rms)
            if more:
                act.wait_ge(m_head.sem, m_head.n(l, h, 0))
            refill(6, 7)

        def mlstm(step, l):
            u0 = first_unit[step, 0]
            mlstm_head(l, -1, u0, False)
            with act.Fori(0, MH - 1) as h:
                mlstm_head(l, h, u0, True)
            mlstm_head(l, MH - 1, u0, False)

        def attn_group(l, g, u0):
            A = nc.scalar.activation
            log_exp_tables()

            def root(j):
                act.wait_ge(t_ss.sem, t_ss.n(l, g, j))
                if j >= 2:
                    act.wait_ge(t_normed.sem, t_normed.n(l, g, j - 2))
                inv_root(t_root[:, j % 2, :], bank[3][:, :], 1.0 / P, (l, g), (t_var, j), t_rms)

            for j in range(NU):
                act.wait_ge(unit_done, u0 + j + 1)
                A(t_raw[:, j, :], bank[j % 2][:, :], ACT.Copy).then_inc(t_filled.sem, 1)
                if j != 1:
                    n = 0 if j == 0 else j - 1
                    act.wait_ge(t_filled.sem, t_filled.n(l, g, j))
                    if n >= 2:
                        act.wait_ge(t_ss.sem, t_ss.n(l, g, n - 2))
                    A(t_sq[:, n % 2, :], t_raw[:, j, :], ACT.Square).then_inc(t_sqd.sem, 1)
                if j == 1:
                    root(0)
                elif j == 2:
                    act.wait_ge(t_vt.sem, t_vt.n(l, g, 0))
                    A(t_vtok[:, :, :], bank[2][:, :].rearrange("p (b t) -> p b t", b=NB),
                      ACT.Copy).then_inc(t_vt_ready.sem, 1)
                elif j > 2:
                    root(j - 2)
            root(AG)

            def exps(n):
                b, q = divmod(n, AG)
                keys, c = (CTX if b < 2 else T), t_col[:, n % 3, :]
                k = l * S_LAYER + S_SINK + AG * g + q
                act.wait_ge(t_masked.sem, t_masked.n(l, g, n))
                A(c[:, 2:3], sml[:, k:k + 1], ACT.Exp, bias=c[:, 1:2])
                src = bank[5 + n % 2][:, 0:keys] if b < 2 else t_s[:, n % 3, :]
                A(t_s[:, n % 3, 0:keys], src, ACT.Exp, bias=c[:, 1:2], accum_out=c[:, 3:4]).then_inc(t_exp.sem, 1)

            exps(n_first(l))
            for n in range(n_first(l), NQ):
                b, q = divmod(n, AG)
                kb = 2 if b < 2 else NB
                if n + 1 < NQ:
                    exps(n + 1)
                act.wait_ge(t_pturn.sem, t_pturn.n(l, g, n))
                if b >= b_first(l) + 2:
                    act.wait_ge(t_out.sem, t_out.n(l, g, b - 2))
                A(t_pt[:, b % 2, 0:kb, P * q:P * q + P], bank[2 + n % 2][:, 0:P * kb].rearrange(
                    "p (k t) -> p k t", k=kb), ACT.Copy).then_inc(t_pcopied.sem, 1)
                if q == 2 and b > b_first(l) or n == NQ - 1:
                    for c in ([b - 1] if n < NQ - 1 else [b]):
                        act.wait_ge(t_out.sem, t_out.n(l, g, c))
                        if not (c == b_first(l) and g == 0):
                            act.wait_ge(t_osplit.sem, t_osplit.n(l, g, c - 1) if c > b_first(l)
                                        else t_osplit.n(l, g - 1, NB - 1))
                        A(t_o[:, :, :], bank[7][:, :].rearrange("p (q t) -> p q t", q=AG),
                          ACT.Copy).then_inc(t_ocopy.sem, 1)

        def attn(step, l):
            for g in range(AKV):
                attn_group(l, g, first_unit[step, g])

        def merge(step, l, p):
            u0, r = first_unit[step, 0], merge_run[step]
            with act.Fori(0, KT // 2) as i:
                for j in range(2):
                    act.wait_ge(unit_done, i * 4 + (u0 + 2 * j + 1))
                    act.wait_ge(b_done.sem, b_done.n(r, i, j - 2))
                    nc.scalar.activation(b_gate[:, j, :], bank[2 * j][:, :], ACT.Sigmoid).then_inc(b_sig.sem, 1)

        for e in (m_filled, m_vt_ready, t_filled, conv_filled):
            act.sem_inc(e.sem, e.credit)
        act.wait_ge(dma_small, 64)
        act.wait_ge(cond_zeroed.sem, cond_zeroed.n(0, 0, 0))
        silu(cond_at[:, :, ADA_M - 2:ADA_M], sml[:, S_COND:S_COND + 16].rearrange("p (k c) -> p k c", c=2)).then_inc(cond_done.sem, 1)
        act.wait_ge(mod_done.sem, 1)
        for step in STEPS:
            kind, l, p = step
            if kind == "norm":
                norm(l, p)
            elif kind == "ffn":
                ffn(step, l, p)
            elif kind == "gates":
                gates(step, l)
            elif kind == "gdn":
                gdn(step, l)
            elif kind == "mlstm":
                mlstm(step, l)
            elif kind == "attn":
                attn(step, l)
            elif kind == "merge":
                merge(step, l, p)

    @blk.vector
    def _(dve):
        step_of = Chain(dve, dve_step)
        V = nc.vector

        def modulation():
            V.memset(cond_at[:, :, :].rearrange("p k c -> p (k c)"), 0.0).then_inc(cond_zeroed.sem, 1)
            dve.wait_ge(dma_small, 64)
            step_of(V.tensor_copy(lev[:, :], lev_f[:, :]))
            for l in range(DEPTH):
                dve.wait_ge(ada_done.sem, ada_done.n(0, 0, (l + 1) * NMOD * 2 - 1))
                V.tensor_copy(ada_rows[0:ADA_M, l, :], bank[l][0:ADA_M, :]).then_inc(ada_copied.sem, 1)
            for l in range(DEPTH):
                dve.wait_ge(ada_turned.sem, ada_turned.n(0, 0, l))
                b = sml[:, l * S_LAYER + S_BADA:l * S_LAYER + S_BADA + NMOD * KT].rearrange(
                    "p (n t) -> p n t", t=4)
                for c in range(2):
                    turned = bank[2 + l][:, 0:4 * ADA_M].rearrange("p (t n c) -> p n t c", t=4, c=2)[:, :, :, c]
                    step_of(V.tensor_tensor(mod[:, l, :, :].rearrange("p (n t) c -> p n t c", t=4)[:, :, :, c],
                                            turned, b, ALU.add))
                for j in range(3):
                    w = sml[:, l * S_LAYER + S_NORM + KT * j:l * S_LAYER + S_NORM + KT * (j + 1)].unsqueeze(2)
                    step_of(V.scalar_tensor_tensor(
                        out=nscale[:, l, j, :, :], in0=mod[:, l, (3 * j + 1) * KT:(3 * j + 2) * KT, :], scalar=1.0,
                        in1=w.to_broadcast([P, KT, 2]), op0=ALU.add, op1=ALU.mult))
                    step_of(V.tensor_scalar(rgate[:, l, j, :, :], mod[:, l, (3 * j + 2) * KT:(3 * j + 3) * KT, :],
                                            1.0 if j == 1 else 0.5, None, ALU.mult))
            V.memset(eps_col[:, :], EPS).then_inc(mod_done.sem, 1)
            dve.wait_ge(mod_done.sem, 1)

        def norm(l, j):
            r = norm_run(l, j)
            dve.wait_ge(rms_done.sem, rms_done.n(r, 0, 0))
            for k in range(KT):
                V.tensor_tensor(sq[:, k, :], H[:, T * k:T * k + T], rms[:, :], ALU.mult).then_inc(nmul_done.sem, 1)
            for k in range(KT):
                dve.wait_ge(nmod_done.sem, nmod_done.n(r, 0, k))
                step_of(V.tensor_copy(xn_hi[:, k, :], sq[:, k, :]))
                V.tensor_tensor(xn_lo[:, k, :], sq[:, k, :], xn_hi[:, k, :].bitcast(F32),
                                ALU.subtract).then_inc(xn_ready.sem, 1)

        def residual(n, i, l, j, src):
            at_n = (i * 4 + n) * T
            for c, (a0, a1) in enumerate(HALVES):
                h = H[:, bass.ds(at_n + a0, a1 - a0)] if not isinstance(i, int) else H[:, at_n + a0:at_n + a1]
                last = V.scalar_tensor_tensor(out=h, in0=src[:, a0:a1], scalar=rgate[:, l, j, i * 4 + n, c:c + 1],
                                              in1=h, op0=ALU.mult, op1=ALU.add)
            return last

        def ffn(step, l, p):
            r, u0 = 2 * l + p, first_unit[step, 0]
            with step_of.turns(0, FT // 2, 4) as i:
                for j in range(2):
                    dve.wait_ge(silu_done.sem, silu_done.n(r, i, j))
                    dve.wait_ge(unit_done, i * 4 + (u0 + 2 * j + 2))
                    step_of(V.tensor_tensor(hid[:, j, :], silu_g[:, j, :], bank[2 * j + 1][:, :], ALU.mult))
                    hi = hid_hi[:, bass.ds((i * 2 + j) * T, T)]
                    lo = hid_lo[:, bass.ds((i * 2 + j) * T, T)]
                    step_of(V.tensor_copy(hi, hid[:, j, :]))
                    V.tensor_tensor(lo, hid[:, j, :], hi.bitcast(F32), ALU.subtract).then_inc(hid_ready.sem, 1)
            u0 = first_unit[step, 1]
            dve.wait_ge(hid_ready.sem, hid_ready.n(r, FT // 2 - 1, 1))
            for i in range(2):
                for n in range(4):
                    dve.wait_ge(unit_done, i * 12 + (u0 + 3 * n + 3))
                    residual(n, i, l, 2 * p, bank[4 + n % 2]).then_inc(res_done.sem, 1)
            signal_stream(l, p)

        def signal_stream(l, p):
            dve.wait_ge(res_done.sem, res_done.n(2 * l + p, 1, 3))
            for k in range(KT):
                dve.sem_inc(stream_ready.sem, 1)

        def gates(step, l):
            u0, s0 = first_unit[step, 0], l * S_LAYER

            def col(c, a0=0, a1=P):
                return sml[a0:a1, s0 + c:s0 + c + 1]

            def scan(dst, src, rows, reverse, length, reset, op0, op1, data0):
                prev = None
                for n, t0 in enumerate(range(0, T, length)):
                    if t0 % reset == 0:
                        prev = 0.0
                    cut = slice(t0, t0 + length)
                    views = [x[rows, cut][:, ::-1] if reverse else x[rows, cut] for x in (dst, data0, src)]
                    step_of(V.tensor_tensor_scan(views[0], views[1], views[2], prev, op0, op1))
                    e = t0 if reverse else t0 + length - 1
                    prev = dst[rows, e:e + 1]

            step_of(V.memset(unit_row[:, :], 1.0))
            dve.wait_ge(unit_done, u0 + 2)
            V.tensor_scalar(zed[:, :], bank[1][:, :], col(S_BB), col(S_SGN), ALU.add,
                            ALU.mult).then_inc(gate_dve.sem, 1)
            dve.wait_ge(gate_act.sem, gate_act.n(l, 0, 4))
            step_of(V.scalar_tensor_tensor(out=zed[:, :], in0=zed[:, :], scalar=0.0, in1=sofp[:, :],
                                           op0=ALU.max, op1=ALU.add))
            step_of(V.tensor_scalar(zed[:, :], zed[:, :], coef[:, 0:1], -1.0, ALU.mult, ALU.mult))
            for d in range(2):
                scan(cum, zed, slice(32 * d, 32 * d + 32), d == 1, CTX, T, ALU.mult, ALU.add, unit_row)
                scan(cum, zed, slice(64 + 32 * d, 96 + 32 * d), d == 1, P, P, ALU.mult, ALU.add, unit_row)
            step_of(V.tensor_tensor(gate_a[0:64, :], gate_a[0:64, :], cum[0:64, :], ALU.subtract))
            for d in range(2):
                scan(run_max, gate_a, slice(32 * d, 32 * d + 32), d == 1, CTX, T, ALU.max, ALU.max, gate_a)
            step_of(V.tensor_scalar(rows_m[0:64, :], run_max[0:64, :], -1.0, None, ALU.mult))
            step_of(V.tensor_copy(rows_m[64:P, :], cum[64:P, :]))
            V.scalar_tensor_tensor(out=rows_n[0:64, :], in0=cum[0:64, :], scalar=-1.0, in1=run_max[0:64, :],
                                   op0=ALU.mult, op1=ALU.subtract).then_inc(gate_dve.sem, 1)
            for j, dst in enumerate((col_a, col_g)):
                dve.wait_ge(gate_pe.sem, gate_pe.n(l, 0, j))
                c = V.tensor_copy(dst[:, :, :], bank[2 + j][:, :].rearrange("p (b t) -> p b t", b=NB))
                if j == 0:
                    step_of(c)
            c.then_inc(gate_dve.sem, 1)
            dve.wait_ge(gate_act.sem, gate_act.n(l, 0, 5))
            step_of(V.scalar_tensor_tensor(out=col_b[:, :, :], in0=col_b[:, :, :], scalar=-1.0,
                                           in1=col_a[:, :, 64:P], op0=ALU.mult, op1=ALU.mult))

        def gdn_conv_w(l, h):
            w0 = l * S_LAYER + S_CONV
            step_of(V.tensor_copy(conv_w[:, :], sml[:, bass.ds(h * (3 * CONV_K) + w0, 3 * CONV_K)]))

        def gdn_tap(l, h, n):
            j, k = divmod(n, CONV_K)
            acc = conv[:, j, :].rearrange("p (s t) -> p s t", s=2)
            tap, src = conv_w[:, n:n + 1], padded[:, j, :, k:k + CTX]
            if k == 0:
                dve.wait_ge(conv_filled.sem, conv_filled.n(l, h, j))
                if j == 2:
                    dve.wait_ge(conv_silu.sem, conv_silu.n(l, h, -1))
                step_of(V.tensor_scalar(acc, src, tap, None, ALU.mult))
            else:
                ins = V.scalar_tensor_tensor(out=acc, in0=src, scalar=tap, in1=acc, op0=ALU.mult, op1=ALU.add)
                if k < CONV_K - 1:
                    step_of(ins)
                else:
                    ins.then_inc(conv_done.sem, 1)

        def gdn_norm(l, h):
            for j in (1, 0):
                dve.wait_ge(qk_rms.sem, qk_rms.n(l, h, 1))
                V.scalar_tensor_tensor(out=qk_n[:, j, :], in0=qkv[:, j, :], scalar=P ** -0.5 if j == 0 else 1.0,
                                       in1=conv[:, j, :], op0=ALU.mult, op1=ALU.mult).then_inc(qk_ready.sem, 1)
                if j == 1:
                    for d in range(2):
                        row = h + GD_ROW[d]
                        V.tensor_copy(pick[:, d, :], con[:, bass.ds(row + C_ID, 1)].to_broadcast([P, P])).then_inc(
                            pick_ready.sem, 1)
            for d in range(2):
                row = h + GD_ROW[d]
                for j, src in enumerate((col_g[:, :, bass.ds(row, 1)], col_a[:, :, bass.ds(row, 1)],
                                         col_b[:, :, bass.ds(row - 64, 1)])):
                    step_of(V.tensor_copy(lane_col[:, d, j, :].unsqueeze(2), src))

        def gdn_head(l, h, more):
            s0 = l * S_LAYER
            q_t = qk_n[:, 0, :]

            def b4(x):
                return x.rearrange("p (b t) -> p b t", b=NB)

            def spread(x):
                return x.unsqueeze(2).to_broadcast([P, NB, P])

            for d in range(2):
                dve.wait_ge(exp_gam.sem, exp_gam.n(l, h, d))
                if d == 0:
                    dve.wait_ge(head_done.sem, head_done.n(l, h, -1))
                for b in range(NB):
                    last = V.scalar_tensor_tensor(
                        out=decay[:, d, b, :], in0=bank[4 + 2 * d][:, P * b:P * b + P],
                        scalar=lane_col[:, d, 0, b:b + 1], in1=con[:, C_MIN + P * d:C_MIN + P * d + P],
                        op0=ALU.subtract, op1=ALU.min)
                last.then_inc(arg_ready.sem, 1)
            for d in range(2):
                dve.wait_ge(kk_done.sem, kk_done.n(l, h, 0))
                dve.wait_ge(decay_done.sem, decay_done.n(l, h, d))
                V.tensor_tensor(prod[:, d, :, :], b4(bank[3][:, :]), decay[:, d, :, :], ALU.mult).then_inc(
                    l_ready.sem, 1)
            for d in range(2):
                e = chunk_end(d)
                dve.wait_ge(kk_done.sem, kk_done.n(l, h, 1))
                step_of(V.tensor_tensor(p_t[:, d, :, :], b4(bank[2][:, :]), decay[:, d, :, :], ALU.mult))
                step_of(V.tensor_copy(end_col[:, d, 0, :].unsqueeze(2), decay[:, d, :, e:e + 1]))
                step_of(V.tensor_copy(end_col[:, d, 1, :].unsqueeze(2), inv_t[:, d, :, e:e + 1]))
                step_of(V.tensor_tensor(q_dec[:, d, :, :], b4(q_t), inv_t[:, d, :, :], ALU.mult))
            for d in range(2):
                dve.wait_ge(l_turned.sem, l_turned.n(l, h, d))
                V.tensor_tensor(a_mat[:, d, :, :], b4(bank[5 + 2 * d][:, :]), spread(lane_col[:, d, 1, :]),
                                ALU.mult).then_inc(a_ready.sem, 1)
                dve.wait_ge(a_ready.sem, a_ready.n(l, h, d))
                m = lev[:, d * len(LEVELS) * P:(d * len(LEVELS) + 1) * P].unsqueeze(1).to_broadcast([P, NB, P])
                step_of(V.tensor_tensor(inv[:, d, :, :], a_mat[:, d, :, :], m, ALU.mult))
                V.tensor_tensor(inv[:, d, :, :], ident.unsqueeze(1).to_broadcast([P, NB, P]), inv[:, d, :, :],
                                ALU.subtract).then_inc(inv0_ready.sem, 1)
            for d in range(2):
                dve.wait_ge(tok_ready.sem, tok_ready.n(l, h, 1))
                step_of(V.tensor_tensor(k_end[:, d, :, :], k_tok[:, :, :], spread(end_col[:, d, 0, :]), ALU.mult))
                V.tensor_tensor(v_beta[:, d, :, :], v_tok[:, :, :], spread(lane_col[:, d, 1, :]),
                                ALU.mult).then_inc(lane_ready.sem, 1)
            if more:
                gdn_conv_w(l, h + 1)
            for j in range(2 * NL):
                v, d = divmod(j, 2)
                dve.wait_ge(corr_done.sem, corr_done.n(l, h, j))
                if j < 2:
                    dve.wait_ge(inv0_copied.sem, inv0_copied.n(l, h, d))
                if v < NL - 1:
                    V.tensor_tensor(inv[:, d, :, :], inv[:, d, :, :], b4(bank[4 + 2 * d][:, :]), ALU.subtract)
                V.tensor_tensor(inv_t[:, d, :, :], inv_t[:, d, :, :], b4(bank[5 + 2 * d][:, :]),
                                ALU.subtract).then_inc(inv_ready.sem, 1)
                for n in (2 * j, 2 * j + 1):
                    if more and n < 3 * CONV_K:
                        gdn_tap(l, h + 1, n)
            for i in range(NB):
                for d in range(2):
                    b = scan_order(d)[i]
                    if i == 0:
                        dve.wait_ge(lane_ready.sem, lane_ready.n(l, h, d))
                        V.tensor_copy(resid[:, d, :], v_beta[:, d, b, :]).then_inc(resid_ready.sem, 1)
                    else:
                        dve.wait_ge(ks_done.sem, ks_done.n(l, h, 2 * (i - 1) + d))
                        V.scalar_tensor_tensor(
                            out=resid[:, d, :], in0=bank[4 + 2 * d][:, 0:P], scalar=lane_col[:, d, 2, b:b + 1],
                            in1=v_beta[:, d, b, :], op0=ALU.mult, op1=ALU.add).then_inc(resid_ready.sem, 1)
                if i < NB - 1:
                    for d in range(2):
                        b = scan_order(d)[i]
                        dve.wait_ge(ds_done.sem, ds_done.n(l, h, 2 * i + d))
                        if i == 0:
                            V.tensor_copy(state[:, d, :], bank[4 + 2 * d][:, 2 * P:3 * P]).then_inc(
                                state_ready.sem, 1)
                        else:
                            V.scalar_tensor_tensor(
                                out=state[:, d, :], in0=state[:, d, :], scalar=end_col[:, d, 1, b:b + 1],
                                in1=bank[4 + 2 * d][:, 2 * P:3 * P], op0=ALU.mult,
                                op1=ALU.add).then_inc(state_ready.sem, 1)
            dve.wait_ge(o_done.sem, o_done.n(l, h, 1))
            dve.wait_ge(o_first.sem, o_first.n(l, h, 0))
            V.tensor_tensor(o_sum, o_sum, bank[7][:, :], ALU.add).then_inc(o_both.sem, 1)
            if more:
                gdn_norm(l, h + 1)
            dve.wait_ge(o_rms.sem, o_rms.n(l, h, 0))
            step_of(V.tensor_tensor(b4(o_sum), b4(o_sum), prod[:, 1, :, :], ALU.mult))
            dve.wait_ge(g_gate_done.sem, g_gate_done.n(l, h, 0))
            step_of(V.scalar_tensor_tensor(out=o_sum, in0=o_sum,
                                           scalar=sml[:, s0 + S_GDN:s0 + S_GDN + 1], in1=g_gate[:, :],
                                           op0=ALU.mult, op1=ALU.mult))
            hi, lo = y_hi[:, bass.ds(h * T, T)], y_lo[:, bass.ds(h * T, T)]
            step_of(V.tensor_copy(hi, o_sum))
            V.tensor_tensor(lo, o_sum, hi.bitcast(F32), ALU.subtract).then_inc(head_done.sem, 1)

        def gdn(step, l):
            V.memset(padded[:, :, :, :].rearrange("p a b c -> p (a b c)"), 0.0).then_inc(pad_zeroed.sem, 1)
            dve.wait_ge(pad_zeroed.sem, pad_zeroed.n(l, 0, 0))
            gdn_conv_w(l, 0)
            for n in range(3 * CONV_K):
                gdn_tap(l, 0, n)
            gdn_norm(l, 0)
            with step_of.turns(0, GH - 1, GDN_STEPS) as h:
                gdn_head(l, h, True)
            gdn_head(l, GH - 1, False)

        def mlstm_head(l, h, u0):
            for d in range(2):
                row = h + ML_ROW[d]
                step_of(V.tensor_copy(m_col[:, d, :].unsqueeze(2), col_a[:, :, bass.ds(row, 1)]))
                V.tensor_copy(m_pick[:, d, :], con[:, bass.ds(row + C_ID, 1)].to_broadcast([P, P])).then_inc(
                    m_picked.sem, 1)
            for d in range(2):
                dve.wait_ge(m_rows.sem, m_rows.n(l, h, d))
                for sb in range(NB):
                    cut = slice(P * sb, P * sb + P)
                    last = V.scalar_tensor_tensor(
                        out=m_w[:, sb, cut], in0=bank[5][:, cut], scalar=m_col[:, d, sb:sb + 1],
                        in1=con[:, C_MIN + P * d:C_MIN + P * d + P], op0=ALU.add, op1=ALU.min)
                last.then_inc(m_arg.sem, 1)
                dve.wait_ge(m_exp.sem, m_exp.n(l, h, d))
                dve.wait_ge(m_kq.sem, m_kq.n(l, h, 2))
                for sb in range(NB):
                    src, c0, f = kq_view(sb)
                    for t0, t1 in joined(d, sb):
                        w = m_w[:, sb, t0:t1]
                        last = V.tensor_tensor(w, src[:, c0 + t0 - f:c0 + t1 - f], w, ALU.mult)
                last.then_inc(m_weighted.sem, 1)
                dve.wait_ge(m_abs.sem, m_abs.n(l, h, d))
                step_of(V.tensor_tensor(m_den[:, :], m_den[:, :], m_floor[:, :], ALU.max))
                step_of(V.reciprocal(m_den[:, :], m_den[:, :]))
                if d == 0:
                    for v in range(MT):
                        last = V.tensor_tensor(m_h[:, v, :], bank[5 + v][:, :], m_den[:, :], ALU.mult)
                else:
                    for v in range(MT):
                        step_of(V.tensor_tensor(m_tmp[:, v, :], bank[5 + v][:, :], m_den[:, :], ALU.mult))
                        last = V.tensor_tensor(m_h[:, v, :], m_h[:, v, :], m_tmp[:, v, :], ALU.add)
                last.then_inc(m_added.sem, 1)
            dve.wait_ge(m_rms.sem, m_rms.n(l, h, 0))
            step_of(V.tensor_copy(m_wn[:, :], sml[:, bass.ds(h * MT + l * S_LAYER + S_MLN, MT)]))
            for v in range(MT):
                step_of(V.tensor_tensor(m_h[:, v, :], m_h[:, v, :], m_den[:, :], ALU.mult))
                step_of(V.scalar_tensor_tensor(out=m_h[:, v, :], in0=m_h[:, v, :], scalar=m_wn[:, v:v + 1],
                                               in1=m_gate[:, v, :], op0=ALU.mult, op1=ALU.mult))
                hi, lo = (y[:, bass.ds((h * MT + v) * T, T)] for y in (y_hi, y_lo))
                step_of(V.tensor_copy(hi, m_h[:, v, :]))
                last = V.tensor_tensor(lo, m_h[:, v, :], hi.bitcast(F32), ALU.subtract)
            last.then_inc(m_head.sem, 1)

        def mlstm(step, l):
            with step_of.turns(0, MH, MLSTM_STEPS) as h:
                mlstm_head(l, h, first_unit[step, 0])

        def attn_group(l, g, u0):
            s0 = l * S_LAYER
            step_of(V.tensor_scalar(t_w[:, 0:1], sml[:, s0 + S_QKN:s0 + S_QKN + 1], P ** -0.5, None, ALU.mult))
            step_of(V.tensor_copy(t_w[:, 1:2], sml[:, s0 + S_QKN + 1:s0 + S_QKN + 2]))
            for j in range(NU - 1):
                n = 0 if j == 0 else j + 1
                x, lat = t_raw[:, n, :], t_raw[:, n, CTX:T]
                dve.wait_ge(t_rms.sem, t_rms.n(l, g, j))
                V.scalar_tensor_tensor(out=x, in0=x, scalar=t_w[:, 1:2] if j == 0 else t_w[:, 0:1],
                                       in1=t_root[:, j % 2, :], op0=ALU.mult, op1=ALU.mult).then_inc(t_normed.sem, 1)
                dve.wait_ge(t_turned.sem, t_turned.n(l, g, j))
                step_of(V.tensor_tensor(t_rot[:, :], bank[4][:, 0:SEQ], con[:, C_SIN:C_SIN + SEQ], ALU.mult))
                step_of(V.tensor_tensor(lat, lat, con[:, C_COS:C_COS + SEQ], ALU.mult))
                V.tensor_tensor(lat, lat, t_rot[:, :], ALU.add).then_inc(t_roped.sem, 1)
            def split_o(b):
                dve.wait_ge(t_ocopy.sem, t_ocopy.n(l, g, b))
                hi, lo = (y[:, :].rearrange("p (h t) -> p h t", h=KT)[:, AG * g:AG * g + AG, P * b:P * b + P]
                          for y in (y_hi, y_lo))
                step_of(V.tensor_copy(hi, t_o[:, :, :]))
                V.tensor_tensor(lo, t_o[:, :, :], hi.bitcast(F32), ALU.subtract).then_inc(t_osplit.sem, 1)

            def row_max(n):
                b, q = divmod(n, AG)
                keys, c = (CTX if b < 2 else T), t_col[:, n % 3, :]
                x, scores = t_s[:, n % 3, 0:keys], bank[5 + n % 2]
                dve.wait_ge(t_scored.sem, t_scored.n(l, g, n))
                if n >= n_first(l) + 3:
                    dve.wait_ge(t_pturn.sem, t_pturn.n(l, g, n - 3))
                if b < 2:
                    step_of(V.tensor_reduce(c[:, 0:1], scores[:, 0:keys], AX.X, ALU.max))
                else:
                    step_of(V.tensor_copy(x[:, 0:CTX], scores[:, 0:CTX]))
                    step_of(V.tensor_tensor(x[:, CTX:T], scores[:, CTX:T],
                                            con[:, C_WIN + (b - 2) * SEQ:C_WIN + (b - 1) * SEQ], ALU.add))
                    step_of(V.tensor_reduce(c[:, 0:1], x, AX.X, ALU.max))
                k = s0 + S_SINK + AG * g + q
                V.tensor_scalar(c[:, 1:2], c[:, 0:1], sml[:, k:k + 1], -1.0, ALU.max, ALU.mult).then_inc(
                    t_masked.sem, 1)

            row_max(n_first(l))
            for n in range(n_first(l), NQ):
                b, q = divmod(n, AG)
                keys, c = (CTX if b < 2 else T), t_col[:, n % 3, :]
                if n + 1 < NQ:
                    row_max(n + 1)
                x = t_s[:, n % 3, 0:keys]
                dve.wait_ge(t_exp.sem, t_exp.n(l, g, n))
                step_of(V.tensor_tensor(c[:, 4:5], c[:, 2:3], c[:, 3:4], ALU.add))
                step_of(V.reciprocal(c[:, 5:6], c[:, 4:5]))
                V.tensor_scalar(x, x, c[:, 5:6], None, ALU.mult).then_inc(t_prob.sem, 1)
                if q == 3 and b > b_first(l):
                    split_o(b - 1)
            split_o(NB - 1)

        def attn(step, l):
            for g in range(AKV):
                attn_group(l, g, first_unit[step, g])

        def merge(step, l, p):
            u0, r = first_unit[step, 0], merge_run[step]
            opens = not any(s[0] == "merge" for s in STEPS[STEPS.index(step) - 2:STEPS.index(step)]) and                 ("gates", l, 0) in STEPS[STEPS.index(step) - 3:STEPS.index(step)]
            with step_of.turns(0, KT // 2, 0 if opens else 2) as i:
                for j in range(2):
                    dve.wait_ge(b_sig.sem, b_sig.n(r, i, j))
                    dve.wait_ge(unit_done, i * 4 + (u0 + 2 * j + 2))
                    y = y_sum[:, bass.ds((i * 2 + j) * T, T)]
                    if opens:
                        V.tensor_tensor(y, b_gate[:, j, :], bank[2 * j + 1][:, :], ALU.mult).then_inc(
                            b_done.sem, 1)
                    else:
                        step_of(V.tensor_tensor(b_tmp[:, j, :], b_gate[:, j, :], bank[2 * j + 1][:, :], ALU.mult))
                        V.tensor_tensor(y, y, b_tmp[:, j, :], ALU.add).then_inc(b_done.sem, 1)

        def project_out(step, l):
            u0 = first_unit[step, 0]
            dve.wait_ge(b_done.sem, b_done.n(max(r for s, r in merge_run.items() if s[1] == l), KT // 2 - 1, 1))
            for k in range(KT):
                cut = slice(T * k, T * k + T)
                step_of(V.tensor_copy(y_hi[:, cut], y_sum[:, cut]))
                V.tensor_tensor(y_lo[:, cut], y_sum[:, cut], y_hi[:, cut].bitcast(F32),
                                ALU.subtract).then_inc(y_split.sem, 1)
            for i in range(2):
                for n in range(4):
                    dve.wait_ge(unit_done, i * 4 + (u0 + n + 1))
                    residual(n, i, l, 1, bank[4 + n % 2]).then_inc(out_res.sem, 1)
            dve.wait_ge(out_res.sem, out_res.n(l, 1, 3))
            for k in range(KT):
                dve.sem_inc(stream_ready.sem, 1)

        modulation()
        for step in STEPS:
            kind, l, p = step
            if kind == "norm":
                norm(l, p)
            elif kind == "ffn":
                ffn(step, l, p)
            elif kind == "gates":
                gates(step, l)
            elif kind == "gdn":
                gdn(step, l)
            elif kind == "mlstm":
                mlstm(step, l)
            elif kind == "attn":
                attn(step, l)
            elif kind == "merge":
                merge(step, l, p)
            elif kind == "out":
                project_out(step, l)

    block.__exit__(None, None, None)


def _layout(**inputs):
    a = {k: np.asarray(v) for k, v in inputs.items()}
    f = np.float32
    arrays = {"tokens": np.ascontiguousarray(np.concatenate([a["ctx"][0], a["x"][0]], 0).T)}

    def tiles(v, n):
        return v.reshape(n, P).T

    small = np.zeros((P, S_ALL), f)
    for l in range(DEPTH):
        s = small[:, l * S_LAYER:(l + 1) * S_LAYER]
        s[:, S_BADA:S_BADA + NMOD * KT] = tiles(a["b_ada"][l], NMOD * KT)
        s[:, S_NORM:S_NORM + 3 * KT] = tiles(a["norm_w"][l].reshape(-1), 3 * KT)
        s[:, S_CONV:S_CONV + 3 * GH * CONV_K] = a["gdn_conv_w"][l].reshape(3, CONV_K, GH, P).transpose(
            3, 2, 0, 1).reshape(P, -1)
        s[:, S_QKN:S_QKN + 2] = a["attn_qk_norm"][l].T
        s[:, S_SINK:S_SINK + AH] = a["attn_sink"][l][None, :]
        s[:, S_MLN:S_MLN + MH * MT] = tiles(a["ml_norm_w"][l].reshape(-1), MH * MT)
        s[:, S_GDN] = a["gdn_norm_w"][l]
        s[:, S_SGN] = 1.0
        for d in range(2):
            s[ML_ROW[d]:ML_ROW[d] + MH, S_BA] = a["ml_i_bias"][l, d]
            s[ML_ROW[d]:ML_ROW[d] + MH, S_BB] = a["ml_f_bias"][l, d]
            s[ML_ROW[d]:ML_ROW[d] + MH, S_SGN] = -1.0
            s[GD_ROW[d]:GD_ROW[d] + GH, S_BB] = a["gdn_dt_bias"][l, d]
            s[GD_ROW[d]:GD_ROW[d] + GH, S_ALOG] = a["gdn_a_log"][l, d]
    for n, v in enumerate((a["c_ctx"], a["c"][0])):
        small[:, S_COND + n:S_COND + 16:2] = tiles(v, KT)
    arrays["smalls"] = small

    wg = np.zeros((DEPTH, D, 2 * P), f)
    for d in range(2):
        for t, part in enumerate((7, 8)):
            c = OFF[part] + d * MH
            wg[:, :, t * P + ML_ROW[d]:t * P + ML_ROW[d] + MH] = a["w_in"][:, :, c:c + MH]
        for t, part in enumerate((13, 14)):
            c = OFF[part] + d * GH
            wg[:, :, t * P + GD_ROW[d]:t * P + GD_ROW[d] + GH] = a["w_in"][:, :, c:c + GH]
    arrays["w_gates"] = wg
    for k, n in (("w_ada", "w_ada"), ("w_gate", "ffn_w_gate"), ("w_up", "ffn_w_up"), ("w_down", "ffn_w_down"),
                 ("w_in", "w_in"), ("w_branch", "w_branch"), ("w_out", "w_out")):
        arrays[k] = np.ascontiguousarray(a[n])

    con = np.zeros((P, C_ALL), f)
    con[:, C_ID:C_ID + P] = np.eye(P)
    con[:, C_ONE:C_ONE + P] = 1.0
    half, quarter = P // 2, P // 4
    for i in range(P):
        j = i % half
        if j < quarter:
            con[i + quarter, C_ROT + i] = -1.0
        else:
            con[i - quarter, C_ROT + i] = 1.0
    inv = (f(10000.0) ** (-np.arange(quarter, dtype=f) / f(quarter))).astype(f)
    tok = np.arange(SEQ)
    for i in range(P):
        pos = (tok // 64 if i < half else tok % 64).astype(f)
        ang = pos * inv[i % quarter]
        con[i, C_COS:C_COS + SEQ] = np.cos(ang)
        con[i, C_SIN:C_SIN + SEQ] = np.sin(ang)
    for b in range(2):
        q = b * P + np.arange(P)[:, None]
        con[:, C_WIN + b * SEQ:C_WIN + (b + 1) * SEQ] = np.where(np.abs(np.arange(SEQ)[None] - q) <= 128, 0.0, -FAR)
    s, t = np.arange(P)[:, None], np.arange(P)[None]
    con[:, C_MIN:C_MIN + P] = np.where(s <= t, 0.0, -FAR)
    con[:, C_MIN + P:C_MIN + 2 * P] = np.where(s >= t, 0.0, -FAR)
    arrays["consts"] = con
    lev = np.zeros((P, 2, len(LEVELS), P), f)
    for n, b in enumerate(LEVELS):
        m = (s // (2 * b) == t // (2 * b)) & ((s // b) % 2 == 1) & ((t // b) % 2 == 0)
        lev[:, 0, n], lev[:, 1, n] = m, m.T
    arrays["levels"] = lev.reshape(P, M_ALL)
    return arrays


_NAMES = ("tokens", "smalls", "consts", "levels", "w_ada", "w_gates", "w_gate", "w_up", "w_down", "w_in",
          "w_branch", "w_out")


def kernel(**inputs):
    import concourse.bacc as _bacc
    from concourse.bass_utils import run_bass_kernel_spmd as _run

    nc = _bacc.Bacc("TRN2", target_bir_lowering=False, num_devices=1)
    arrays = _layout(**inputs)
    args = [nc.dram_tensor(n, arrays[n].shape, mybir.dt.from_np(arrays[n].dtype), kind="ExternalInput").ap()
            for n in _NAMES]
    out = nc.dram_tensor("out", (D, SEQ), F32, kind="ExternalOutput").ap()
    trunk_kernel(nc, *args, out)
    r = _run(nc, [arrays], core_ids=[0])
    return np.ascontiguousarray(r.results[0]["out"].T)[None]
```

```python
from contextlib import contextmanager

import numpy as np
import concourse.bass as bass
from concourse import mybir

F32 = mybir.dt.float32
F32R = mybir.dt.float32r
BF16 = mybir.dt.bfloat16
ALU = mybir.AluOpType
ACT = mybir.ActivationFunctionType
AX = mybir.AxisListType

P = 128
DEPTH, D, DFF, NMOD = 2, 1024, 2816, 9
KT = D // P
FT = DFF // P
CTX, SEQ = 256, 256
T = CTX + SEQ
NB = T // P
SHARE = KT // 2
CB = CTX // P
HALVES = ((0, CTX), (CTX, T))
EPS = 1e-6
FAR = 1e30
AH, AKV, AG = 8, 2, 4
MH, MT = 4, 2
GH = 8
CONV_K = 5
SPLITS = (1024, 256, 256, 1024, 1024, 1024, 1024, 8, 8, 1024, 1024, 1024, 1024, 16, 16, 3072)
OFF = [sum(SPLITS[:i]) for i in range(len(SPLITS) + 1)]

ML_ROW = (0, 32)
GD_ROW = (64, 96)

S_BADA, S_NORM, S_CONV, S_QKN, S_SINK = 0, 72, 96, 216, 218
S_MLN, S_GDN, S_BA, S_BB, S_SGN, S_ALOG = 226, 234, 235, 236, 237, 238
S_LAYER = 240
S_COND = DEPTH * S_LAYER
S_ALL = S_COND + 16
C_ID, C_ONE, C_ROT, C_COS, C_SIN, C_WIN, C_MIN, C_LEV = 0, 128, 256, 384, 640, 896, 1408, 1664
DOWN_CUTS = ((0, 8), (8, 7), (15, 7))
LEVELS = (1, 2, 4, 8, 16, 32, 64)
C_ALL = C_LEV
ADA_M = 2 * KT
GDN_STEPS = 34
MLSTM_STEPS = 15
M_ALL = 2 * len(LEVELS) * P


class Event:

    def __init__(self, sem, per, times, credit=0, skip=0):
        self.sem, self.per, self.times, self.credit, self.skip = sem, per, times, credit, skip

    def n(self, run, turn, j):
        skip = self.skip if run == DEPTH - 1 else 0
        return turn * (self.per - skip) + (run * self.times * self.per + j + 1 - skip + self.credit)


class Chain:

    def __init__(self, eng, sem):
        self.eng, self.sem, self.count, self.turn = eng, sem, 0, None

    def __call__(self, ins):
        ins.then_inc(self.sem, 1)
        self.count += 1
        self.eng.wait_ge(self.sem, self.count if self.turn is None else self.turn + self.count)

    @contextmanager
    def turns(self, start, end, per):
        base = self.count
        with self.eng.Fori(start, end) as i:
            self.turn = (i - start) * per
            yield i
        assert self.count == base + per, (self.count - base, per)
        self.turn = None
        self.count = base + per * (end - start)


class Job:

    def __init__(self, turns, units, whole=False, shared=False):
        self.turns, self.units, self.whole, self.shared = turns, units, whole, shared


def layer_steps(l):
    return [("norm", l, 0), ("ffn", l, 0), ("norm", l, 1), ("gates", l, 0), ("gdn", l, 0), ("merge", l, 2),
            ("mlstm", l, 0), ("merge", l, 1), ("attn", l, 0), ("merge", l, 0), ("out", l, 0),
            ("norm", l, 2), ("ffn", l, 1)]


STEPS = [("ada", 0, 0)] + [s for l in range(DEPTH) for s in layer_steps(l)]

MODULATIONS = {
    ("ada", 0, 0): [(0, 0), (0, 1)], ("norm", 0, 0): [(0, 2), (0, 3), (0, 4)], ("norm", 0, 1): [(0, 5)],
    ("gates", 0, 0): [(0, 6)], ("gdn", 0, 0): [(0, 7)], ("mlstm", 0, 0): [(0, 8), (1, 0)],
    ("out", 0, 0): [(1, 1)], ("norm", 0, 2): [(1, 2)], ("norm", 1, 0): [(1, 3), (1, 4)],
    ("norm", 1, 1): [(1, 5)], ("gates", 1, 0): [(1, 6)], ("gdn", 1, 0): [(1, 7)], ("mlstm", 1, 0): [(1, 8)]}


def ada_number(l, m):
    return [v for step in STEPS for v in MODULATIONS.get(step, [])].index((l, m))


def weight_jobs(w_ada, w_gates, w_gate, w_up, w_down, w_in, w_branch, w_out):
    jobs = {}
    for step in STEPS:
        kind, l, p = step
        if kind == "ffn":
            gu = []
            for j in range(2):
                gu += [(w_gate[l, p], 0, KT, P * j, 2 * P), (w_up[l, p], 0, KT, P * j, 2 * P)]
            down = [(w_down[l, p], P * k0, kn, P * j, 4 * P) for j in range(4) for k0, kn in DOWN_CUTS]
            shared = l == DEPTH - 1 and p == 1
            jobs[step] = [Job(FT // 2, gu, shared=shared), Job(2, down, shared=shared)]
        elif kind == "gates":
            jobs[step] = [Job(1, [(w_gates[l], 0, KT, P * j, 0) for j in range(2)])]
        elif kind == "gdn":
            jobs[step] = [Job(GH, [(w_in[l], 0, KT, OFF[c], P) for c in (9, 10, 11, 12)])]
        elif kind == "mlstm":
            jobs[step] = [Job(MH, [(w_in[l], 0, KT, OFF[c] + P * t, MT * P) for c in (3, 4, 5, 6) for t in range(MT)])]
        elif kind == "attn":
            jobs[step] = [Job(1, [(w_in[l], 0, KT, OFF[1] + P * g, 0), (w_in[l], 0, KT, OFF[2] + P * g, 0)]
                              + [(w_in[l], 0, KT, OFF[0] + P * (AG * g + q), 0) for q in range(AG)])
                          for g in range(AKV)]
        elif kind == "merge":
            units = []
            for j in range(2):
                units += [(w_in[l], 0, KT, OFF[15] + p * D + P * j, 2 * P), (w_branch[l, p], 0, KT, P * j, 2 * P)]
            jobs[step] = [Job(KT // 2, units, shared=l == DEPTH - 1)]
        elif kind == "out":
            jobs[step] = [Job(2, [(w_out[l], 0, KT, P * j, 4 * P) for j in range(4)], shared=l == DEPTH - 1)]
        else:
            jobs[step] = []
        if kind in ("ada", "norm", "gates", "gdn", "mlstm", "out"):
            ada = [(w_ada[v], 0, KT, D * m + P * t, 0) for v, m in MODULATIONS.get(step, []) for t in range(KT)]
            jobs[step].insert(0 if kind == "out" else len(jobs[step]), Job(1, ada, whole=True))
    return jobs


def trunk_kernel(nc, tokens, smalls, consts, levels, w_ada, w_gates, w_gate, w_up, w_down, w_in, w_branch,
                 w_out, out, debug=None):
    jobs = weight_jobs(w_ada, w_gates, w_gate, w_up, w_down, w_in, w_branch, w_out)

    at = [nc.sbuf_base]
    top = nc.sbuf_usable_end

    def place(name, shape, dt, where=None):
        size = int(np.prod(shape[1:])) * (2 if dt == BF16 else 4)
        where = at if where is None else where
        where[0] = (where[0] + 31) // 32 * 32
        t = nc.alloc_sbuf_tensor_at(name, shape, dt, offset=where[0])
        where[0] += size
        assert where[0] <= top, (name, where[0], top)
        return t

    H = place("H", [P, KT * T], F32)
    xn_hi = place("xn_hi", [P, KT, T], F32R)
    xn_lo = place("xn_lo", [P, KT, T], F32R)
    raw = place("raw", [P, 4, KT * P], F32)
    w_whole = place("w_whole", [P, 2, KT * P], F32, list(at))
    w_hi = place("w_hi", [P, 2, KT * P], F32R)
    w_lo = place("w_lo", [P, 2, KT * P], F32R)
    con = place("con", [P, C_ALL], F32)
    lev = place("lev", [P, M_ALL], BF16)
    sml = place("sml", [P, S_ALL], F32)
    cond_at = place("cond_at", [P, KT, 2 * ADA_M - 2], F32)
    ada_rows = place("ada_rows", [P, 2, P], F32)
    mod = place("mod", [P, DEPTH, NMOD * KT, 2], F32)
    nscale = place("nscale", [P, DEPTH, 3, KT, 2], F32)
    eps_col = place("eps_col", [P, 1], F32)
    rgate = place("rgate", [P, DEPTH, 3, KT, 2], F32)
    arena = at[0]

    ident, ones, rot = con[:, C_ID:C_ID + P], con[:, C_ONE:C_ONE + P], con[:, C_ROT:C_ROT + P]

    a = [arena]
    sq = place("sq", [P, KT, T], F32, a)
    rms = place("rms", [P, T], F32, a)
    lev_f = place("lev_f", [P, M_ALL], F32, a)
    a = [arena]
    hid_hi = place("hid_hi", [P, FT * T], F32R, a)
    hid_lo = place("hid_lo", [P, FT * T], F32R, a)
    silu_g = place("silu_g", [P, 2, T], F32, a)
    hid = place("hid", [P, 2, T], F32, a)

    a = [arena]
    rows_m = place("rows_m", [P, T], F32, a)
    rows_n = place("rows_n", [P, T], F32, a)
    col_a = place("col_a", [P, NB, P], F32, a)
    col_g = place("col_g", [P, NB, P], F32, a)
    col_b = place("col_b", [P, NB, P // 2], F32, a)
    y_hi = place("y_hi", [P, KT * T], F32R, a)
    y_lo = place("y_lo", [P, KT * T], F32R, a)
    mix = a[0]
    y_sum = place("y_sum", [P, KT * T], F32, a)
    branch = a[0]
    a = [mix]
    gate_a = place("gate_a", [P, T], F32, a)
    zed = place("zed", [P, T], F32, a)
    sofp = place("sofp", [P, T], F32, a)
    cum = place("cum", [P, T], F32, a)
    unit_row = place("unit_row", [P, T], F32, a)
    run_max = place("run_max", [P, T], F32, a)
    coef = place("coef", [P, 1], F32, a)
    PAD = CONV_K // 2
    a = [mix]
    padded = place("padded", [P, 3, 2, CTX + 2 * PAD], F32, a)
    conv = place("conv", [P, 3, T], F32, a)
    qkv = place("qkv", [P, 3, T], F32, a)
    qk_n = place("qk_n", [P, 2, T], F32, a)
    g_raw = place("g_raw", [P, T], F32, a)
    g_gate = place("g_gate", [P, T], F32, a)
    k_tok = place("k_tok", [P, NB, P], F32, a)
    v_tok = place("v_tok", [P, NB, P], F32, a)
    conv_w = place("conv_w", [P, 3 * CONV_K], F32, a)
    pick = place("pick", [P, 2, P], F32, a)
    lane_col = place("lane_col", [P, 2, 3, NB], F32, a)
    end_col = place("end_col", [P, 2, 2, NB], F32, a)
    decay = place("decay", [P, 2, NB, P], F32, a)
    p_t = place("p_t", [P, 2, NB, P], F32, a)
    a_mat = place("a_mat", [P, 2, NB, P], F32, a)
    o_sum = decay[:, 0, :, :].rearrange("p b t -> p (b t)")
    inv = place("inv", [P, 2, NB, P], F32, a)
    inv_t = place("inv_t", [P, 2, NB, P], F32, a)
    prod = place("prod", [P, 2, NB, P], F32, a)
    q_dec = place("q_dec", [P, 2, NB, P], F32, a)
    k_end = place("k_end", [P, 2, NB, P], F32, a)
    v_beta = place("v_beta", [P, 2, NB, P], F32, a)
    resid = place("resid", [P, 2, P], F32, a)
    v_new = place("v_new", [P, 2, P], F32, a)
    state = place("state", [P, 2, P], F32, a)
    a = [branch]
    m_qkv = place("m_qkv", [P, 3, MT, T], F32, a)
    m_gate = place("m_gate", [P, MT, T], F32, a)
    m_vtok = place("m_vtok", [P, NB, MT * P], F32, a)
    m_w = place("m_w", [P, NB, T], F32, a)
    m_den = place("m_den", [P, T], F32, a)
    m_floor = place("m_floor", [P, T], F32, a)
    m_h = place("m_h", [P, MT, T], F32, a)
    m_tmp = place("m_tmp", [P, MT, T], F32, a)
    m_pick = place("m_pick", [P, 2, P], F32, a)
    m_wn = place("m_wn", [P, MT], F32, a)
    m_col = place("m_col", [P, 2, NB], F32, a)
    a = [branch]
    t_raw = place("t_raw", [P, 6, T], F32, a)
    t_sq = place("t_sq", [P, 2, T], F32, a)
    t_root = place("t_root", [P, 2, T], F32, a)
    t_rot = place("t_rot", [P, SEQ], F32, a)
    t_vtok = place("t_vtok", [P, NB, P], F32, a)
    t_s = place("t_s", [P, 3, T], F32, a)
    t_pt = place("t_pt", [P, 2, NB, AG * P], F32, a)
    t_o = place("t_o", [P, AG, P], F32, a)
    t_col = place("t_col", [P, 3, 6], F32, a)
    t_w = place("t_w", [P, 2], F32, a)
    a = [branch]
    b_gate = place("b_gate", [P, 2, T], F32, a)
    b_tmp = place("b_tmp", [P, 2, T], F32, a)

    bank = [nc.alloc_psum_tensor(f"bank{i}", [P, 512], F32) for i in range(8)]

    def event(name, per, times, credit=0, skip=0):
        return Event(nc.alloc_semaphore(name), per, times, credit, skip)

    sml_landed, con_landed, lev_landed, tokens_landed = (
        nc.alloc_semaphore(n) for n in ("sml_landed", "con_landed", "lev_landed", "tokens_landed"))
    raw_landed = [nc.alloc_semaphore(f"raw_landed{j}") for j in range(4)]
    hi_done = nc.alloc_semaphore("hi_done")
    split_done = nc.alloc_semaphore("split_done")
    share_done = nc.alloc_semaphore("share_done")
    unit_done = nc.alloc_semaphore("unit_done")
    out_done = nc.alloc_semaphore("out_done")
    ada_copied = event("ada_copied", NMOD, DEPTH)
    ada_turned = event("ada_turned", NMOD, DEPTH)
    mod_ready = event("mod_ready", NMOD, DEPTH)
    cond_zeroed = event("cond_zeroed", 1, 1)
    cond_done = event("cond_done", 1, 1)
    eps_set = event("eps_set", 1, 1)
    dve_step, pool_turn, sp_turn = (nc.alloc_semaphore(n) for n in ("dve_step", "pool_turn", "sp_turn"))

    sq_done = event("sq_done", KT, 1)
    ss_done = event("ss_done", 1, 1)
    rvar_done = event("rvar_done", 1, 1)
    rms_done = event("rms_done", 1, 1)
    nmul_done = event("nmul_done", KT, 1)
    nmod_done = event("nmod_done", KT, 1)
    xn_ready = event("xn_ready", KT, 1)
    stream_ready = event("stream_ready", KT, 1)
    silu_done = event("silu_done", 2, FT // 2)
    hid_ready = event("hid_ready", 2, FT // 2, credit=2)
    res_done = event("res_done", 4, 2, credit=2)

    gate_act = event("gate_act", 6, 1)
    gate_dve = event("gate_dve", 3, 1)
    gate_pe = event("gate_pe", 2, 1)
    pad_zeroed = event("pad_zeroed", 1, 1)
    conv_filled = event("conv_filled", 3, GH, credit=1)
    conv_done = event("conv_done", 3, GH, credit=3)
    conv_silu = event("conv_silu", 3, GH)
    g_filled = event("g_filled", 1, GH)
    g_gate_done = event("g_gate_done", 1, GH)
    qk_sq = event("qk_sq", 2, GH)
    qk_ss = event("qk_ss", 2, GH)
    qk_var = event("qk_var", 2, GH)
    qk_rms = event("qk_rms", 2, GH)
    qk_ready = event("qk_ready", 2, GH)
    tok_t = event("tok_t", 2, GH)
    tok_ready = event("tok_ready", 2, GH)
    kk_done = event("kk_done", 2, GH)
    pick_ready = event("pick_ready", 2, GH)
    gam_row = event("gam_row", 2, GH)
    exp_gam = event("exp_gam", 2, GH)
    arg_ready = event("arg_ready", 2, GH)
    decay_done = event("decay_done", 2, GH)
    l_ready = event("l_ready", 2, GH)
    l_turned = event("l_turned", 2, GH)
    a_ready = event("a_ready", 2, GH)
    inv0_ready = event("inv0_ready", 2, GH)
    inv0_turned = event("inv0_turned", 2, GH)
    inv0_copied = event("inv0_copied", 2, GH)
    NL = len(LEVELS) - 1
    block_ready = event("block_ready", 2 * NL, GH)
    prod_done = event("prod_done", 2 * NL, GH)
    prod_ready = event("prod_ready", 2 * NL, GH)
    corr_done = event("corr_done", 2 * NL, GH)
    inv_t_ready = event("inv_t_ready", 2 * NL, GH)
    inv_turned = event("inv_turned", 2 * (NL - 1), GH)
    inv_ready = event("inv_ready", 2 * (NL - 1), GH)
    lane_ready = event("lane_ready", 2, GH)
    ks_done = event("ks_done", 2 * (NB - 1), GH)
    resid_ready = event("resid_ready", 2 * NB, GH)
    v_new_done = event("v_new_done", 2 * NB, GH)
    v_new_ready = event("v_new_ready", 2 * NB, GH)
    ds_done = event("ds_done", 2 * (NB - 1), GH)
    state_ready = event("state_ready", 2 * (NB - 1), GH)
    o_done = event("o_done", 2, GH)
    o_first = event("o_first", 1, GH)
    o_both = event("o_both", 1, GH)
    o_sq = event("o_sq", 1, GH)
    o_ss = event("o_ss", 1, GH)
    o_var = event("o_var", 1, GH, credit=1)
    o_rms = event("o_rms", 1, GH)
    head_done = event("head_done", 1, GH, credit=1)
    m_filled = event("m_filled", 8, MH, credit=8)
    m_vt = event("m_vt", MT, MH)
    m_vt_ready = event("m_vt_ready", MT, MH, credit=MT)
    m_picked = event("m_picked", 2, MH)
    m_kq = event("m_kq", 3, MH)
    m_rows = event("m_rows", 2, MH)
    m_arg = event("m_arg", 2, MH)
    m_exp = event("m_exp", 2, MH)
    m_weighted = event("m_weighted", 2, MH)
    m_num = event("m_num", 2, MH)
    m_abs = event("m_abs", 2, MH)
    m_added = event("m_added", 2, MH, credit=2)
    m_sq = event("m_sq", 1, MH)
    m_ss = event("m_ss", 1, MH)
    m_var = event("m_var", 1, MH)
    m_rms = event("m_rms", 1, MH)
    m_head = event("m_head", 1, MH, credit=1)
    NU = 2 + AG
    t_filled = event("t_filled", NU, AKV, credit=NU)
    t_sqd = event("t_sqd", NU - 1, AKV)
    t_ss = event("t_ss", NU - 1, AKV)
    t_var = event("t_var", NU - 1, AKV)
    t_rms = event("t_rms", NU - 1, AKV)
    t_normed = event("t_normed", NU - 1, AKV)
    t_turned = event("t_turned", NU - 1, AKV)
    t_roped = event("t_roped", NU - 1, AKV)
    t_vt = event("t_vt", 1, AKV)
    t_vt_ready = event("t_vt_ready", 1, AKV)
    NQ = NB * AG
    t_scored = event("t_scored", NQ, AKV, skip=AG * CB)
    t_masked = event("t_masked", NQ, AKV, skip=AG * CB)
    t_exp = event("t_exp", NQ, AKV, skip=AG * CB)
    t_prob = event("t_prob", NQ, AKV, skip=AG * CB)
    t_pturn = event("t_pturn", NQ, AKV, skip=AG * CB)
    t_pcopied = event("t_pcopied", NQ, AKV, skip=AG * CB)
    t_out = event("t_out", NB, AKV, skip=CB)
    t_ocopy = event("t_ocopy", NB, AKV, skip=CB)
    t_osplit = event("t_osplit", NB, AKV, skip=CB)
    b_sig = event("b_sig", 2, KT // 2)
    b_done = event("b_done", 2, KT // 2, credit=2)
    y_split = event("y_split", KT, 1)
    out_res = event("out_res", 4, 2, credit=2)
    credits = (o_var, out_res, m_added, m_head, hid_ready, res_done, conv_done, head_done, b_done)

    def first_token(l, step=None):
        if step is not None and (step[0] == "ffn" and step[2] == 0 or step[0] == "norm" and step[2] < 2):
            return 0
        return CTX if l == DEPTH - 1 else 0

    def b_first(l):
        return first_token(l) // P

    def n_first(l):
        return AG * b_first(l)

    def scan_order(d):
        return (0, 1, 2, 3) if d == 0 else (1, 0, 3, 2)

    def chunk_end(d):
        return P - 1 if d == 0 else 0

    merge_run = {s: n for n, s in enumerate(s for s in STEPS if s[0] == "merge")}

    def branch_whole(l, p):
        if p == 2:
            return head_done.sem, head_done.n(l, GH - 1, 0)
        if p == 1:
            return m_head.sem, m_head.n(l, MH - 1, 0)
        return t_osplit.sem, t_osplit.n(l, AKV - 1, NB - 1)

    def reach(d, sb, f0):
        t0, t1 = P * sb, P * sb + P
        spans = [(t0, t1, True)]
        if d == 0:
            spans += [(t1, T, False)] if t1 < T else []
        else:
            lo = 0 if t0 < CTX else CTX
            spans += [(lo, t0, False)] if lo < t0 else []
            spans += [(CTX, T, False)] if t0 < CTX else []
        return [(max(a0, f0), a1, diagonal) for a0, a1, diagonal in spans if a1 > f0]

    def joined(d, sb, f0):
        out = []
        for t0, t1, _ in sorted(reach(d, sb, f0)):
            if out and out[-1][1] == t0:
                out[-1] = (out[-1][0], t1)
            else:
                out.append((t0, t1))
        return out

    def by_reach(d):
        return (0, 1, 2, 3) if d == 0 else (1, 0, 3, 2)

    def kq_view(sb):
        return (bank[2 + sb], 0, 0) if sb < 2 else (bank[4], CTX * (sb - 2), CTX)

    block = nc.Block()
    blk = block.__enter__()

    first_unit, is_shared = {}, []
    for step in STEPS:
        for n, job in enumerate(jobs[step]):
            first_unit[step, n] = len(is_shared)
            is_shared += [job.shared] * (job.turns * len(job.units))

    def shared_by(u):
        return sum(is_shared[:u + 1])

    ADA_BANKS = (bank[6], bank[5])

    def ada_job(step):
        return [job.whole for job in jobs[step]].index(True)

    def ada_pairs(step):
        return range((len(MODULATIONS.get(step, [])) + 1) // 2)

    def ada_pair(step, pair):
        return range(2 * pair, min(2 * pair + 2, len(MODULATIONS.get(step, []))))

    def ada_first(step):
        return sum(len(MODULATIONS.get(s, [])) for s in STEPS[:STEPS.index(step)])

    def norm_run(l, j):
        return 3 * l + j

    @blk.sync
    def _(sp):
        sp.dma_start(sml[:, :], smalls).then_inc(sml_landed, 16)
        sp.dma_start(con[:, :], consts).then_inc(con_landed, 16)

        def load(u, turn_units, i, unit):
            w, row, kn, col, step = unit
            if not isinstance(i, int) or u + turn_units * i >= 4:
                sp.wait_ge(split_done, turn_units * i + (u - 3))
                if isinstance(i, int):
                    if is_shared[u + turn_units * i - 4]:
                        sp.wait_ge(share_done, shared_by(u + turn_units * i - 4))
                elif is_shared[u]:
                    sp.sem_inc(sp_turn, 1)
                    sp.wait_ge(share_done, turn_units * i + (shared_by(u - 4 + turn_units) - turn_units))
                if not isinstance(i, int):
                    sp.sem_inc(sp_turn, 1)
            src = w[row:row + P * kn, bass.ds(i * step + col, P)] if not isinstance(i, int) else \
                w[row:row + P * kn, i * step + col:i * step + col + P]
            sp.dma_start(raw[:, u % 4, 0:kn * P].rearrange("p (k n) -> p k n", k=kn),
                         src.rearrange("(k p) n -> p k n", p=P)).then_inc(raw_landed[u % 4], 16)

        for step in STEPS:
            if step == STEPS[1]:
                sp.dma_start(H[:, :].rearrange("p (k t) -> p k t", k=KT),
                             tokens.rearrange("(k p) t -> p k t", p=P)).then_inc(tokens_landed, 16)
                sp.dma_start(lev_f[:, :], levels).then_inc(lev_landed, 16)
            for n, job in enumerate(jobs[step]):
                u0, m = first_unit[step, n], len(job.units)
                start = 0
                if job.turns == 1 or u0 < 4 or job.shared or any(is_shared[u0 - 4:u0]):
                    for j, unit in enumerate(job.units):
                        load(u0 + j, m, 0, unit)
                    start = 1
                if start < job.turns:
                    with sp.Fori(start, job.turns) as i:
                        for j, unit in enumerate(job.units):
                            load(u0 + j, m, i, unit)
        sp.wait_ge(stream_ready.sem, stream_ready.n(len([s for s in STEPS if s[0] == "norm"]) - 1, 0, KT - 1))
        sp.dma_start(out.rearrange("(k p) t -> p k t", p=P),
                     H[:, :].rearrange("p (k t) -> p k t", k=KT)[:, :, CTX:T]).then_inc(out_done, 16)
        sp.wait_ge(out_done, 16)

    @blk.gpsimd
    def _(pool):
        def split(u, turn_units, i, kn):
            n = kn * P
            n_low = SHARE * P if is_shared[u] else n
            pool.wait_ge(raw_landed[u % 4], i * (4 * turn_units) + (16 * (u // 4) + 16))
            if not isinstance(i, int) or u + turn_units * i >= 2:
                pool.wait_ge(unit_done, turn_units * i + (u - 1))
            if not isinstance(i, int):
                pool.sem_inc(pool_turn, 1)
            nc.gpsimd.tensor_scalar(w_hi[:, u % 2, 0:n], raw[:, u % 4, 0:n], 1.0, 1.0, ALU.mult,
                                    ALU.mult).then_inc(hi_done, 1)
            pool.wait_ge(hi_done, turn_units * i + (u + 1))
            nc.gpsimd.tensor_tensor(w_lo[:, u % 2, 0:n_low], raw[:, u % 4, 0:n_low],
                                    w_hi[:, u % 2, 0:n_low].bitcast(F32),
                                    ALU.subtract).then_inc(split_done, 1)

        def pass_on(u):
            pool.wait_ge(raw_landed[u % 4], 16 * (u // 4) + 16)
            if u >= 2:
                pool.wait_ge(unit_done, u - 1)
            nc.gpsimd.tensor_scalar(w_whole[:, u % 2, :], raw[:, u % 4, :], 1.0, 1.0, ALU.mult,
                                    ALU.mult).then_inc(hi_done, 1)
            pool.wait_ge(hi_done, u + 1)
            pool.sem_inc(split_done, 1)

        def split_job(step, n, start=0):
            job, u0 = jobs[step][n], first_unit[step, n]
            m = len(job.units)
            if job.whole:
                for j in range(m):
                    pass_on(u0 + j)
                return
            if job.turns == 1 or u0 < 2:
                for j, unit in enumerate(job.units):
                    split(u0 + j, m, 0, unit[2])
                start = 1
            if start < job.turns:
                with pool.Fori(start, job.turns) as i:
                    for j, unit in enumerate(job.units):
                        split(u0 + j, m, i, unit[2])

        def level_blocks(l, h, levels):
            for v in levels:
                for d in range(2):
                    j = 2 * v + d
                    if v == 0:
                        pool.wait_ge(inv0_ready.sem, inv0_ready.n(l, h, d))
                    else:
                        pool.wait_ge(prod_done.sem, prod_done.n(l, h, j - 2))
                    m = lev[:, (d * len(LEVELS) + v + 1) * P:(d * len(LEVELS) + v + 2) * P].unsqueeze(1)
                    nc.gpsimd.tensor_tensor(decay[:, d, :, :], a_mat[:, d, :, :], m.to_broadcast([P, NB, P]),
                                            ALU.mult).then_inc(block_ready.sem, 1)

        for e in credits:
            if e.credit:
                pool.sem_inc(e.sem, e.credit)
        for step in STEPS:
            kind, l, p = step
            if kind == "gdn":
                u0 = first_unit[step, 0]
                for j in range(4):
                    split(u0 + j, 4, 0, KT)
                with pool.Fori(0, GH - 1) as h:
                    for j in range(3):
                        split(u0 + 4 + j, 4, h, KT)
                    level_blocks(l, h, (0,))
                    split(u0 + 7, 4, h, KT)
                    level_blocks(l, h, range(1, NL))
                split_job(step, 1)
                level_blocks(l, GH - 1, range(NL))
            else:
                for n in range(len(jobs[step])):
                    split_job(step, n)

    @blk.tensor
    def _(pe):
        mm = nc.tensor.matmul

        def unit(u, i, m, kn, dst, hi, lo, start=True, stop=True, rows=None):
            rows = range(kn) if rows is None else rows
            if rows[0] == 0:
                pe.wait_ge(split_done, m * i + (u + 1))
                if is_shared[u]:
                    pe.wait_ge(share_done, m * i + shared_by(u))
            for k in rows:
                wh, wl = w_hi[:, u % 2, P * k:P * k + P], w_lo[:, u % 2, P * k:P * k + P]
                mm(dst, wh, hi(k), start=start and k == 0, stop=False)
                mm(dst, wh, lo(k), start=False, stop=False)
                last = mm(dst, wl, hi(k), start=False, stop=stop and k == kn - 1)
            if rows[-1] == kn - 1:
                last.then_inc(unit_done, 1)

        def split_tiles(hi, lo, t0):
            def view(x, k):
                return x[:, k, t0:T] if len(x.shape) == 3 else x[:, T * k + t0:T * k + T]
            return (lambda k: view(hi, k)), (lambda k: view(lo, k))

        xh, xl = split_tiles(xn_hi, xn_lo, 0)

        def ada_unit(step, n, dst):
            if not jobs[step][ada_job(step)].units:
                return
            u, t = first_unit[step, ada_job(step)] + n, n % KT
            number = ada_first(step) + n // KT
            if t == 0 and number > 0:
                pe.wait_ge(mod_ready.sem, number - n // KT % 2)
            pe.wait_ge(split_done, u + 1)
            for k in range(KT):
                last = mm(dst[0:ADA_M, 0:P], cond_at[:, k, ADA_M - 2 - 2 * t:2 * ADA_M - 2 - 2 * t],
                          w_whole[:, u % 2, P * k:P * k + P], start=t == 0 and k == 0,
                          stop=t == KT - 1 and k == KT - 1)
            last.then_inc(unit_done, 1)

        def ada_turn(step, banks, pair=0):
            for n in ada_pair(step, pair):
                number = ada_first(step) + n
                pe.wait_ge(ada_copied.sem, number + 1)
                nc.tensor.transpose(banks[n % len(banks)][:, P:P + ADA_M], ada_rows[0:ADA_M, n % 2, :],
                                    ident[0:ADA_M, 0:ADA_M]).then_inc(ada_turned.sem, 1)

        def ada(step, banks):
            for pair in ada_pairs(step):
                for v in ada_pair(step, pair):
                    for n in range(KT * v, KT * v + KT):
                        ada_unit(step, n, banks[v % 2])
                ada_turn(step, banks, pair)

        def norm(l, j):
            r, f0 = norm_run(l, j), first_token(l, ("norm", l, j))
            for k in range(KT):
                pe.wait_ge(sq_done.sem, sq_done.n(r, 0, k))
                last = mm(bank[7][:, f0:T], ones, sq[:, k, f0:T], start=k == 0, stop=k == KT - 1)
            last.then_inc(ss_done.sem, 1)
            ada(("norm", l, j), ADA_BANKS)

        def ffn(step, l, p):
            r, f0 = 2 * l + p, first_token(l, step)
            xh, xl = split_tiles(xn_hi, xn_lo, f0)
            hh, hl = split_tiles(hid_hi, hid_lo, f0)
            u0, nr = first_unit[step, 0], norm_run(l, 2 * p)
            with pe.Fori(0, FT // 2) as i:
                for j in range(2):
                    pe.wait_ge(hid_ready.sem, hid_ready.n(r, i, j - 2))
                    if j == 0:
                        for k in range(KT):
                            pe.wait_ge(xn_ready.sem, xn_ready.n(nr, 0, k))
                            unit(u0, i, 4, KT, bank[0][:, f0:T], xh, xl, rows=(k,))
                    else:
                        unit(u0 + 2, i, 4, KT, bank[2][:, f0:T], xh, xl)
                    unit(u0 + 2 * j + 1, i, 4, KT, bank[2 * j + 1][:, f0:T], xh, xl)
            u0 = first_unit[step, 1]
            pe.wait_ge(hid_ready.sem, hid_ready.n(r, FT // 2 - 1, 1))
            with pe.Fori(0, 2) as i:
                for j in range(4):
                    pe.wait_ge(res_done.sem, res_done.n(r, i, j - 2))
                    for c, (k0, kn) in enumerate(DOWN_CUTS):
                        unit(u0 + 3 * j + c, i, 12, kn, bank[4 + j % 2][:, f0:T],
                             lambda k: hh(k0 + k), lambda k: hl(k0 + k),
                             start=c == 0, stop=c == 2)

        def gates(step, l):
            u0 = first_unit[step, 0]
            for k in range(KT):
                pe.wait_ge(xn_ready.sem, xn_ready.n(norm_run(l, 1), 0, k))
                unit(u0, 0, 2, KT, bank[0][:, :], xh, xl, rows=(k,))
            unit(u0 + 1, 0, 2, KT, bank[1][:, :], xh, xl)
            for n in range(KT):
                ada_unit(step, n, bank[6])
            u1 = first_unit[("gdn", l, 0), 0]
            pe.wait_ge(gate_act.sem, gate_act.n(l, 0, 0))
            gdn_project(l, 0, 0, u1, 0)
            pe.wait_ge(gate_dve.sem, gate_dve.n(l, 0, 0))
            gdn_project(l, 0, 1, u1, 0)
            pe.wait_ge(gate_dve.sem, gate_dve.n(l, 0, 1))
            for b in range(NB):
                last = nc.tensor.transpose(bank[2][:, P * b:P * b + P], gate_a[:, P * b:P * b + P], ident)
            last.then_inc(gate_pe.sem, 1)
            for b in range(NB):
                last = nc.tensor.transpose(bank[3][:, P * b:P * b + P], rows_m[:, P * b:P * b + P], ident)
            last.then_inc(gate_pe.sem, 1)
            ada_turn(step, (bank[6],))

        def gdn_project(l, h, j, u, i, rows=range(KT)):
            if rows[0] == 0:
                if j == 0:
                    pe.wait_ge(conv_filled.sem, conv_filled.n(l, h, -1))
                elif j == 1:
                    pe.wait_ge(g_filled.sem, g_filled.n(l, h, -1))
                else:
                    pe.wait_ge(conv_filled.sem, conv_filled.n(l, h, j - 2))
            f0 = 0 if j in (1, 2) else first_token(l)
            unit(u + j, i, 4, KT, bank[j % 2][:, f0:T], *split_tiles(xn_hi, xn_lo, f0), rows=rows)

        def gdn_squares(l, h):
            for j in range(2):
                pe.wait_ge(qk_sq.sem, qk_sq.n(l, h, j))
                f0 = first_token(l) if j == 0 else 0
                mm(bank[2 + j][:, f0:T], ones, conv[:, j, f0:T], start=True, stop=True).then_inc(qk_ss.sem, 1)

        def gdn_head(l, h, u0, more):
            q_t, k_t, v_t = qk_n[:, 0, :], qk_n[:, 1, :], qkv[:, 2, :]

            def blocks(b):
                return slice(P * b, P * b + P)

            step = ("gdn", l, 0)

            def project(j, k0, k1):
                if more:
                    gdn_project(l, h + 1, j, u0 + 4, h, range(k0, k1))
                elif j < 2:
                    for n in range(*{(0, 0): (0, 3), (0, 6): (3, 4), (1, 0): (4, 8)}[j, k0]):
                        if n == 0:
                            pe.wait_ge(conv_filled.sem, conv_filled.n(l, h, 2))
                        ada_unit(step, n, bank[0])

            pe.wait_ge(qk_ready.sem, qk_ready.n(l, h, 0))
            for b in range(NB):
                last = nc.tensor.transpose(bank[3][:, blocks(b)], k_t[:, blocks(b)], ident)
            last.then_inc(tok_t.sem, 1)
            for d in range(2):
                pe.wait_ge(pick_ready.sem, pick_ready.n(l, h, d))
                mm(bank[4 + 2 * d][:, :], pick[:, d, :], rows_m[:, :], start=True,
                   stop=True).then_inc(gam_row.sem, 1)
            pe.wait_ge(o_var.sem, o_var.n(l, h, -1))
            pe.wait_ge(conv_silu.sem, conv_silu.n(l, h, 2))
            for b in range(NB):
                last = nc.tensor.transpose(bank[2][:, blocks(b)], v_t[:, blocks(b)], ident)
            last.then_inc(tok_t.sem, 1)
            pe.wait_ge(qk_ready.sem, qk_ready.n(l, h, 1))
            for j, x in enumerate((k_t, q_t)):
                pe.wait_ge(tok_ready.sem, tok_ready.n(l, h, j))
                for b in range(b_first(l) if j == 1 else 0, NB):
                    last = mm(bank[3 - j][:, blocks(b)], k_t[:, blocks(b)], x[:, blocks(b)], start=True, stop=True)
                last.then_inc(kk_done.sem, 1)
                if j == 0:
                    project(0, 0, 6)
            for d in range(2):
                pe.wait_ge(l_ready.sem, l_ready.n(l, h, d))
                for b in range(NB):
                    last = nc.tensor.transpose(bank[5 + 2 * d][:, blocks(b)], prod[:, d, b, :], ident)
                last.then_inc(l_turned.sem, 1)
            project(0, 6, KT)
            project(1, 0, KT)
            for d in range(2):
                pe.wait_ge(inv0_ready.sem, inv0_ready.n(l, h, d))
                for b in range(NB):
                    last = nc.tensor.transpose(bank[4 + 2 * d][:, blocks(b)], inv[:, d, b, :], ident)
                last.then_inc(inv0_turned.sem, 1)
            for v in range(NL):
                for d in range(2):
                    j = 2 * v + d
                    if v == 0:
                        pe.wait_ge(inv0_copied.sem, inv0_copied.n(l, h, d))
                    else:
                        pe.wait_ge(inv_t_ready.sem, inv_t_ready.n(l, h, j - 2))
                        if v == NL - 1 and more:
                            pe.wait_ge(qk_var.sem, qk_var.n(l, h + 1, d))
                        for b in range(NB):
                            last = nc.tensor.transpose(bank[2 + d][:, blocks(b)], inv_t[:, d, b, :], ident)
                        last.then_inc(inv_turned.sem, 1)
                    pe.wait_ge(block_ready.sem, block_ready.n(l, h, j))
                    for b in range(NB):
                        last = mm(bank[4 + 2 * d][:, blocks(b)], decay[:, d, b, :], inv_t[:, d, b, :],
                                  start=True, stop=True)
                    last.then_inc(prod_done.sem, 1)
                if v == 0:
                    project(2, 0, 4)
                elif v == NL - 2 and more:
                    project(3, 0, 2)
                    pe.wait_ge(inv_ready.sem, inv_ready.n(l, h, 2 * v - 1))
                    gdn_squares(l, h + 1)
                for d in range(2):
                    j = 2 * v + d
                    pe.wait_ge(prod_ready.sem, prod_ready.n(l, h, j))
                    if v > 0:
                        pe.wait_ge(inv_ready.sem, inv_ready.n(l, h, j - 2))
                    for b in range(NB):
                        last = mm(bank[5 + 2 * d][:, blocks(b)], inv[:, d, b, :], prod[:, d, b, :],
                                  start=True, stop=True)
                    last.then_inc(corr_done.sem, 1)
                if v == 0:
                    project(2, 4, KT)
            for i in range(NB):
                for d in range(2):
                    b = scan_order(d)[i]
                    if i == 0 and d == 0:
                        pe.wait_ge(inv_t_ready.sem, inv_t_ready.n(l, h, 2 * NL - 1))
                        pe.wait_ge(lane_ready.sem, lane_ready.n(l, h, 1))
                    elif i > 0:
                        pe.wait_ge(state_ready.sem, state_ready.n(l, h, 2 * (i - 1) + d))
                        mm(bank[4 + 2 * d][:, 0:P], k_t[:, blocks(b)], state[:, d, :], start=True,
                           stop=True).then_inc(ks_done.sem, 1)
                project(3, i + 2, i + 3)
                for d in range(2):
                    b = scan_order(d)[i]
                    if i > 0 and b >= b_first(l):
                        mm(bank[5 + 2 * d][:, blocks(b)], state[:, d, :], q_dec[:, d, b, :], start=True, stop=False)
                    pe.wait_ge(resid_ready.sem, resid_ready.n(l, h, 2 * i + d))
                    mm(bank[4 + 2 * d][:, P:2 * P], inv_t[:, d, b, :], resid[:, d, :], start=True,
                       stop=True).then_inc(v_new_done.sem, 1)
                for d in range(2):
                    b = scan_order(d)[i]
                    pe.wait_ge(v_new_ready.sem, v_new_ready.n(l, h, 2 * i + d))
                    if i < NB - 1:
                        mm(bank[4 + 2 * d][:, 2 * P:3 * P], k_end[:, d, b, :], v_new[:, d, :], start=True,
                           stop=True).then_inc(ds_done.sem, 1)
                    if b >= b_first(l):
                        last = mm(bank[5 + 2 * d][:, blocks(b)], v_new[:, d, :], p_t[:, d, b, :], start=i == 0,
                                  stop=True)
                    if i == NB - 1:
                        last.then_inc(o_done.sem, 1)
            project(3, NB + 2, KT)
            if not more:
                ada_turn(step, (bank[0],))
            pe.wait_ge(o_sq.sem, o_sq.n(l, h, 0))
            f0 = first_token(l)
            mm(bank[2][:, f0:T], ones, prod[:, 0, b_first(l):, :].rearrange("p b t -> p (b t)"), start=True,
               stop=True).then_inc(o_ss.sem, 1)

        def gdn(step, l):
            u0 = first_unit[step, 0]
            for j in (2, 3):
                gdn_project(l, 0, j, u0, 0)
            pe.wait_ge(gate_dve.sem, gate_dve.n(l, 0, 2))
            gdn_squares(l, 0)
            pe.wait_ge(mod_ready.sem, ada_first(("gdn", l, 0)))
            with pe.Fori(0, GH - 1) as h:
                gdn_head(l, h, u0, True)
            gdn_head(l, GH - 1, u0, False)

        def mlstm_project(l, h, j, u0, m=8):
            pe.wait_ge(m_filled.sem, m_filled.n(l, h, j - 2))
            f0 = 0 if 2 <= j < 6 else first_token(l)
            unit(u0 + j, h, m, KT, bank[j % 2][:, f0:T], *split_tiles(xn_hi, xn_lo, f0))

        def mlstm_head(l, h, u0, more):
            step = ("mlstm", l, 0)

            def project(*js):
                if not more:
                    for n in range(*{(0,): (0, 3), (1,): (3, 5), (2,): (5, 8), (3, 4): (8, 11), (5, 6): (11, 16),
                                     (7,): (16, 16)}[js]):
                        if n == 0:
                            pe.wait_ge(m_filled.sem, m_filled.n(l, h, 7))
                        if n < KT * len(MODULATIONS.get(step, [])):
                            ada_unit(step, n, bank[n // KT])
                for j in js if more else ():
                    pe.wait_ge(m_filled.sem, m_filled.n(l, h + 1, j - 2))
                    f = 0 if 2 <= j < 6 else f0
                    unit(u0 + 8 + j, h, 8, KT, bank[j % 2][:, f:T], *split_tiles(xn_hi, xn_lo, f))

            f0 = first_token(l)

            pe.wait_ge(m_filled.sem, m_filled.n(l, h, 5))
            pe.wait_ge(m_head.sem, m_head.n(l, h, -1))
            for v in range(MT):
                for b in range(NB):
                    last = nc.tensor.transpose(bank[5 + v][:, P * b:P * b + P],
                                               m_qkv[:, 2, v, P * b:P * b + P], ident)
                last.then_inc(m_vt.sem, 1)
            for sb in range(NB):
                dst, c0, f = kq_view(sb)
                t0 = max(f, f0)
                for v in range(MT):
                    last = mm(dst[:, c0 + t0 - f:c0 + T - f], m_qkv[:, 1, v, P * sb:P * sb + P], m_qkv[:, 0, v, t0:T],
                              start=v == 0, stop=v == MT - 1)
                if sb != 2:
                    last.then_inc(m_kq.sem, 1)
            project(0)
            for d in range(2):
                pe.wait_ge(m_picked.sem, m_picked.n(l, h, d))
                if d == 0:
                    pe.wait_ge(m_vt_ready.sem, m_vt_ready.n(l, h, MT - 1))
                else:
                    pe.wait_ge(m_added.sem, m_added.n(l, h, 0))
                mm(bank[5][:, f0:T], m_pick[:, d, :], rows_m[:, f0:T], start=True, stop=True)
                mm(bank[6][:, f0:T], m_pick[0:64, d, :], rows_n[0:64, f0:T], start=True, stop=True).then_inc(m_rows.sem, 1)
                project(*((1,) if d == 0 else (3, 4)))
                pe.wait_ge(m_weighted.sem, m_weighted.n(l, h, d))
                for n in range(1 + MT):
                    dst = bank[7] if n == 0 else bank[4 + n]
                    for i, sb in enumerate(by_reach(d)):
                        w = ones if n == 0 else m_vtok[:, sb, P * (n - 1):P * n]
                        for c0, c1 in joined(d, sb, f0):
                            last = mm(dst[:, c0:c1], w, m_w[:, sb, c0:c1], start=i == 0, stop=i == NB - 1)
                last.then_inc(m_num.sem, 1)
                project(*((2,) if d == 0 else (5, 6)))
            pe.wait_ge(m_sq.sem, m_sq.n(l, h, 0))
            for v in range(MT):
                last = mm(bank[5][:, f0:T], ones, m_tmp[:, v, f0:T], start=v == 0, stop=v == MT - 1)
            last.then_inc(m_ss.sem, 1)
            project(7)
            if not more:
                ada_turn(step, (bank[0], bank[1]))

        def mlstm(step, l):
            u0 = first_unit[step, 0]
            for j in range(8):
                mlstm_project(l, 0, j, u0)
            with pe.Fori(0, MH - 1) as h:
                mlstm_head(l, h, u0, True)
            mlstm_head(l, MH - 1, u0, False)

        def attn_group(l, g, u0):
            def mean_square(j):
                pe.wait_ge(t_sqd.sem, t_sqd.n(l, g, j))
                if j > 0:
                    pe.wait_ge(t_var.sem, t_var.n(l, g, j - 1))
                f0 = first_token(l) if j > 0 else 0
                mm(bank[3][:, f0:T], ones, t_sq[:, j % 2, f0:T], start=True, stop=True).then_inc(t_ss.sem, 1)

            def rotary_partner(j):
                pe.wait_ge(t_normed.sem, t_normed.n(l, g, j))
                if j > 0:
                    pe.wait_ge(t_roped.sem, t_roped.n(l, g, j - 1))
                mm(bank[4][:, 0:SEQ], rot, t_raw[:, 0 if j == 0 else j + 1, CTX:T], start=True,
                   stop=True).then_inc(t_turned.sem, 1)

            for j in range(NU):
                pe.wait_ge(t_filled.sem, t_filled.n(l, g, j - 2))
                f0 = first_token(l) if j > 1 else 0
                unit(u0 + j, 0, 0, KT, bank[j % 2][:, f0:T], *split_tiles(xn_hi, xn_lo, f0))
                if j == 1:
                    mean_square(0)
                elif j == 2:
                    pe.wait_ge(t_filled.sem, t_filled.n(l, g, 1))
                    for b in range(NB):
                        last = nc.tensor.transpose(bank[2][:, P * b:P * b + P], t_raw[:, 1, P * b:P * b + P], ident)
                    last.then_inc(t_vt.sem, 1)
                    rotary_partner(0)
                elif j > 2:
                    mean_square(j - 2)
                if j > 3:
                    rotary_partner(j - 3)
            mean_square(AG)
            rotary_partner(AG - 1)
            rotary_partner(AG)
            pe.wait_ge(t_vt_ready.sem, t_vt_ready.n(l, g, 0))
            pe.wait_ge(t_roped.sem, t_roped.n(l, g, NU - 2))

            def score(n):
                b, q = divmod(n, AG)
                keys = CTX if b < 2 else T
                if n >= n_first(l) + 2:
                    pe.wait_ge(t_exp.sem, t_exp.n(l, g, n - 2))
                last = mm(bank[5 + n % 2][:, 0:keys], t_raw[:, 2 + q, P * b:P * b + P], t_raw[:, 0, 0:keys],
                          start=True, stop=b < CB)
                if b >= CB:
                    k0 = P * (NB - 1 + CB - b)
                    c0 = C_WIN + (b - CB) * SEQ + k0 - CTX
                    last = mm(bank[5 + n % 2][:, k0:k0 + P], ident, con[:, c0:c0 + P], start=False, stop=True)
                last.then_inc(t_scored.sem, 1)

            def blend(b):
                kb = 2 if b < 2 else NB
                pe.wait_ge(t_pcopied.sem, t_pcopied.n(l, g, AG * b + AG - 1))
                if b > b_first(l):
                    pe.wait_ge(t_ocopy.sem, t_ocopy.n(l, g, b - 1))
                for k in range(kb):
                    last = mm(bank[7][:, :], t_vtok[:, k, :], t_pt[:, b % 2, k, :], start=k == 0, stop=k == kb - 1)
                last.then_inc(t_out.sem, 1)

            score(n_first(l))
            score(n_first(l) + 1)
            for n in range(n_first(l), NQ):
                b, q = divmod(n, AG)
                kb = 2 if b < 2 else NB
                if n + 2 < NQ:
                    score(n + 2)
                pe.wait_ge(t_prob.sem, t_prob.n(l, g, n))
                if n >= n_first(l) + 2:
                    pe.wait_ge(t_pcopied.sem, t_pcopied.n(l, g, n - 2))
                for k in range(kb):
                    last = nc.tensor.transpose(bank[2 + n % 2][:, P * k:P * k + P],
                                               t_s[:, n % 3, P * k:P * k + P], ident)
                last.then_inc(t_pturn.sem, 1)
                if q == 1 and b > b_first(l):
                    blend(b - 1)
            blend(NB - 1)

        def attn(step, l):
            for g in range(AKV):
                attn_group(l, g, first_unit[step, g])

        def merge(step, l, p):
            u0, r, f0 = first_unit[step, 0], merge_run[step], first_token(l)
            pe.wait_ge(*branch_whole(l, p))
            if p > 0:
                ada_step = ("gdn" if p == 2 else "mlstm", l, 0)
                pe.wait_ge(mod_ready.sem, ada_first(ada_step) + len(MODULATIONS.get(ada_step, [])))
            with pe.Fori(0, KT // 2) as i:
                for j in range(2):
                    pe.wait_ge(b_done.sem, b_done.n(r, i, j - 2))
                    unit(u0 + 2 * j, i, 4, KT, bank[2 * j][:, f0:T], *split_tiles(xn_hi, xn_lo, f0))
                    unit(u0 + 2 * j + 1, i, 4, KT, bank[2 * j + 1][:, f0:T], *split_tiles(y_hi, y_lo, f0))
            pe.wait_ge(b_done.sem, b_done.n(r, KT // 2 - 1, 1))

        def project_out(step, l):
            u0, f0 = first_unit[step, 1], first_token(l)
            ada(step, ADA_BANKS)
            with pe.Fori(0, 2) as i:
                for j in range(4):
                    pe.wait_ge(out_res.sem, out_res.n(l, i, j - 2))
                    for k in range(KT):
                        if j == 0:
                            pe.wait_ge(y_split.sem, y_split.n(l, 0, k))
                        unit(u0 + j, i, 4, KT, bank[4 + j % 2][:, f0:T], *split_tiles(y_hi, y_lo, f0), rows=(k,))

        pe.wait_ge(cond_done.sem, cond_done.n(0, 0, 0))
        for step in STEPS:
            kind, l, p = step
            if kind == "ada":
                pe.wait_ge(con_landed, 16)
                ada(step, ADA_BANKS)
            elif kind == "norm":
                norm(l, p)
            elif kind == "ffn":
                ffn(step, l, p)
            elif kind == "gates":
                gates(step, l)
            elif kind == "gdn":
                gdn(step, l)
            elif kind == "mlstm":
                mlstm(step, l)
            elif kind == "attn":
                attn(step, l)
            elif kind == "merge":
                merge(step, l, p)
            elif kind == "out":
                project_out(step, l)

    @blk.scalar
    def _(act):
        def silu(dst, src):
            return nc.scalar.activation(dst, src, ACT.Silu)

        def inv_root(dst, src, scale, turn, logged, done):
            nc.scalar.activation(dst, src, ACT.Ln, scale=scale, bias=eps_col[:, 0:1]).then_inc(logged[0].sem, 1)
            act.wait_ge(logged[0].sem, logged[0].n(*turn, logged[1]))
            nc.scalar.activation(dst, dst, ACT.Exp, scale=-0.5).then_inc(done.sem, 1)

        def log_exp_tables():
            act.preload_act_table_set("natural_log_exp_and_others")

        def norm(l, j):
            r, f0 = norm_run(l, j), first_token(l, ("norm", l, j))
            for k in range(KT):
                if r > 0:
                    act.wait_ge(stream_ready.sem, stream_ready.n(r - 1, 0, k))
                nc.scalar.activation(sq[:, k, f0:T], H[:, T * k + f0:T * k + T], ACT.Square).then_inc(sq_done.sem, 1)
            log_exp_tables()
            act.wait_ge(ss_done.sem, ss_done.n(r, 0, 0))
            inv_root(rms[:, f0:T], bank[7][:, f0:T], 1.0 / D, (r, 0), (rvar_done, 0), rms_done)
            act.wait_ge(mod_ready.sem, max(ada_number(l, 3 * j), ada_number(l, 3 * j + 1)) + 1)
            for k in range(KT):
                act.wait_ge(nmul_done.sem, nmul_done.n(r, 0, k))
                for c, (a0, a1) in enumerate(HALVES):
                    if a0 < f0:
                        continue
                    last = nc.scalar.activation(sq[:, k, a0:a1], sq[:, k, a0:a1], ACT.Identity,
                                                scale=nscale[:, l, j, k, c:c + 1],
                                                bias=mod[:, l, 3 * j * KT + k, c:c + 1])
                last.then_inc(nmod_done.sem, 1)

        def ffn(step, l, p):
            r, u0, f0 = 2 * l + p, first_unit[step, 0], first_token(l, step)
            with act.Fori(0, FT // 2) as i:
                for j in range(2):
                    act.wait_ge(unit_done, i * 4 + (u0 + 2 * j + 1))
                    act.wait_ge(hid_ready.sem, hid_ready.n(r, i, j - 2))
                    silu(silu_g[:, j, f0:T], bank[2 * j][:, f0:T]).then_inc(silu_done.sem, 1)

        def gates(step, l):
            u0, s0 = first_unit[step, 0], l * S_LAYER
            A = nc.scalar.activation
            act.wait_ge(unit_done, u0 + 1)
            A(gate_a[0:64, :], bank[0][0:64, :], ACT.Identity, bias=sml[0:64, s0 + S_BA:s0 + S_BA + 1])
            A(gate_a[64:P, :], bank[0][64:P, :], ACT.Sigmoid).then_inc(gate_act.sem, 1)
            A(coef[:, :], sml[:, s0 + S_ALOG:s0 + S_ALOG + 1], ACT.Exp).then_inc(gate_act.sem, 1)
            act.wait_ge(gate_dve.sem, gate_dve.n(l, 0, 0))
            A(sofp[:, :], zed[:, :], ACT.Abs).then_inc(gate_act.sem, 1)
            act.wait_ge(gate_act.sem, gate_act.n(l, 0, 2))
            A(sofp[:, :], sofp[:, :], ACT.Exp, scale=-1.0).then_inc(gate_act.sem, 1)
            act.wait_ge(gate_act.sem, gate_act.n(l, 0, 3))
            A(sofp[:, :], sofp[:, :], ACT.Ln, bias=1.0).then_inc(gate_act.sem, 1)
            act.wait_ge(gate_dve.sem, gate_dve.n(l, 0, 2))
            A(col_b[:, :, :], col_g[:, :, 64:P], ACT.Exp).then_inc(gate_act.sem, 1)

        def gdn_fill(l, h, j, landed):
            act.wait_ge(unit_done, landed)
            if j < 3:
                act.wait_ge(conv_done.sem, conv_done.n(l, h, j - 3))
                s0 = first_token(l) // CTX if j == 0 else 0
                nc.scalar.activation(padded[:, j, s0:2, PAD:PAD + CTX], bank[j % 2][:, CTX * s0:T].rearrange(
                    "p (s t) -> p s t", s=2 - s0), ACT.Copy).then_inc(conv_filled.sem, 1)
            else:
                f0 = first_token(l)
                nc.scalar.activation(g_raw[:, f0:T], bank[1][:, f0:T], ACT.Copy).then_inc(g_filled.sem, 1)

        def gdn_silu(l, h, j):
            act.wait_ge(conv_done.sem, conv_done.n(l, h, j))
            if j == 0:
                act.wait_ge(qk_ready.sem, qk_ready.n(l, h, -1))
            f0 = first_token(l) if j == 0 else 0
            silu(qkv[:, j, f0:T], conv[:, j, f0:T]).then_inc(conv_silu.sem, 1)

        def gdn_square(l, h, j):
            act.wait_ge(conv_silu.sem, conv_silu.n(l, h, j))
            f0 = first_token(l) if j == 0 else 0
            nc.scalar.activation(conv[:, j, f0:T], qkv[:, j, f0:T], ACT.Square).then_inc(qk_sq.sem, 1)

        def gdn_root(l, h):
            for j in range(2):
                act.wait_ge(qk_ss.sem, qk_ss.n(l, h, j))
                f0 = first_token(l) if j == 0 else 0
                inv_root(conv[:, j, f0:T], bank[2 + j][:, f0:T], 1.0, (l, h), (qk_var, j), qk_rms)

        def gdn_head(l, h, u0, more):
            A = nc.scalar.activation

            f0, b0 = first_token(l), b_first(l)

            def by_block(x):
                return x.rearrange("p (b t) -> p b t", t=P)

            def fill(j):
                if more:
                    gdn_fill(l, h + 1, j, h * 4 + (u0 + 4 + j + 1))

            act.wait_ge(tok_t.sem, tok_t.n(l, h, 0))
            A(k_tok[:, :, :], by_block(bank[3][:, :]), ACT.Copy).then_inc(tok_ready.sem, 1)
            for d in range(2):
                act.wait_ge(gam_row.sem, gam_row.n(l, h, d))
                A(inv_t[:, d, :, :], by_block(bank[4 + 2 * d][:, :]), ACT.Exp).then_inc(exp_gam.sem, 1)
            act.wait_ge(tok_t.sem, tok_t.n(l, h, 1))
            A(v_tok[:, :, :], by_block(bank[2][:, :]), ACT.Copy).then_inc(tok_ready.sem, 1)
            for d in range(2):
                act.wait_ge(arg_ready.sem, arg_ready.n(l, h, d))
                A(decay[:, d, :, :], decay[:, d, :, :], ACT.Exp).then_inc(decay_done.sem, 1)
            fill(0)
            fill(1)
            for d in range(2):
                act.wait_ge(inv0_turned.sem, inv0_turned.n(l, h, d))
                A(inv_t[:, d, :, :], by_block(bank[4 + 2 * d][:, :]), ACT.Copy).then_inc(inv0_copied.sem, 1)
            for v in range(NL):
                for d in range(2):
                    if v > 0:
                        act.wait_ge(inv_turned.sem, inv_turned.n(l, h, 2 * v + d - 2))
                        A(inv[:, d, :, :], by_block(bank[2 + d][:, :]), ACT.Copy).then_inc(inv_ready.sem, 1)
                    act.wait_ge(prod_done.sem, prod_done.n(l, h, 2 * v + d))
                    A(prod[:, d, :, :], by_block(bank[4 + 2 * d][:, :]), ACT.Copy).then_inc(prod_ready.sem, 1)
                if v == 0:
                    fill(2)
                if v == 1 and more:
                    gdn_silu(l, h + 1, 0)
                    gdn_square(l, h + 1, 0)
                if v == 2:
                    if more:
                        gdn_silu(l, h + 1, 1)
                        gdn_square(l, h + 1, 1)
                    act.wait_ge(g_filled.sem, g_filled.n(l, h, 0))
                    act.wait_ge(head_done.sem, head_done.n(l, h, -1))
                    silu(g_gate[:, f0:T], g_raw[:, f0:T]).then_inc(g_gate_done.sem, 1)
                if v == 3:
                    if more:
                        gdn_silu(l, h + 1, 2)
                    log_exp_tables()
                if v == NL - 2 and more:
                    gdn_root(l, h + 1)
            for j in range(2 * NB):
                d = j % 2
                act.wait_ge(v_new_done.sem, v_new_done.n(l, h, j))
                A(v_new[:, d, :], bank[4 + 2 * d][:, P:2 * P], ACT.Copy).then_inc(v_new_ready.sem, 1)
            act.wait_ge(o_done.sem, o_done.n(l, h, 0))
            A(decay[:, 0, b0:, :], by_block(bank[5][:, f0:T]), ACT.Copy).then_inc(o_first.sem, 1)
            act.wait_ge(o_both.sem, o_both.n(l, h, 0))
            A(prod[:, 0, b0:, :], decay[:, 0, b0:, :], ACT.Square).then_inc(o_sq.sem, 1)
            fill(3)
            act.wait_ge(o_ss.sem, o_ss.n(l, h, 0))
            inv_root(prod[:, 1, b0:, :], by_block(bank[2][:, f0:T]), 1.0 / P, (l, h), (o_var, 0), o_rms)

        def gdn(step, l):
            u0 = first_unit[step, 0]
            act.wait_ge(pad_zeroed.sem, pad_zeroed.n(l, 0, 0))
            for j in range(4):
                gdn_fill(l, 0, j, u0 + j + 1)
            for j in range(3):
                gdn_silu(l, 0, j)
                if j < 2:
                    gdn_square(l, 0, j)
            log_exp_tables()
            gdn_root(l, 0)
            with act.Fori(0, GH - 1) as h:
                gdn_head(l, h, u0, True)
            gdn_head(l, GH - 1, u0, False)

        def mlstm_head(l, h, u0, more):
            A, f0 = nc.scalar.activation, first_token(l)

            def fill(h, j, u):
                act.wait_ge(unit_done, u)
                if j < 6:
                    f = f0 if j < 2 else 0
                    A(m_qkv[:, j // 2, j % 2, f:T], bank[j % 2][:, f:T], ACT.Copy,
                      scale=(MT * P) ** -0.5 if j < 2 else 1.0).then_inc(m_filled.sem, 1)
                else:
                    A(m_gate[:, j % 2, f0:T], bank[j % 2][:, f0:T], ACT.Sigmoid).then_inc(m_filled.sem, 1)

            def refill(*js):
                for j in js if more else ():
                    fill(h + 1, j, h * 8 + (u0 + 8 + j + 1))

            if isinstance(h, int) and h == -1:
                for j in range(8):
                    fill(0, j, u0 + j + 1)
                return
            for v in range(MT):
                act.wait_ge(m_vt.sem, m_vt.n(l, h, v))
                A(m_vtok[:, :, P * v:P * v + P], bank[5 + v][:, :].rearrange("p (b t) -> p b t", b=NB),
                  ACT.Copy).then_inc(m_vt_ready.sem, 1)
            act.wait_ge(m_kq.sem, m_kq.n(l, h, 2))
            refill(0)
            log_exp_tables()
            for d in range(2):
                act.wait_ge(m_arg.sem, m_arg.n(l, h, d))
                A(m_floor[:, f0:T], bank[6][:, f0:T], ACT.Exp)
                for sb in range(NB):
                    for t0, t1, diagonal in reach(d, sb, f0):
                        w = m_w[:, sb, t0:t1]
                        if diagonal:
                            last = A(w, w, ACT.Exp)
                        else:
                            last = A(w, bank[5][:, t0:t1], ACT.Exp, bias=m_col[:, d, sb:sb + 1])
                last.then_inc(m_exp.sem, 1)
                refill(*((1,) if d == 0 else (3, 4)))
                act.wait_ge(m_num.sem, m_num.n(l, h, d))
                A(m_den[:, f0:T], bank[7][:, f0:T], ACT.Abs).then_inc(m_abs.sem, 1)
                refill(*((2,) if d == 0 else ()))
            act.wait_ge(m_added.sem, m_added.n(l, h, 1))
            for v in range(MT):
                last = A(m_tmp[:, v, f0:T], m_h[:, v, f0:T], ACT.Square)
            last.then_inc(m_sq.sem, 1)
            refill(5)
            act.wait_ge(m_ss.sem, m_ss.n(l, h, 0))
            inv_root(m_den[:, f0:T], bank[5][:, f0:T], 1.0 / (MT * P), (l, h), (m_var, 0), m_rms)
            if more:
                act.wait_ge(m_head.sem, m_head.n(l, h, 0))
            refill(6, 7)

        def mlstm(step, l):
            u0 = first_unit[step, 0]
            mlstm_head(l, -1, u0, False)
            with act.Fori(0, MH - 1) as h:
                mlstm_head(l, h, u0, True)
            mlstm_head(l, MH - 1, u0, False)

        def attn_group(l, g, u0):
            A = nc.scalar.activation
            log_exp_tables()

            def root(j):
                act.wait_ge(t_ss.sem, t_ss.n(l, g, j))
                if j >= 2:
                    act.wait_ge(t_normed.sem, t_normed.n(l, g, j - 2))
                f0 = first_token(l) if j > 0 else 0
                inv_root(t_root[:, j % 2, f0:T], bank[3][:, f0:T], 1.0 / P, (l, g), (t_var, j), t_rms)

            for j in range(NU):
                act.wait_ge(unit_done, u0 + j + 1)
                f0 = first_token(l) if j > 1 else 0
                A(t_raw[:, j, f0:T], bank[j % 2][:, f0:T], ACT.Copy).then_inc(t_filled.sem, 1)
                if j != 1:
                    n = 0 if j == 0 else j - 1
                    act.wait_ge(t_filled.sem, t_filled.n(l, g, j))
                    if n >= 2:
                        act.wait_ge(t_ss.sem, t_ss.n(l, g, n - 2))
                    A(t_sq[:, n % 2, f0:T], t_raw[:, j, f0:T], ACT.Square).then_inc(t_sqd.sem, 1)
                if j == 1:
                    root(0)
                elif j == 2:
                    act.wait_ge(t_vt.sem, t_vt.n(l, g, 0))
                    A(t_vtok[:, :, :], bank[2][:, :].rearrange("p (b t) -> p b t", b=NB),
                      ACT.Copy).then_inc(t_vt_ready.sem, 1)
                elif j > 2:
                    root(j - 2)
            root(AG)

            def exps(n):
                b, q = divmod(n, AG)
                keys, c = (CTX if b < 2 else T), t_col[:, n % 3, :]
                k = l * S_LAYER + S_SINK + AG * g + q
                act.wait_ge(t_masked.sem, t_masked.n(l, g, n))
                A(c[:, 2:3], sml[:, k:k + 1], ACT.Exp, bias=c[:, 1:2])
                A(t_s[:, n % 3, 0:keys], bank[5 + n % 2][:, 0:keys], ACT.Exp, bias=c[:, 1:2], accum_out=c[:, 3:4]).then_inc(t_exp.sem, 1)

            exps(n_first(l))
            for n in range(n_first(l), NQ):
                b, q = divmod(n, AG)
                kb = 2 if b < 2 else NB
                if n + 1 < NQ:
                    exps(n + 1)
                act.wait_ge(t_pturn.sem, t_pturn.n(l, g, n))
                if b >= b_first(l) + 2:
                    act.wait_ge(t_out.sem, t_out.n(l, g, b - 2))
                A(t_pt[:, b % 2, 0:kb, P * q:P * q + P], bank[2 + n % 2][:, 0:P * kb].rearrange(
                    "p (k t) -> p k t", k=kb), ACT.Copy).then_inc(t_pcopied.sem, 1)
                if q == 2 and b > b_first(l) or n == NQ - 1:
                    for c in ([b - 1] if n < NQ - 1 else [b]):
                        act.wait_ge(t_out.sem, t_out.n(l, g, c))
                        if not (c == b_first(l) and g == 0):
                            act.wait_ge(t_osplit.sem, t_osplit.n(l, g, c - 1) if c > b_first(l)
                                        else t_osplit.n(l, g - 1, NB - 1))
                        A(t_o[:, :, :], bank[7][:, :].rearrange("p (q t) -> p q t", q=AG),
                          ACT.Copy).then_inc(t_ocopy.sem, 1)

        def attn(step, l):
            for g in range(AKV):
                attn_group(l, g, first_unit[step, g])

        def merge(step, l, p):
            u0, r, f0 = first_unit[step, 0], merge_run[step], first_token(l)
            with act.Fori(0, KT // 2) as i:
                for j in range(2):
                    act.wait_ge(unit_done, i * 4 + (u0 + 2 * j + 1))
                    act.wait_ge(b_done.sem, b_done.n(r, i, j - 2))
                    nc.scalar.activation(b_gate[:, j, f0:T], bank[2 * j][:, f0:T], ACT.Sigmoid).then_inc(b_sig.sem, 1)

        for e in (m_filled, m_vt_ready, t_filled, conv_filled):
            act.sem_inc(e.sem, e.credit)
        act.wait_ge(sml_landed, 16)
        act.wait_ge(cond_zeroed.sem, cond_zeroed.n(0, 0, 0))
        silu(cond_at[:, :, ADA_M - 2:ADA_M], sml[:, S_COND:S_COND + 16].rearrange(
            "p (k c) -> p k c", c=2)).then_inc(cond_done.sem, 1)
        act.wait_ge(tokens_landed, 16)
        act.wait_ge(eps_set.sem, eps_set.n(0, 0, 0))
        for step in STEPS:
            kind, l, p = step
            if kind == "norm":
                norm(l, p)
            elif kind == "ffn":
                ffn(step, l, p)
            elif kind == "gates":
                gates(step, l)
            elif kind == "gdn":
                gdn(step, l)
            elif kind == "mlstm":
                mlstm(step, l)
            elif kind == "attn":
                attn(step, l)
            elif kind == "merge":
                merge(step, l, p)

    @blk.vector
    def _(dve):
        step_of = Chain(dve, dve_step)
        V = nc.vector

        def start():
            V.memset(cond_at[:, :, :].rearrange("p k c -> p (k c)"), 0.0).then_inc(cond_zeroed.sem, 1)
            V.memset(eps_col[:, :], EPS).then_inc(eps_set.sem, 1)
            dve.wait_ge(sml_landed, 16)

        def ada_copy(step, banks, pair=0):
            for n in ada_pair(step, pair):
                dve.wait_ge(unit_done, first_unit[step, ada_job(step)] + KT * (n + 1))
                V.tensor_copy(ada_rows[0:ADA_M, n % 2, :],
                              banks[n % len(banks)][0:ADA_M, 0:P]).then_inc(ada_copied.sem, 1)

        def ada_finish(step, banks, pair=0):
            for n in ada_pair(step, pair):
                l, m = MODULATIONS[step][n]
                dve.wait_ge(ada_turned.sem, ada_first(step) + n + 1)
                v, (j, part), tiles = mod[:, l, KT * m:KT * m + KT, :], divmod(m, 3), [P, KT, 2]
                b = l * S_LAYER + S_BADA + KT * m
                ins = V.tensor_tensor(v, banks[n % len(banks)][:, P:P + ADA_M].rearrange("p (t c) -> p t c", c=2),
                                      sml[:, b:b + KT].unsqueeze(2).to_broadcast(tiles), ALU.add)
                if part > 0:
                    step_of(ins)
                if part == 1:
                    w = l * S_LAYER + S_NORM + KT * j
                    ins = V.scalar_tensor_tensor(out=nscale[:, l, j, :, :], in0=v, scalar=1.0,
                                                 in1=sml[:, w:w + KT].unsqueeze(2).to_broadcast(tiles),
                                                 op0=ALU.add, op1=ALU.mult)
                elif part == 2:
                    ins = V.tensor_scalar(rgate[:, l, j, :, :], v, 1.0 if j == 1 else 0.5, None, ALU.mult)
                ins.then_inc(mod_ready.sem, 1)
                dve.wait_ge(mod_ready.sem, ada_first(step) + n + 1)

        def ada(step, banks):
            for pair in ada_pairs(step):
                ada_copy(step, banks, pair)
                ada_finish(step, banks, pair)

        def norm(l, j):
            r, f0 = norm_run(l, j), first_token(l, ("norm", l, j))
            dve.wait_ge(rms_done.sem, rms_done.n(r, 0, 0))
            for k in range(KT + 2):
                if k < KT:
                    V.tensor_tensor(sq[:, k, f0:T], H[:, T * k + f0:T * k + T], rms[:, f0:T],
                                    ALU.mult).then_inc(nmul_done.sem, 1)
                if k < 2:
                    continue
                k -= 2
                dve.wait_ge(nmod_done.sem, nmod_done.n(r, 0, k))
                step_of(V.tensor_copy(xn_hi[:, k, f0:T], sq[:, k, f0:T]))
                V.tensor_tensor(xn_lo[:, k, f0:T], sq[:, k, f0:T], xn_hi[:, k, f0:T].bitcast(F32),
                                ALU.subtract).then_inc(xn_ready.sem, 1)
            ada(("norm", l, j), ADA_BANKS)

        def share(step, n, j, i=0):
            job = jobs[step][n]
            if not job.shared:
                return
            m, u = len(job.units), first_unit[step, n]
            kn = job.units[j % m][2]
            dve.wait_ge(hi_done, m * i + (u + j + 1))
            cut = slice(SHARE * P, kn * P)
            V.tensor_tensor(w_lo[:, (u + j) % 2, cut], raw[:, (u + j) % 4, cut],
                            w_hi[:, (u + j) % 2, cut].bitcast(F32), ALU.subtract).then_inc(share_done, 1)

        def residual(n, i, l, j, src, f0):
            at_n = (i * 4 + n) * T
            for c, (a0, a1) in enumerate(HALVES):
                if a0 < f0:
                    continue
                h = H[:, bass.ds(at_n + a0, a1 - a0)] if not isinstance(i, int) else H[:, at_n + a0:at_n + a1]
                last = V.scalar_tensor_tensor(out=h, in0=src[:, a0:a1], scalar=rgate[:, l, j, i * 4 + n, c:c + 1],
                                              in1=h, op0=ALU.mult, op1=ALU.add)
            return last

        def ffn(step, l, p):
            r, u0, f0 = 2 * l + p, first_unit[step, 0], first_token(l, step)
            def turn(i, more):
                for j in range(2):
                    for n in (2 * j + 2, 2 * j + 3) if j == 0 or more else ():
                        share(step, 0, n, i)
                    dve.wait_ge(silu_done.sem, silu_done.n(r, i, j))
                    dve.wait_ge(unit_done, i * 4 + (u0 + 2 * j + 2))
                    step_of(V.tensor_tensor(hid[:, j, f0:T], silu_g[:, j, f0:T], bank[2 * j + 1][:, f0:T],
                                            ALU.mult))
                    hi = hid_hi[:, bass.ds((i * 2 + j) * T + f0, T - f0)]
                    lo = hid_lo[:, bass.ds((i * 2 + j) * T + f0, T - f0)]
                    step_of(V.tensor_copy(hi, hid[:, j, f0:T]))
                    V.tensor_tensor(lo, hid[:, j, f0:T], hi.bitcast(F32), ALU.subtract).then_inc(hid_ready.sem, 1)

            for n in range(2):
                share(step, 0, n)
            with step_of.turns(0, FT // 2 - 1, 4) as i:
                turn(i, True)
            turn(FT // 2 - 1, False)
            u0, m = first_unit[step, 1], 4 * len(DOWN_CUTS)
            for n in range(2):
                share(step, 1, n)
            dve.wait_ge(hid_ready.sem, hid_ready.n(r, FT // 2 - 1, 1))
            for i in range(2):
                for n in range(4):
                    for x in range(3 * (4 * i + n) + 2, min(3 * (4 * i + n) + 5, 2 * m)):
                        share(step, 1, x)
                    dve.wait_ge(unit_done, i * m + (u0 + 3 * n + 3))
                    residual(n, i, l, 2 * p, bank[4 + n % 2], f0).then_inc(res_done.sem, 1)
            signal_stream(l, p)

        def signal_stream(l, p):
            dve.wait_ge(res_done.sem, res_done.n(2 * l + p, 1, 3))
            for k in range(KT):
                dve.sem_inc(stream_ready.sem, 1)

        def gates(step, l):
            u0, s0 = first_unit[step, 0], l * S_LAYER

            def col(c, a0=0, a1=P):
                return sml[a0:a1, s0 + c:s0 + c + 1]

            def scan(dst, src, rows, reverse, length, reset, op0, op1, data0):
                prev = None
                for n, t0 in enumerate(range(0, T, length)):
                    if t0 % reset == 0:
                        prev = 0.0
                    cut = slice(t0, t0 + length)
                    views = [x[rows, cut][:, ::-1] if reverse else x[rows, cut] for x in (dst, data0, src)]
                    step_of(V.tensor_tensor_scan(views[0], views[1], views[2], prev, op0, op1))
                    e = t0 if reverse else t0 + length - 1
                    prev = dst[rows, e:e + 1]

            step_of(V.memset(unit_row[:, :], 1.0))
            dve.wait_ge(unit_done, u0 + 2)
            V.tensor_scalar(zed[:, :], bank[1][:, :], col(S_BB), col(S_SGN), ALU.add,
                            ALU.mult).then_inc(gate_dve.sem, 1)
            dve.wait_ge(gate_act.sem, gate_act.n(l, 0, 4))
            step_of(V.scalar_tensor_tensor(out=zed[:, :], in0=zed[:, :], scalar=0.0, in1=sofp[:, :],
                                           op0=ALU.max, op1=ALU.add))
            step_of(V.tensor_scalar(zed[:, :], zed[:, :], coef[:, 0:1], -1.0, ALU.mult, ALU.mult))
            for d in range(2):
                scan(cum, zed, slice(32 * d, 32 * d + 32), d == 1, CTX, T, ALU.mult, ALU.add, unit_row)
                scan(cum, zed, slice(64 + 32 * d, 96 + 32 * d), d == 1, P, P, ALU.mult, ALU.add, unit_row)
            step_of(V.tensor_tensor(gate_a[0:64, :], gate_a[0:64, :], cum[0:64, :], ALU.subtract))
            for d in range(2):
                scan(run_max, gate_a, slice(32 * d, 32 * d + 32), d == 1, CTX, T, ALU.max, ALU.max, gate_a)
            step_of(V.tensor_scalar(rows_m[0:64, :], run_max[0:64, :], -1.0, None, ALU.mult))
            step_of(V.tensor_copy(rows_m[64:P, :], cum[64:P, :]))
            V.scalar_tensor_tensor(out=rows_n[0:64, :], in0=cum[0:64, :], scalar=-1.0, in1=run_max[0:64, :],
                                   op0=ALU.mult, op1=ALU.subtract).then_inc(gate_dve.sem, 1)
            ada_copy(step, (bank[6],))
            for j, dst in enumerate((col_a, col_g)):
                dve.wait_ge(gate_pe.sem, gate_pe.n(l, 0, j))
                c = V.tensor_copy(dst[:, :, :], bank[2 + j][:, :].rearrange("p (b t) -> p b t", b=NB))
                if j == 0:
                    step_of(c)
            c.then_inc(gate_dve.sem, 1)
            dve.wait_ge(gate_act.sem, gate_act.n(l, 0, 5))
            step_of(V.scalar_tensor_tensor(out=col_b[:, :, :], in0=col_b[:, :, :], scalar=-1.0,
                                           in1=col_a[:, :, 64:P], op0=ALU.mult, op1=ALU.mult))
            ada_finish(step, (bank[6],))

        def gdn_conv_w(l, h):
            w0 = l * S_LAYER + S_CONV
            step_of(V.tensor_copy(conv_w[:, :], sml[:, bass.ds(h * (3 * CONV_K) + w0, 3 * CONV_K)]))

        def gdn_tap(l, h, n):
            j, k = divmod(n, CONV_K)
            s0 = first_token(l) // CTX if j == 0 else 0
            acc = conv[:, j, CTX * s0:T].rearrange("p (s t) -> p s t", s=2 - s0)
            tap, src = conv_w[:, n:n + 1], padded[:, j, s0:2, k:k + CTX]
            if k == 0:
                dve.wait_ge(conv_filled.sem, conv_filled.n(l, h, j))
                if j == 2:
                    dve.wait_ge(conv_silu.sem, conv_silu.n(l, h, -1))
                step_of(V.tensor_scalar(acc, src, tap, None, ALU.mult))
            else:
                ins = V.scalar_tensor_tensor(out=acc, in0=src, scalar=tap, in1=acc, op0=ALU.mult, op1=ALU.add)
                if k < CONV_K - 1:
                    step_of(ins)
                else:
                    ins.then_inc(conv_done.sem, 1)

        def gdn_norm(l, h):
            for j in (1, 0):
                dve.wait_ge(qk_rms.sem, qk_rms.n(l, h, 1))
                f0 = first_token(l) if j == 0 else 0
                V.scalar_tensor_tensor(out=qk_n[:, j, f0:T], in0=qkv[:, j, f0:T],
                                       scalar=P ** -0.5 if j == 0 else 1.0, in1=conv[:, j, f0:T], op0=ALU.mult, op1=ALU.mult).then_inc(qk_ready.sem, 1)
                if j == 1:
                    for d in range(2):
                        row = h + GD_ROW[d]
                        V.tensor_copy(pick[:, d, :], con[:, bass.ds(row + C_ID, 1)].to_broadcast([P, P])).then_inc(
                            pick_ready.sem, 1)
            for d in range(2):
                row = h + GD_ROW[d]
                for j, src in enumerate((col_g[:, :, bass.ds(row, 1)], col_a[:, :, bass.ds(row, 1)],
                                         col_b[:, :, bass.ds(row - 64, 1)])):
                    step_of(V.tensor_copy(lane_col[:, d, j, :].unsqueeze(2), src))

        def gdn_head(l, h, more):
            s0 = l * S_LAYER
            f0, b0 = first_token(l), b_first(l)
            q_t = qk_n[:, 0, f0:T]

            def b4(x):
                return x.rearrange("p (b t) -> p b t", t=P)

            def spread(x):
                return x.unsqueeze(2).to_broadcast([P, NB, P])

            for d in range(2):
                dve.wait_ge(exp_gam.sem, exp_gam.n(l, h, d))
                if d == 0:
                    dve.wait_ge(head_done.sem, head_done.n(l, h, -1))
                for b in range(NB):
                    last = V.scalar_tensor_tensor(
                        out=decay[:, d, b, :], in0=bank[4 + 2 * d][:, P * b:P * b + P],
                        scalar=lane_col[:, d, 0, b:b + 1], in1=con[:, C_MIN + P * d:C_MIN + P * d + P],
                        op0=ALU.subtract, op1=ALU.min)
                last.then_inc(arg_ready.sem, 1)
            for d in range(2):
                dve.wait_ge(kk_done.sem, kk_done.n(l, h, 0))
                dve.wait_ge(decay_done.sem, decay_done.n(l, h, d))
                V.tensor_tensor(prod[:, d, :, :], b4(bank[3][:, :]), decay[:, d, :, :], ALU.mult).then_inc(
                    l_ready.sem, 1)
            for d in range(2):
                e = chunk_end(d)
                dve.wait_ge(kk_done.sem, kk_done.n(l, h, 1))
                step_of(V.tensor_tensor(p_t[:, d, b0:, :], b4(bank[2][:, f0:T]), decay[:, d, b0:, :], ALU.mult))
                step_of(V.tensor_copy(end_col[:, d, 0, :].unsqueeze(2), decay[:, d, :, e:e + 1]))
                step_of(V.tensor_copy(end_col[:, d, 1, :].unsqueeze(2), inv_t[:, d, :, e:e + 1]))
                step_of(V.tensor_tensor(q_dec[:, d, b0:, :], b4(q_t), inv_t[:, d, b0:, :], ALU.mult))
            for d in range(2):
                dve.wait_ge(l_turned.sem, l_turned.n(l, h, d))
                V.tensor_tensor(a_mat[:, d, :, :], b4(bank[5 + 2 * d][:, :]), spread(lane_col[:, d, 1, :]),
                                ALU.mult).then_inc(a_ready.sem, 1)
                dve.wait_ge(a_ready.sem, a_ready.n(l, h, d))
                m = lev[:, d * len(LEVELS) * P:(d * len(LEVELS) + 1) * P].unsqueeze(1).to_broadcast([P, NB, P])
                step_of(V.tensor_tensor(inv[:, d, :, :], a_mat[:, d, :, :], m, ALU.mult))
                V.tensor_tensor(inv[:, d, :, :], ident.unsqueeze(1).to_broadcast([P, NB, P]), inv[:, d, :, :],
                                ALU.subtract).then_inc(inv0_ready.sem, 1)
            if more:
                gdn_conv_w(l, h + 1)
                for n in range(CONV_K):
                    gdn_tap(l, h + 1, n)
            for d in range(2):
                dve.wait_ge(tok_ready.sem, tok_ready.n(l, h, 1))
                step_of(V.tensor_tensor(k_end[:, d, :, :], k_tok[:, :, :], spread(end_col[:, d, 0, :]), ALU.mult))
                V.tensor_tensor(v_beta[:, d, :, :], v_tok[:, :, :], spread(lane_col[:, d, 1, :]),
                                ALU.mult).then_inc(lane_ready.sem, 1)
            n = CONV_K
            for v in range(NL):
                for d in range(2):
                    j = 2 * v + d
                    dve.wait_ge(corr_done.sem, corr_done.n(l, h, j))
                    if v == 0:
                        dve.wait_ge(inv0_copied.sem, inv0_copied.n(l, h, d))
                    V.tensor_tensor(inv_t[:, d, :, :], inv_t[:, d, :, :], b4(bank[5 + 2 * d][:, :]),
                                    ALU.subtract).then_inc(inv_t_ready.sem, 1)
                    for _ in range(1 + d):
                        if more and n < 3 * CONV_K:
                            gdn_tap(l, h + 1, n)
                            n += 1
            if not more:
                ada_copy(("gdn", l, 0), (bank[0],))
            for i in range(NB):
                for d in range(2):
                    b = scan_order(d)[i]
                    if i == 0:
                        dve.wait_ge(lane_ready.sem, lane_ready.n(l, h, d))
                        V.tensor_copy(resid[:, d, :], v_beta[:, d, b, :]).then_inc(resid_ready.sem, 1)
                    else:
                        dve.wait_ge(ks_done.sem, ks_done.n(l, h, 2 * (i - 1) + d))
                        V.scalar_tensor_tensor(
                            out=resid[:, d, :], in0=bank[4 + 2 * d][:, 0:P], scalar=lane_col[:, d, 2, b:b + 1],
                            in1=v_beta[:, d, b, :], op0=ALU.mult, op1=ALU.add).then_inc(resid_ready.sem, 1)
                if i < NB - 1:
                    for d in range(2):
                        b = scan_order(d)[i]
                        dve.wait_ge(ds_done.sem, ds_done.n(l, h, 2 * i + d))
                        if i == 0:
                            V.tensor_copy(state[:, d, :], bank[4 + 2 * d][:, 2 * P:3 * P]).then_inc(
                                state_ready.sem, 1)
                        else:
                            V.scalar_tensor_tensor(
                                out=state[:, d, :], in0=state[:, d, :], scalar=end_col[:, d, 1, b:b + 1],
                                in1=bank[4 + 2 * d][:, 2 * P:3 * P], op0=ALU.mult,
                                op1=ALU.add).then_inc(state_ready.sem, 1)
            dve.wait_ge(o_done.sem, o_done.n(l, h, 1))
            dve.wait_ge(o_first.sem, o_first.n(l, h, 0))
            V.tensor_tensor(o_sum[:, f0:T], o_sum[:, f0:T], bank[7][:, f0:T], ALU.add).then_inc(o_both.sem, 1)
            if more:
                gdn_norm(l, h + 1)
            dve.wait_ge(o_rms.sem, o_rms.n(l, h, 0))
            step_of(V.tensor_tensor(decay[:, 0, b0:, :], decay[:, 0, b0:, :], prod[:, 1, b0:, :], ALU.mult))
            dve.wait_ge(g_gate_done.sem, g_gate_done.n(l, h, 0))
            step_of(V.scalar_tensor_tensor(out=o_sum[:, f0:T], in0=o_sum[:, f0:T],
                                           scalar=sml[:, s0 + S_GDN:s0 + S_GDN + 1], in1=g_gate[:, f0:T],
                                           op0=ALU.mult, op1=ALU.mult))
            hi, lo = (y[:, bass.ds(h * T + f0, T - f0)] for y in (y_hi, y_lo))
            step_of(V.tensor_copy(hi, o_sum[:, f0:T]))
            V.tensor_tensor(lo, o_sum[:, f0:T], hi.bitcast(F32), ALU.subtract).then_inc(head_done.sem, 1)

        def gdn(step, l):
            V.memset(padded[:, :, :, :].rearrange("p a b c -> p (a b c)"), 0.0).then_inc(pad_zeroed.sem, 1)
            dve.wait_ge(pad_zeroed.sem, pad_zeroed.n(l, 0, 0))
            gdn_conv_w(l, 0)
            for n in range(3 * CONV_K):
                gdn_tap(l, 0, n)
            gdn_norm(l, 0)
            with step_of.turns(0, GH - 1, GDN_STEPS) as h:
                gdn_head(l, h, True)
            gdn_head(l, GH - 1, False)
            ada_finish(step, (bank[0],))

        def mlstm_head(l, h, more):
            f0 = first_token(l)
            for d in range(2):
                row = h + ML_ROW[d]
                step_of(V.tensor_copy(m_col[:, d, :].unsqueeze(2), col_a[:, :, bass.ds(row, 1)]))
                V.tensor_copy(m_pick[:, d, :], con[:, bass.ds(row + C_ID, 1)].to_broadcast([P, P])).then_inc(
                    m_picked.sem, 1)
            for d in range(2):
                dve.wait_ge(m_rows.sem, m_rows.n(l, h, d))
                for sb in range(b_first(l), NB):
                    cut = slice(P * sb, P * sb + P)
                    last = V.scalar_tensor_tensor(
                        out=m_w[:, sb, cut], in0=bank[5][:, cut], scalar=m_col[:, d, sb:sb + 1],
                        in1=con[:, C_MIN + P * d:C_MIN + P * d + P], op0=ALU.add, op1=ALU.min)
                last.then_inc(m_arg.sem, 1)
                dve.wait_ge(m_exp.sem, m_exp.n(l, h, d))
                dve.wait_ge(m_kq.sem, m_kq.n(l, h, 2))
                for sb in range(NB):
                    src, c0, f = kq_view(sb)
                    for t0, t1 in joined(d, sb, f0):
                        w = m_w[:, sb, t0:t1]
                        last = V.tensor_tensor(w, src[:, c0 + t0 - f:c0 + t1 - f], w, ALU.mult)
                last.then_inc(m_weighted.sem, 1)
                dve.wait_ge(m_abs.sem, m_abs.n(l, h, d))
                step_of(V.tensor_tensor(m_den[:, f0:T], m_den[:, f0:T], m_floor[:, f0:T], ALU.max))
                step_of(V.reciprocal(m_den[:, f0:T], m_den[:, f0:T]))
                if d == 0:
                    for v in range(MT):
                        last = V.tensor_tensor(m_h[:, v, f0:T], bank[5 + v][:, f0:T], m_den[:, f0:T], ALU.mult)
                else:
                    for v in range(MT):
                        step_of(V.tensor_tensor(m_tmp[:, v, f0:T], bank[5 + v][:, f0:T], m_den[:, f0:T], ALU.mult))
                        last = V.tensor_tensor(m_h[:, v, f0:T], m_h[:, v, f0:T], m_tmp[:, v, f0:T], ALU.add)
                last.then_inc(m_added.sem, 1)
            if not more:
                ada_copy(("mlstm", l, 0), (bank[0], bank[1]))
            dve.wait_ge(m_rms.sem, m_rms.n(l, h, 0))
            step_of(V.tensor_copy(m_wn[:, :], sml[:, bass.ds(h * MT + l * S_LAYER + S_MLN, MT)]))
            for v in range(MT):
                step_of(V.tensor_tensor(m_h[:, v, f0:T], m_h[:, v, f0:T], m_den[:, f0:T], ALU.mult))
                step_of(V.scalar_tensor_tensor(out=m_h[:, v, f0:T], in0=m_h[:, v, f0:T], scalar=m_wn[:, v:v + 1],
                                               in1=m_gate[:, v, f0:T], op0=ALU.mult, op1=ALU.mult))
                hi, lo = (y[:, bass.ds((h * MT + v) * T + f0, T - f0)] for y in (y_hi, y_lo))
                step_of(V.tensor_copy(hi, m_h[:, v, f0:T]))
                last = V.tensor_tensor(lo, m_h[:, v, f0:T], hi.bitcast(F32), ALU.subtract)
            last.then_inc(m_head.sem, 1)

        def mlstm(step, l):
            with step_of.turns(0, MH - 1, MLSTM_STEPS) as h:
                mlstm_head(l, h, True)
            mlstm_head(l, MH - 1, False)
            ada_finish(step, (bank[0], bank[1]))

        def attn_group(l, g, u0):
            s0 = l * S_LAYER
            step_of(V.tensor_scalar(t_w[:, 0:1], sml[:, s0 + S_QKN:s0 + S_QKN + 1], P ** -0.5, None, ALU.mult))
            step_of(V.tensor_copy(t_w[:, 1:2], sml[:, s0 + S_QKN + 1:s0 + S_QKN + 2]))
            for j in range(NU - 1):
                n = 0 if j == 0 else j + 1
                f0 = first_token(l) if j > 0 else 0
                x, lat = t_raw[:, n, f0:T], t_raw[:, n, CTX:T]
                dve.wait_ge(t_rms.sem, t_rms.n(l, g, j))
                V.scalar_tensor_tensor(out=x, in0=x, scalar=t_w[:, 1:2] if j == 0 else t_w[:, 0:1],
                                       in1=t_root[:, j % 2, f0:T], op0=ALU.mult, op1=ALU.mult).then_inc(t_normed.sem, 1)
                dve.wait_ge(t_turned.sem, t_turned.n(l, g, j))
                step_of(V.tensor_tensor(t_rot[:, :], bank[4][:, 0:SEQ], con[:, C_SIN:C_SIN + SEQ], ALU.mult))
                step_of(V.tensor_tensor(lat, lat, con[:, C_COS:C_COS + SEQ], ALU.mult))
                V.tensor_tensor(lat, lat, t_rot[:, :], ALU.add).then_inc(t_roped.sem, 1)
            def split_o(b):
                dve.wait_ge(t_ocopy.sem, t_ocopy.n(l, g, b))
                hi, lo = (y[:, :].rearrange("p (h t) -> p h t", h=KT)[:, AG * g:AG * g + AG, P * b:P * b + P]
                          for y in (y_hi, y_lo))
                step_of(V.tensor_copy(hi, t_o[:, :, :]))
                V.tensor_tensor(lo, t_o[:, :, :], hi.bitcast(F32), ALU.subtract).then_inc(t_osplit.sem, 1)

            def row_max(n):
                b, q = divmod(n, AG)
                keys, c = (CTX if b < 2 else T), t_col[:, n % 3, :]
                scores = bank[5 + n % 2]
                dve.wait_ge(t_scored.sem, t_scored.n(l, g, n))
                if n >= n_first(l) + 3:
                    dve.wait_ge(t_pturn.sem, t_pturn.n(l, g, n - 3))
                step_of(V.tensor_reduce(c[:, 0:1], scores[:, 0:keys], AX.X, ALU.max))
                k = s0 + S_SINK + AG * g + q
                V.tensor_scalar(c[:, 1:2], c[:, 0:1], sml[:, k:k + 1], -1.0, ALU.max, ALU.mult).then_inc(
                    t_masked.sem, 1)

            row_max(n_first(l))
            for n in range(n_first(l), NQ):
                b, q = divmod(n, AG)
                keys, c = (CTX if b < 2 else T), t_col[:, n % 3, :]
                if n + 1 < NQ:
                    row_max(n + 1)
                x = t_s[:, n % 3, 0:keys]
                dve.wait_ge(t_exp.sem, t_exp.n(l, g, n))
                step_of(V.tensor_tensor(c[:, 4:5], c[:, 2:3], c[:, 3:4], ALU.add))
                step_of(V.reciprocal(c[:, 5:6], c[:, 4:5]))
                V.tensor_scalar(x, x, c[:, 5:6], None, ALU.mult).then_inc(t_prob.sem, 1)
                if q == 3 and b > b_first(l):
                    split_o(b - 1)
            split_o(NB - 1)

        def attn(step, l):
            for g in range(AKV):
                attn_group(l, g, first_unit[step, g])

        def merge(step, l, p):
            u0, r, f0 = first_unit[step, 0], merge_run[step], first_token(l)
            opens = r == min(n for s, n in merge_run.items() if s[1] == l)

            def turn(i, more):
                for j in range(2):
                    for n in (2 * j + 2, 2 * j + 3) if j == 0 or more else ():
                        share(step, 0, n, i)
                    dve.wait_ge(b_sig.sem, b_sig.n(r, i, j))
                    dve.wait_ge(unit_done, i * 4 + (u0 + 2 * j + 2))
                    y = y_sum[:, bass.ds((i * 2 + j) * T + f0, T - f0)]
                    if opens:
                        V.tensor_tensor(y, b_gate[:, j, f0:T], bank[2 * j + 1][:, f0:T], ALU.mult).then_inc(
                            b_done.sem, 1)
                    else:
                        step_of(V.tensor_tensor(b_tmp[:, j, f0:T], b_gate[:, j, f0:T], bank[2 * j + 1][:, f0:T],
                                                ALU.mult))
                        V.tensor_tensor(y, y, b_tmp[:, j, f0:T], ALU.add).then_inc(b_done.sem, 1)

            for n in range(2):
                share(step, 0, n)
            with step_of.turns(0, KT // 2 - 1, 0 if opens else 2) as i:
                turn(i, True)
            turn(KT // 2 - 1, False)

        def project_out(step, l):
            u0, f0 = first_unit[step, 1], first_token(l)
            dve.wait_ge(b_done.sem, b_done.n(max(r for s, r in merge_run.items() if s[1] == l), KT // 2 - 1, 1))
            for n in range(2):
                share(step, 1, n)
            for k in range(KT):
                cut = slice(T * k + f0, T * k + T)
                step_of(V.tensor_copy(y_hi[:, cut], y_sum[:, cut]))
                V.tensor_tensor(y_lo[:, cut], y_sum[:, cut], y_hi[:, cut].bitcast(F32),
                                ALU.subtract).then_inc(y_split.sem, 1)
            ada(step, ADA_BANKS)
            for i in range(2):
                for n in range(4):
                    if 4 * i + n + 2 < KT:
                        share(step, 1, 4 * i + n + 2)
                    dve.wait_ge(unit_done, i * 4 + (u0 + n + 1))
                    residual(n, i, l, 1, bank[4 + n % 2], f0).then_inc(out_res.sem, 1)
            dve.wait_ge(out_res.sem, out_res.n(l, 1, 3))
            for k in range(KT):
                dve.sem_inc(stream_ready.sem, 1)

        start()
        for step in STEPS:
            kind, l, p = step
            if kind == "ada":
                ada(step, ADA_BANKS)
                dve.wait_ge(con_landed, 16)
                dve.wait_ge(lev_landed, 16)
                step_of(V.tensor_copy(lev[:, :], lev_f[:, :]))
            elif kind == "norm":
                norm(l, p)
            elif kind == "ffn":
                ffn(step, l, p)
            elif kind == "gates":
                gates(step, l)
            elif kind == "gdn":
                gdn(step, l)
            elif kind == "mlstm":
                mlstm(step, l)
            elif kind == "attn":
                attn(step, l)
            elif kind == "merge":
                merge(step, l, p)
            elif kind == "out":
                project_out(step, l)

    block.__exit__(None, None, None)


def _layout(**inputs):
    a = {k: np.asarray(v) for k, v in inputs.items()}
    f = np.float32
    arrays = {"tokens": np.ascontiguousarray(np.concatenate([a["ctx"][0], a["x"][0]], 0).T)}

    def tiles(v, n):
        return v.reshape(n, P).T

    small = np.zeros((P, S_ALL), f)
    for l in range(DEPTH):
        s = small[:, l * S_LAYER:(l + 1) * S_LAYER]
        s[:, S_BADA:S_BADA + NMOD * KT] = tiles(a["b_ada"][l], NMOD * KT)
        s[:, S_NORM:S_NORM + 3 * KT] = tiles(a["norm_w"][l].reshape(-1), 3 * KT)
        s[:, S_CONV:S_CONV + 3 * GH * CONV_K] = a["gdn_conv_w"][l].reshape(3, CONV_K, GH, P).transpose(
            3, 2, 0, 1).reshape(P, -1)
        s[:, S_QKN:S_QKN + 2] = a["attn_qk_norm"][l].T
        s[:, S_SINK:S_SINK + AH] = a["attn_sink"][l][None, :]
        s[:, S_MLN:S_MLN + MH * MT] = tiles(a["ml_norm_w"][l].reshape(-1), MH * MT)
        s[:, S_GDN] = a["gdn_norm_w"][l]
        s[:, S_SGN] = 1.0
        for d in range(2):
            s[ML_ROW[d]:ML_ROW[d] + MH, S_BA] = a["ml_i_bias"][l, d]
            s[ML_ROW[d]:ML_ROW[d] + MH, S_BB] = a["ml_f_bias"][l, d]
            s[ML_ROW[d]:ML_ROW[d] + MH, S_SGN] = -1.0
            s[GD_ROW[d]:GD_ROW[d] + GH, S_BB] = a["gdn_dt_bias"][l, d]
            s[GD_ROW[d]:GD_ROW[d] + GH, S_ALOG] = a["gdn_a_log"][l, d]
    for n, v in enumerate((a["c_ctx"], a["c"][0])):
        small[:, S_COND + n:S_COND + 16:2] = tiles(v, KT)
    arrays["smalls"] = small

    wg = np.zeros((DEPTH, D, 2 * P), f)
    for d in range(2):
        for t, part in enumerate((7, 8)):
            c = OFF[part] + d * MH
            wg[:, :, t * P + ML_ROW[d]:t * P + ML_ROW[d] + MH] = a["w_in"][:, :, c:c + MH]
        for t, part in enumerate((13, 14)):
            c = OFF[part] + d * GH
            wg[:, :, t * P + GD_ROW[d]:t * P + GD_ROW[d] + GH] = a["w_in"][:, :, c:c + GH]
    arrays["w_gates"] = wg
    for k, n in (("w_ada", "w_ada"), ("w_gate", "ffn_w_gate"), ("w_up", "ffn_w_up"), ("w_down", "ffn_w_down"),
                 ("w_in", "w_in"), ("w_branch", "w_branch"), ("w_out", "w_out")):
        arrays[k] = np.ascontiguousarray(a[n])

    con = np.zeros((P, C_ALL), f)
    con[:, C_ID:C_ID + P] = np.eye(P)
    con[:, C_ONE:C_ONE + P] = 1.0
    half, quarter = P // 2, P // 4
    for i in range(P):
        j = i % half
        if j < quarter:
            con[i + quarter, C_ROT + i] = -1.0
        else:
            con[i - quarter, C_ROT + i] = 1.0
    inv = (f(10000.0) ** (-np.arange(quarter, dtype=f) / f(quarter))).astype(f)
    tok = np.arange(SEQ)
    for i in range(P):
        pos = (tok // 64 if i < half else tok % 64).astype(f)
        ang = pos * inv[i % quarter]
        con[i, C_COS:C_COS + SEQ] = np.cos(ang)
        con[i, C_SIN:C_SIN + SEQ] = np.sin(ang)
    for b in range(2):
        q = b * P + np.arange(P)[:, None]
        con[:, C_WIN + b * SEQ:C_WIN + (b + 1) * SEQ] = np.where(np.abs(np.arange(SEQ)[None] - q) <= 128, 0.0, -FAR)
    s, t = np.arange(P)[:, None], np.arange(P)[None]
    con[:, C_MIN:C_MIN + P] = np.where(s <= t, 0.0, -FAR)
    con[:, C_MIN + P:C_MIN + 2 * P] = np.where(s >= t, 0.0, -FAR)
    arrays["consts"] = con
    lev = np.zeros((P, 2, len(LEVELS), P), f)
    for n, b in enumerate(LEVELS):
        m = (s // (2 * b) == t // (2 * b)) & ((s // b) % 2 == 1) & ((t // b) % 2 == 0)
        lev[:, 0, n], lev[:, 1, n] = m, m.T
    arrays["levels"] = lev.reshape(P, M_ALL)
    return arrays


_NAMES = ("tokens", "smalls", "consts", "levels", "w_ada", "w_gates", "w_gate", "w_up", "w_down", "w_in",
          "w_branch", "w_out")


def kernel(**inputs):
    import concourse.bacc as _bacc
    from concourse.bass_utils import run_bass_kernel_spmd as _run

    nc = _bacc.Bacc("TRN2", target_bir_lowering=False, num_devices=1)
    arrays = _layout(**inputs)
    args = [nc.dram_tensor(n, arrays[n].shape, mybir.dt.from_np(arrays[n].dtype), kind="ExternalInput").ap()
            for n in _NAMES]
    out = nc.dram_tensor("out", (D, SEQ), F32, kind="ExternalOutput").ap()
    trunk_kernel(nc, *args, out)
    r = _run(nc, [arrays], core_ids=[0])
    return np.ascontiguousarray(r.results[0]["out"].T)[None]
```
